# Optimizing a Trainium2 kernel written in Bass

```python
import math
import jax, jax.numpy as jnp
from jax import lax
import numpy as np

D_MODEL = 1024
BATCH = 1
SEQ = 256
DEPTH = 2

CHUNK = 64
Q_BLOCK = 128
NORM_EPS = 1e-6

D_RNN = D_MODEL
LRU_BLOCKS = 16
LRU_BLOCK_DIM = D_RNN // LRU_BLOCKS
CONV_WIDTH = 4
LRU_C = 8.0

DIFF_HEADS = 8
DIFF_HEAD_DIM = D_MODEL // DIFF_HEADS // 2
DIFF_WIDTH = DIFF_HEADS * 2 * DIFF_HEAD_DIM

SWA_Q_HEADS = 16
SWA_KV_HEADS = 2
SWA_HEAD_DIM = 64
SWA_GROUP = SWA_Q_HEADS // SWA_KV_HEADS
WINDOW = 128
WINDOW_CHUNKS = WINDOW // CHUNK

REL_BUCKETS = 32
REL_MAX_DISTANCE = 1024
N_ATTN_HEADS = DIFF_HEADS + SWA_Q_HEADS

N_BRANCHES = 3

PEER_HEADS = 8
PEER_N_KEYS = 128
PEER_N_EXPERTS = PEER_N_KEYS * PEER_N_KEYS
PEER_TOPK = 16
PEER_D_KEY = 256
PEER_HALF = PEER_D_KEY // 2
PEER_BLOCK = 128

SPLITS = (D_RNN, D_RNN, DIFF_WIDTH, DIFF_WIDTH, DIFF_WIDTH,
          SWA_Q_HEADS * SWA_HEAD_DIM, SWA_KV_HEADS * SWA_HEAD_DIM, SWA_KV_HEADS * SWA_HEAD_DIM)
D_IN_PROJ = sum(SPLITS)

kernel_name = "hybrid_lru_diffattn_swa_peer_block"

def rms_norm(x, g):
    xf = x.astype(jnp.float32)
    y = xf * lax.rsqrt(jnp.mean(xf * xf, axis=-1, keepdims=True) + NORM_EPS)
    return (y * g.astype(jnp.float32)).astype(x.dtype)

def rel_bucket(rel):
    nb = REL_BUCKETS // 2
    max_exact = nb // 2
    side = jnp.where(rel > 0, nb, 0)
    n = jnp.abs(rel)
    nf = jnp.maximum(n, 1).astype(jnp.float32)
    large = max_exact + (jnp.log(nf / max_exact) / math.log(REL_MAX_DISTANCE / max_exact)
                         * (nb - max_exact)).astype(jnp.int32)
    large = jnp.minimum(large, nb - 1)
    return side + jnp.where(n < max_exact, n, large)

def _lru_combine(left, right):
    a_l, b_l = left
    a_r, b_r = right
    return a_r * a_l, a_r * b_l + b_r

def rglru_branch(xb, gb, conv_w, conv_b, wx, bx, wa, ba, a_param):
    B, S, _ = xb.shape
    xpad = jnp.pad(xb, ((0, 0), (CONV_WIDTH - 1, 0), (0, 0)))
    xc = conv_b
    for j in range(CONV_WIDTH):
        xc = xc + xpad[:, j:j + S] * conv_w[j]
    xr = xc.reshape(B, S, LRU_BLOCKS, LRU_BLOCK_DIM)
    gate_x = jax.nn.sigmoid(jnp.einsum('bsni,nij->bsnj', xr, wx) + bx).reshape(B, S, D_RNN)
    gate_a = jax.nn.sigmoid(jnp.einsum('bsni,nij->bsnj', xr, wa) + ba).reshape(B, S, D_RNN)
    log_a = LRU_C * gate_a.astype(jnp.float32) * jax.nn.log_sigmoid(a_param.astype(jnp.float32))
    a = jnp.exp(log_a)
    mult = jnp.sqrt(-jnp.expm1(2.0 * log_a))
    b_in = mult * (gate_x * xc).astype(jnp.float32)
    _, h = lax.associative_scan(_lru_combine, (a, b_in), axis=1)
    return h.astype(xb.dtype) * jax.nn.gelu(gb)

def diff_attention(q, k, v, lam, lam_init, subln_g, bias_tab):
    B, S = q.shape[:2]
    q = q.reshape(B, S, 2 * DIFF_HEADS, DIFF_HEAD_DIM)
    k = k.reshape(B, S, 2 * DIFF_HEADS, DIFF_HEAD_DIM)
    v = v.reshape(B, S, DIFF_HEADS, 2 * DIFF_HEAD_DIM)
    scale = DIFF_HEAD_DIM ** -0.5
    nqb = S // Q_BLOCK
    qb = jnp.moveaxis(q.reshape(B, nqb, Q_BLOCK, 2 * DIFF_HEADS, DIFF_HEAD_DIM), 1, 0)
    kpos = jnp.arange(S)

    def block(args):
        qblk, bi = args
        qpos = bi * Q_BLOCK + jnp.arange(Q_BLOCK)
        rel = kpos[None, :] - qpos[:, None]
        bias = jnp.moveaxis(bias_tab[rel_bucket(rel)], -1, 0).astype(jnp.float32)
        allowed = (kpos[None, :] // CHUNK) <= (qpos[:, None] // CHUNK)
        s = jnp.einsum('bqhd,bkhd->bhqk', qblk, k).astype(jnp.float32) * scale
        s = s.reshape(B, DIFF_HEADS, 2, Q_BLOCK, S) + bias[None, :, None]
        p = jax.nn.softmax(jnp.where(allowed, s, -jnp.inf), axis=-1)
        attn = p[:, :, 0] - lam * p[:, :, 1]
        return jnp.einsum('bhqk,bkhe->bqhe', attn.astype(v.dtype), v)

    o = lax.map(block, (qb, jnp.arange(nqb)))
    o = jnp.moveaxis(o, 0, 1).reshape(B, S, DIFF_HEADS, 2 * DIFF_HEAD_DIM)
    o = rms_norm(o, subln_g) * (1.0 - lam_init)
    return o.reshape(B, S, DIFF_WIDTH)

def _window(t, nc):
    tp = jnp.pad(t, ((0, 0), (WINDOW_CHUNKS - 1, 0), (0, 0), (0, 0), (0, 0)))
    return jnp.concatenate([tp[:, j:j + nc] for j in range(WINDOW_CHUNKS)], axis=2)

def swa_attention(q, k, v, sinks, bias_tab):
    B, S = q.shape[:2]
    nc = S // CHUNK
    W = WINDOW_CHUNKS * CHUNK
    qc = q.reshape(B, nc, CHUNK, SWA_KV_HEADS, SWA_GROUP, SWA_HEAD_DIM)
    kw = _window(k.reshape(B, nc, CHUNK, SWA_KV_HEADS, SWA_HEAD_DIM), nc)
    vw = _window(v.reshape(B, nc, CHUNK, SWA_KV_HEADS, SWA_HEAD_DIM), nc)
    qi = jnp.arange(CHUNK)
    m = jnp.arange(W)
    rel = m[None, :] - (WINDOW_CHUNKS - 1) * CHUNK - qi[:, None]
    bias = jnp.moveaxis(bias_tab[rel_bucket(rel)], -1, 0).astype(jnp.float32)
    bias = bias.reshape(SWA_KV_HEADS, SWA_GROUP, CHUNK, W)
    valid = (jnp.arange(nc)[:, None] - (WINDOW_CHUNKS - 1) + m[None, :] // CHUNK) >= 0
    s = jnp.einsum('bnqhgd,bnkhd->bnhgqk', qc, kw).astype(jnp.float32) * (SWA_HEAD_DIM ** -0.5) + bias
    s = jnp.where(valid[None, :, None, None, None, :], s, -jnp.inf)
    sink = jnp.broadcast_to(sinks.astype(jnp.float32).reshape(SWA_KV_HEADS, SWA_GROUP, 1, 1),
                            s.shape[:-1] + (1,))
    p = jax.nn.softmax(jnp.concatenate([s, sink], axis=-1), axis=-1)[..., :-1]
    o = jnp.einsum('bnhgqk,bnkhd->bnqhgd', p.astype(v.dtype), vw)
    return o.reshape(B, S, SWA_Q_HEADS * SWA_HEAD_DIM)

def peer_ffn(h, w_q, sub_keys, u, v):
    B, S, D = h.shape
    T = B * S
    ht = h.reshape(T, D)
    q = (ht @ w_q).reshape(T, PEER_HEADS, 2, PEER_HALF)
    scores = jnp.einsum('thcd,hckd->thck', q, sub_keys).astype(jnp.float32)
    s1, i1 = lax.top_k(scores[:, :, 0], PEER_TOPK)
    s2, i2 = lax.top_k(scores[:, :, 1], PEER_TOPK)
    cand_s = (s1[..., :, None] + s2[..., None, :]).reshape(T, PEER_HEADS, PEER_TOPK * PEER_TOPK)
    cand_i = (i1[..., :, None] * PEER_N_KEYS + i2[..., None, :]).reshape(T, PEER_HEADS, PEER_TOPK * PEER_TOPK)
    top_s, pos = lax.top_k(cand_s, PEER_TOPK)
    idx = jnp.take_along_axis(cand_i, pos, axis=-1)
    g = jax.nn.softmax(top_s, axis=-1)
    nb = T // PEER_BLOCK

    def block(args):
        hb, ib, gb = args
        ue = u[ib]
        ve = v[ib]
        act = jax.nn.gelu(jnp.einsum('pd,phkd->phk', hb, ue))
        return jnp.einsum('phk,phkd->pd', gb.astype(hb.dtype) * act, ve)

    out = lax.map(block, (ht.reshape(nb, PEER_BLOCK, D),
                          idx.reshape(nb, PEER_BLOCK, PEER_HEADS, PEER_TOPK),
                          g.reshape(nb, PEER_BLOCK, PEER_HEADS, PEER_TOPK)))
    return out.reshape(B, S, D)

def setup_inputs(seed: int = 0) -> dict:
    key = jax.random.key(seed)
    ks = jax.random.split(key, 24)
    f32 = jnp.float32

    def nrm(k, shape, scale):
        return jax.random.normal(k, shape, f32) * scale

    x = nrm(ks[0], (BATCH, SEQ, D_MODEL), 1.0)
    rel_bias = nrm(ks[1], (REL_BUCKETS, N_ATTN_HEADS), 0.5)
    final_norm_g = 1.0 + nrm(ks[2], (D_MODEL,), 0.02)
    norm_mix_g = 1.0 + nrm(ks[3], (DEPTH, D_MODEL), 0.02)
    w_in = nrm(ks[4], (DEPTH, D_MODEL, D_IN_PROJ), D_MODEL ** -0.5)
    conv_w = nrm(ks[5], (DEPTH, CONV_WIDTH, D_RNN), CONV_WIDTH ** -0.5)
    conv_b = nrm(ks[6], (DEPTH, D_RNN), 0.02)
    lru_wx = nrm(ks[7], (DEPTH, LRU_BLOCKS, LRU_BLOCK_DIM, LRU_BLOCK_DIM), LRU_BLOCK_DIM ** -0.5)
    lru_bx = nrm(ks[8], (DEPTH, LRU_BLOCKS, LRU_BLOCK_DIM), 0.02)
    lru_wa = nrm(ks[9], (DEPTH, LRU_BLOCKS, LRU_BLOCK_DIM, LRU_BLOCK_DIM), LRU_BLOCK_DIM ** -0.5)
    lru_ba = nrm(ks[10], (DEPTH, LRU_BLOCKS, LRU_BLOCK_DIM), 0.02)
    a0 = jax.random.uniform(ks[11], (DEPTH, D_RNN), f32, 0.9, 0.999) ** (1.0 / LRU_C)
    lru_a_param = jnp.log(a0) - jnp.log1p(-a0)
    diff_lambda = nrm(ks[12], (DEPTH, 4, DIFF_HEAD_DIM), 0.1)
    diff_subln_g = 1.0 + nrm(ks[13], (DEPTH, 2 * DIFF_HEAD_DIM), 0.02)
    swa_sinks = nrm(ks[14], (DEPTH, SWA_Q_HEADS), 0.5)
    w_gate = nrm(ks[15], (DEPTH, D_MODEL, N_BRANCHES * D_MODEL), D_MODEL ** -0.5)
    b_gate = nrm(ks[16], (DEPTH, N_BRANCHES * D_MODEL), 0.02)
    w_branch = nrm(ks[17], (DEPTH, N_BRANCHES, D_MODEL, D_MODEL), D_MODEL ** -0.5)
    w_out = nrm(ks[18], (DEPTH, D_MODEL, D_MODEL), D_MODEL ** -0.5)
    norm_ffn_g = 1.0 + nrm(ks[19], (DEPTH, D_MODEL), 0.02)
    peer_wq = nrm(ks[20], (DEPTH, D_MODEL, PEER_HEADS * PEER_D_KEY), D_MODEL ** -0.5)
    peer_subkeys = nrm(ks[21], (DEPTH, PEER_HEADS, 2, PEER_N_KEYS, PEER_HALF), PEER_HALF ** -0.5)
    peer_u = nrm(ks[22], (DEPTH, PEER_N_EXPERTS, D_MODEL), D_MODEL ** -0.5)
    peer_v = nrm(ks[23], (DEPTH, PEER_N_EXPERTS, D_MODEL), PEER_HEADS ** -0.5)
    return {"x": x, "rel_bias": rel_bias, "final_norm_g": final_norm_g, "norm_mix_g": norm_mix_g,
            "w_in": w_in, "conv_w": conv_w, "conv_b": conv_b, "lru_wx": lru_wx, "lru_bx": lru_bx,
            "lru_wa": lru_wa, "lru_ba": lru_ba, "lru_a_param": lru_a_param,
            "diff_lambda": diff_lambda, "diff_subln_g": diff_subln_g, "swa_sinks": swa_sinks,
            "w_gate": w_gate, "b_gate": b_gate, "w_branch": w_branch, "w_out": w_out,
            "norm_ffn_g": norm_ffn_g, "peer_wq": peer_wq, "peer_subkeys": peer_subkeys,
            "peer_u": peer_u, "peer_v": peer_v}

def reference(x, rel_bias, final_norm_g, norm_mix_g, w_in, conv_w, conv_b, lru_wx, lru_bx,
              lru_wa, lru_ba, lru_a_param, diff_lambda, diff_subln_g, swa_sinks, w_gate, b_gate,
              w_branch, w_out, norm_ffn_g, peer_wq, peer_subkeys, peer_u, peer_v):
    B, S, D = x.shape
    split_at = [int(i) for i in np.cumsum(SPLITS)[:-1]]
    bias_diff = rel_bias[:, :DIFF_HEADS]
    bias_swa = rel_bias[:, DIFF_HEADS:]
    for l in range(DEPTH):
        h = rms_norm(x, norm_mix_g[l])
        proj = h @ w_in[l]
        lru_x, lru_g, dq, dk, dv, sq, sk, sv = jnp.split(proj, split_at, axis=-1)

        o_lru = rglru_branch(lru_x, lru_g, conv_w[l], conv_b[l], lru_wx[l], lru_bx[l],
                             lru_wa[l], lru_ba[l], lru_a_param[l])

        lam_init = 0.8 - 0.6 * math.exp(-0.3 * l)
        lp = diff_lambda[l].astype(jnp.float32)
        lam = jnp.exp(jnp.sum(lp[0] * lp[1])) - jnp.exp(jnp.sum(lp[2] * lp[3])) + lam_init
        o_diff = diff_attention(dq, dk, dv, lam, lam_init, diff_subln_g[l], bias_diff)

        o_swa = swa_attention(sq, sk, sv, swa_sinks[l], bias_swa)

        gates = jax.nn.sigmoid(h @ w_gate[l] + b_gate[l]).reshape(B, S, N_BRANCHES, D)
        branches = jnp.stack([o_lru, o_diff, o_swa], axis=2)
        up = jnp.einsum('bsnw,nwd->bsnd', branches, w_branch[l])
        x = x + jnp.sum(gates * up, axis=2) @ w_out[l]

        h2 = rms_norm(x, norm_ffn_g[l])
        x = x + peer_ffn(h2, peer_wq[l], peer_subkeys[l], peer_u[l], peer_v[l])
    return rms_norm(x, final_norm_g)


_drawn_inputs = setup_inputs


def setup_inputs(seed=0):
    import zlib

    import numpy as np

    out = dict(_drawn_inputs(seed))
    spreads = {}
    factors = {'final_norm_g': 7.76,
     'lru_bx': 4.477,
     'lru_ba': 5.368,
     'swa_sinks': 6.608,
     'b_gate': 2.785}
    for name, (base, spread) in spreads.items():
        noise = np.random.default_rng([zlib.crc32(name.encode()), seed]).standard_normal(out[name].shape)
        drawn = base * np.exp(spread * noise) if base else spread * noise
        out[name] = __import__('jax').numpy.asarray(drawn.astype(out[name].dtype))
    for name, factor in factors.items():
        out[name] = (out[name] * factor).astype(out[name].dtype)
    return out
```

```python
import concourse.bass as bass
from concourse import mybir
from contextlib import ExitStack
import numpy as np

F32 = mybir.dt.float32
F32R = mybir.dt.float32r
U32 = mybir.dt.uint32
I32 = mybir.dt.int32
ALU = mybir.AluOpType
ACT = mybir.ActivationFunctionType
AX = mybir.AxisListType.X

P = 128
DEPTH = 2
SEQ = 256
D = 1024
DC = D // P
TT = SEQ // P
HEADS_DIFF = 8
HEADS_SWA = 16
CHUNK = 64
N_GROUPS = SEQ // 4
TOPK = 16
PEER_HEADS = 8
KEYS = 128
EPS = 1e-6
LRU_C = 8.0
SCALE = 0.125
MASKED = -1e30
TAKEN = -3e38

N_IN = 50
N_GATE = 24
N_BRANCH = 24
N_OUT = 8
N_WQ = 16
N_U = KEYS
N_V = KEYS
T_LRUX, T_LRUG, T_DQ, T_DK, T_DV, T_SQ, T_SK, T_SV = 0, 8, 16, 24, 32, 40, 48, 49
MIX_BLOCKS = N_IN + N_GATE + N_BRANCH + N_OUT
PEER_BLOCKS = N_WQ + N_U + N_V
LAYER_PAIRS = (MIX_BLOCKS + PEER_BLOCKS) // 2

V_MIXG, V_CONVW, V_CONVB, V_BX, V_BA, V_APAR, V_BGATE, V_FFNG, V_SUBLN, N_VEC = 0, 8, 40, 48, 56, 64, 72, 96, 104, 105
C_ID, C_FLIP, C_IOTA, C_LO, C_HI, C_NEG, N_CST = 0, 128, 256, 384, 512, 640, 704

N_REL = 384
N_BIAS = HEADS_DIFF + HEADS_SWA

CAND_N = [TOPK // (i + 1) for i in range(TOPK)]
CAND_OFF = [sum(CAND_N[:i]) for i in range(TOPK)]
N_CAND = sum(CAND_N)
PAIR_RANKS = sum(n > 1 for n in CAND_N)


def spread(ap, dim, n):
    shape = list(ap.shape)
    shape[dim] = n
    return ap.to_broadcast(shape)


class Chain:

    def __init__(self, eng, sem, drains=False):
        self.eng, self.sem, self.drains = eng, sem, drains
        self.base, self.turn, self.per, self.n = 0, None, 0, 0

    def value(self):
        done = self.base + self.n
        return done if self.turn is None else self.turn * self.per + done

    def __call__(self, ins):
        self.n += 1
        ins.then_inc(self.sem, 1)
        if self.turn is not None and self.drains:
            self.eng.drain()
        else:
            self.eng.wait_ge(self.sem, self.value())

    def enter(self, turn, per):
        self.base, self.turn, self.per, self.n = self.base + self.n, turn, per, 0

    def leave(self, turns):
        assert self.n == self.per, (self.n, self.per)
        self.base, self.turn, self.n = self.base + turns * self.per, None, 0


def blocks_loop(eng, first, count, body):
    fours = count // 4
    if fours:
        with eng.Fori(0, fours) as n:
            for i in range(4):
                body(n * 4 + i, n * 4 + (first + i), (first + i) % 4, n, i)
    for b in range(4 * fours, count):
        body(b, first + b, (first + b) % 4, None, b - 4 * fours)


def trunk(nc, stream, vecs, cst, rel_bias, bucket_onehot, lam_consts, final_g, diff_lambda, sinks,
          lru_w, subkeys, x_in, out):
    top = ExitStack()

    def sb(stack, name, shape, dt=F32):
        return stack.enter_context(nc.sbuf_tensor(name, shape, dt))

    with top:
        sem_list = []

        def sem(name):
            s = top.enter_context(nc.semaphore(name))
            sem_list.append(s)
            return s

        x = sb(top, "x", [P, TT, D])
        consts = sb(top, "consts", [P, N_CST])
        vec = sb(top, "vec", [P, N_VEC])
        raw = sb(top, "raw", [P, 2, 2, D])
        w_hi = sb(top, "w_hi", [P, 4, 512], F32R)
        w_lo = sb(top, "w_lo", [P, 4, 512], F32R)
        h_hi = sb(top, "h_hi", [P, DC, SEQ], F32R)
        h_lo = sb(top, "h_lo", [P, DC, SEQ], F32R)
        a_hi = sb(top, "a_hi", [P, 2, SEQ], F32R)
        a_lo = sb(top, "a_lo", [P, 2, SEQ], F32R)
        ss = sb(top, "ss", [P, TT])
        rstd = sb(top, "rstd", [P, TT])
        warm = sb(top, "warm", [P, 1])
        halfpow = sb(top, "halfpow", [P, 16])
        bank = [top.enter_context(nc.psum_tensor(f"bank{i}", [P, 512], F32)) for i in range(8)]
        ident = consts[:, C_ID:C_ID + P]
        flip8 = consts[:, C_FLIP:C_FLIP + P]
        iota = consts[:, C_IOTA:C_IOTA + P]
        row_lo = consts[0:1, C_LO:C_LO + P]
        row_hi = consts[0:1, C_HI:C_HI + P]
        neg = consts[0:1, C_NEG:C_NEG + CHUNK]
        tdram = nc.dram_tensor("rel_line", (N_BIAS, N_REL), F32, kind="Internal").ap()
        hankel = nc.dram_tensor("rel_hankel", (N_BIAS, P, SEQ), F32, kind="Internal").ap()

        raw_in = [sem(f"raw_in{i}") for i in range(2)]
        w_hi_done = sem("w_hi_done")
        w_parts = sem("w_parts")
        w_used = sem("w_used")
        up_read = sem("up_read")
        a_hi_done = sem("a_hi_done")
        a_parts = sem("a_parts")
        s_act, s_dve, s_pool = sem("s_act"), sem("s_dve"), sem("s_pool")
        sums_done = sem("sums_done")
        rstd_done = sem("rstd_done")
        xr_done = sem("xr_done")
        tp_done = sem("tp_done")
        tp_read = sem("tp_read")
        h_done = sem("h_done")
        const_in = sem("const_in")
        vec_in = sem("vec_in")
        stored = sem("stored")
        once = sem("once")
        proj_done = sem("proj_done")
        lam_sum, lam_exp, lam_done = sem("lam_sum"), sem("lam_exp"), sem("lam_done")
        conv_done, lru_mm, lru_sig = sem("conv_done"), sem("lru_mm"), sem("lru_sig")
        lru_xg, lru_exp, lru_u, lru_sqrt, lru_done = sem("lru_xg"), sem("lru_exp"), sem("lru_u"), sem("lru_sqrt"), sem("lru_done")
        vt_done, vt_read = sem("vt_done"), sem("vt_read")
        sk_turned = sem("sk_turned")
        hank_in = [sem(f"hank_in{i}") for i in range(2)]
        staged = sem("staged")
        scored, max_done, exp_done, attn_done = sem("scored"), sem("max_done"), sem("exp_done"), sem("attn_done")
        pt_done, pt_read, pv_done, pv_read = sem("pt_done"), sem("pt_read"), sem("pv_done"), sem("pv_read")
        pad_done = sem("pad_done")
        on_sum, on_pow, on_done, ot_done, ot_read = sem("on_sum"), sem("on_pow"), sem("on_done"), sem("ot_done"), sem("ot_read")
        o_hi_done, o_parts = sem("o_hi_done"), sem("o_parts")
        mix_done = sem("mix_done")
        x_done = sem("x_done")
        q_done, sc_done, sc_read = sem("q_done"), sem("sc_done"), sem("sc_read")
        soft_in, soft_out, routed = sem("soft_in"), sem("soft_out"), sem("routed")
        rt_done, rt_read = sem("rt_done"), sem("rt_read")
        hot_done, g_done, g_read = sem("hot_done"), sem("g_done"), sem("g_read")
        per_layer = list(sem_list)

        def clear():
            with nc.Block() as block:
                @block.sync
                def _(sp):
                    for s in per_layer:
                        sp.sem_clear(s)

        with ExitStack() as part:
            onehot_sb = sb(part, "onehot_sb", [32, N_REL])
            rel_sb = sb(part, "rel_sb", [32, N_BIAS])
            line_sb = sb(part, "line_sb", [N_BIAS, N_REL])
            with nc.Block() as block:
                @block.sync
                def _(sp):
                    sp.dma_start(onehot_sb[:], bucket_onehot).then_inc(const_in, 16)
                    sp.dma_start(rel_sb[:], rel_bias).then_inc(const_in, 16)
                    sp.dma_start(consts[:], cst).then_inc(vec_in, 16)
                    sp.dma_start(x[:], x_in.rearrange("(a p) d -> p a d", p=P)).then_inc(vec_in, 16)
                    sp.wait_ge(once, 3)
                    sp.dma_start(tdram, line_sb[:]).then_inc(stored, 16)
                    sp.wait_ge(stored, 16)
                    sp.dma_start(hankel, bass.AP(tdram.tensor, 0, [[N_REL, N_BIAS], [1, P], [1, SEQ]])).then_inc(stored, 16)
                    sp.wait_ge(stored, 32)
                    sp.wait_ge(vec_in, 32)

                @block.tensor
                def _(pe):
                    pe.wait_ge(const_in, 32)
                    pe.matmul(bank[0][0:N_BIAS, 0:N_REL], rel_sb[:], onehot_sb[:], start=True, stop=True).then_inc(once, 1)

                @block.vector
                def _(dve):
                    dve.memset(halfpow[:], -0.5).then_inc(once, 1)
                    dve.wait_ge(once, 2)
                    dve.tensor_copy(line_sb[:], bank[0][0:N_BIAS, 0:N_REL]).then_inc(once, 1)
        clear()

        def load_pairs(sp, layer, part_pair, first, end):
            base = layer * LAYER_PAIRS + part_pair

            def load(p, slot):
                sp.wait_ge(w_parts, p * 4 + 4)
                sp.dma_start(raw[:, slot, :, :], stream[bass.ds(base + p, 1)].rearrange("o b p c -> p (o b) c")).then_inc(raw_in[slot], 16)
            twos = (end - first) // 2
            with sp.Fori(0, twos) as n:
                load(n * 2 + first, first % 2)
                load(n * 2 + (first + 1), (first + 1) % 2)
            if (end - first) % 2:
                load(end - 1, (end - 1) % 2)

        def split_hi(act, blk, ring):
            slot, sub = ring // 2, ring % 2
            if sub == 0:
                act.wait_ge(raw_in[slot], blk * 4 + (16 - 4 * ring))
            for k in range(2):
                act.wait_ge(w_used, blk * 2 + (k + 1))
                act.activation(w_hi[:, (ring % 2) * 2 + k, :], raw[:, slot, sub, 512 * k:512 * k + 512], ACT.Copy).then_inc(w_hi_done, 1)

        def split_lo(dve, blk, ring):
            slot, sub = ring // 2, ring % 2
            for k in range(2):
                q = (ring % 2) * 2 + k
                dve.wait_ge(w_hi_done, blk * 2 + (k + 1))
                dve.tensor_tensor(w_lo[:, q, :], raw[:, slot, sub, 512 * k:512 * k + 512], w_hi[:, q, :].bitcast(F32), ALU.subtract).then_inc(w_parts, 1)

        def up_block(pe, blk, ring, n_up, ps, rhs_hi, rhs_lo):
            pe.wait_ge(up_read, n_up + 1)
            for k in range(2):
                q = (ring % 2) * 2 + k
                pe.wait_ge(w_parts, blk * 2 + (k + 9))
                for c in range(4):
                    hi, lo = w_hi[:, q, P * c:P * c + P], w_lo[:, q, P * c:P * c + P]
                    first, last = k == 0 and c == 0, k == 1 and c == 3
                    pe.matmul(ps, hi, rhs_hi(4 * k + c), start=first, stop=False)
                    pe.matmul(ps, hi, rhs_lo(4 * k + c), start=False, stop=False)
                    ins = pe.matmul(ps, lo, rhs_hi(4 * k + c), start=False, stop=last)
                ins.then_inc(w_used, 1)

        def down_block(pe, blk, ring, k_blk, acc, first, last):
            pe.wait_ge(a_parts, k_blk + 1)
            a = ring % 2
            for k in range(2):
                q = (ring % 2) * 2 + k
                pe.wait_ge(w_parts, blk * 2 + (k + 9))
                for t in range(TT):
                    hi, lo = a_hi[:, a, P * t:P * t + P], a_lo[:, a, P * t:P * t + P]
                    ps = acc[2 * t + k][:, :]
                    pe.matmul(ps, hi, w_hi[:, q, :], start=first, stop=False)
                    pe.matmul(ps, hi, w_lo[:, q, :], start=False, stop=False)
                    ins = pe.matmul(ps, lo, w_hi[:, q, :], start=False, stop=last)
                ins.then_inc(w_used, 1)

        def table_of(act, ch, func):
            ch(act.activation(warm[:], halfpow[:, 0:1], func))

        def norm_act(act, ch):
            for t in range(TT):
                ch(act.activation(xr[:, t, :], x[:, t, :], ACT.Square, accum_out=ss[:, t:t + 1]))
            act.activation(rstd[:], ss[:], ACT.Copy, scale=1.0 / D, bias=EPS).then_inc(sums_done, 1)

        def norm_pool(pool):
            pool.wait_ge(sums_done, 1)
            pool.tensor_tensor(rstd[:], rstd[:], halfpow[:, 0:TT], ALU.pow).then_inc(rstd_done, 1)

        def norm_dve(dve, ch, g_col, h):
            dve.wait_ge(rstd_done, 1)
            for t in range(TT):
                dve.tensor_scalar(xr[:, t, :], x[:, t, :], rstd[:, t:t + 1], None, ALU.mult).then_inc(xr_done, 1)
            dve.wait_ge(vec_in, VEC_LOADS)
            for c in range(DC):
                dve.wait_ge(tp_done, c + 1)
                dve.tensor_scalar(h[:, c, :], bank[4 + c % 2][:, 0:SEQ], vec[:, g_col + c:g_col + c + 1], None, ALU.mult).then_inc(tp_read, 1)
                dve.wait_ge(tp_read, c + 1)
                ch(dve.tensor_copy(h_hi[:, c, :], h[:, c, :]))
                dve.tensor_tensor(h_lo[:, c, :], h[:, c, :], h_hi[:, c, :].bitcast(F32), ALU.subtract).then_inc(h_done, 1)

        def norm_pe(pe):
            pe.wait_ge(xr_done, TT)
            for c in range(DC):
                if c >= 2:
                    pe.wait_ge(tp_read, c - 1)
                for t in range(TT):
                    ins = pe.transpose(bank[4 + c % 2][:, P * t:P * t + P], xr[:, t, P * c:P * c + P], ident)
                ins.then_inc(tp_done, 1)

        def part_hi(act, src, k, a):
            act.activation(a_hi[:, a, :], src(k), ACT.Copy).then_inc(a_hi_done, 1)

        def part_lo(dve, src, k, a):
            dve.wait_ge(a_hi_done, k + 1)
            dve.tensor_tensor(a_lo[:, a, :], src(k), a_hi[:, a, :].bitcast(F32), ALU.subtract).then_inc(a_parts, 1)

        def add_to_x(dve, acc, halves):
            dve.wait_ge(w_used, halves)
            for t in range(TT):
                for k in range(2):
                    part = x[:, t, 512 * k:512 * k + 512]
                    dve.tensor_tensor(part, part, acc[2 * t + k][:, :], ALU.add).then_inc(x_done, 1)
            dve.wait_ge(x_done, 2 * TT)

        def one(ap):
            return ap.rearrange("p o s -> p (o s)")

        with nc.Fori(0, DEPTH) as layer:
            with ExitStack() as part:
                proj = sb(part, "proj", [P, N_IN, SEQ])
                gates = sb(part, "gates", [P, N_GATE, SEQ])
                o_hi = sb(part, "o_hi", [P, N_BRANCH, SEQ], F32R)
                o_lo = sb(part, "o_lo", [P, N_BRANCH, SEQ], F32R)
                mix = sb(part, "mix", [P, DC, SEQ])
                v_nat = sb(part, "v_nat", [P, TT, D + P])
                hank = sb(part, "hank", [P, 2, 2, SEQ])
                qk = sb(part, "qk", [P, 2, 3, SEQ])
                small = sb(part, "small", [P, 96])
                xr = mix[:].rearrange("p (a b) s -> p a (b s)", a=TT)
                lru_ws = qk[:].rearrange("p a b s -> p (a b s)")[:, 0:D].rearrange("p (m i c) -> p m i c", i=2, c=64)
                lamv = hank[:, 0, 0, :].rearrange("p (a b) -> p a b", a=4)
                gate_x = v_nat[:].rearrange("p a b -> p (a b)")[:, 0:DC * SEQ].rearrange("p (a b) -> p a b", a=DC)
                prob = mix[:, 0:4, :].rearrange("p (a b) s -> p a b s", a=2)
                prob_t = mix[:, 4:8, :].rearrange("p (a b) (c s) -> p a (b c) s", a=2, c=2)
                o_nat = proj[:, T_DV:T_DV + 8, :].rearrange("p (a b) (c s) -> p a (b c) s", a=TT, c=2)
                o_sq = proj[:, T_DK:T_DK + 8, :].rearrange("p (a b) (c s) -> p a (b c) s", a=TT, c=2)
                skd = proj[:, T_LRUX:T_LRUX + 2, :]
                gated = hank[:, 0, :, :]
                top_s, nmax, zsum, rz, esink = [small[:, 4 * i:4 * i + 4] for i in range(5)]
                nlam, lsum, lam_e = small[:, 20:21], small[:, 22:24], small[:, 24:26]
                log_a, ls_e, ls_z, ls_p = [small[:, 28 + 8 * i:36 + 8 * i] for i in range(4)]
                oss, orstd = small[:, 28:44], small[:, 44:60]
                nsink, lam_c = small[:, 64:80], small[:, 80:82]
                B_BR, B_OUT = N_IN + N_GATE, N_IN + N_GATE + N_BRANCH
                OUTS = (T_LRUG, T_DQ, T_SQ)
                VEC_LOADS = 5 * 16

                with nc.Block() as block:
                    @block.sync
                    def _(sp):
                        sp.sem_inc(w_parts, 8)
                        sp.dma_start(vec[:], vecs[bass.ds(layer, 1)].rearrange("o p c -> (o p) c")).then_inc(vec_in, 16)
                        sp.dma_start(hank[:, 0, 0, :], spread(diff_lambda[bass.ds(layer, 1)], 0, P)).then_inc(vec_in, 16)
                        sp.dma_start(nsink, spread(sinks[bass.ds(layer, 1)], 0, P)).then_inc(vec_in, 16)
                        sp.dma_start(lam_c, spread(lam_consts[bass.ds(layer, 1)], 0, P)).then_inc(vec_in, 16)
                        sp.dma_start(lru_ws, lru_w[bass.ds(layer, 1)].rearrange("o p a b c -> (o p) a b c")).then_inc(vec_in, 16)
                        before = B_BR // 2 + 2
                        load_pairs(sp, layer, 0, 0, before)
                        sp.wait_ge(lru_done, 1)
                        for g in range(2):
                            for side in range(2):
                                sp.dma_start(skd[64 * side:64 * side + 64, g, :], proj[64 * g:64 * g + 64, T_SK, :]).then_inc(sk_turned, 16)
                        with sp.Fori(0, 4) as n:
                            for s in range(2):
                                sp.wait_ge(scored, n * 4 + (2 * s + 2))
                                sp.dma_start(hank[:, s, 0, :], hankel[bass.ds(n * 2 + s, 1)].rearrange("h p f -> (h p) f")).then_inc(hank_in[s], 16)
                        with sp.Fori(4, 8) as n:
                            for s in range(2):
                                sp.wait_ge(scored, n * 4 + (2 * s + 2))
                                sp.dma_start(hank[:, s, :, :], hankel[bass.ds(n * 4 + (2 * s - HEADS_DIFF), 2)].rearrange("h p f -> p h f")).then_inc(hank_in[s], 16)
                        load_pairs(sp, layer, 0, before, MIX_BLOCKS // 2)

                    @block.gpsimd
                    def _(pool):
                        ch = Chain(pool, s_pool, drains=True)
                        norm_pool(pool)
                        pool.wait_ge(proj_done, N_IN + N_GATE)
                        pool.wait_ge(lru_done, 1)
                        for s in range(2):
                            for c in range(2):
                                ch(pool.memset(qk[64 - 64 * c:128 - 64 * c, s, c, :], 0.0))

                        def unit_in(m, s, swa, g):
                            pool.wait_ge(scored, m * 2 + 2)
                            if swa:
                                for c in range(2):
                                    r = slice(64 * c, 64 * c + 64)
                                    ch(pool.tensor_copy(qk[r, s, c, :], one(proj[r, bass.ds(m + (T_SQ - HEADS_DIFF), 1), :])))
                                pool.tensor_copy(qk[:, s, 2, :], skd[:, g, :]).then_inc(staged, 1)
                            else:
                                for c in range(2):
                                    r = slice(64 * c, 64 * c + 64)
                                    ch(pool.tensor_copy(qk[r, s, c, :], one(proj[r, bass.ds(m + T_DQ, 1), :])))
                                pool.tensor_copy(qk[:, s, 2, :], one(proj[:, bass.ds(m + T_DK, 1), :])).then_inc(staged, 1)
                        with pool.Fori(0, 4) as n:
                            ch.enter(n, 4)
                            for s in range(2):
                                unit_in(n * 2 + s, s, False, 0)
                        ch.leave(4)
                        pool.wait_ge(sk_turned, 64)
                        for g in range(2):
                            with pool.Fori(4 + 2 * g, 6 + 2 * g) as n:
                                ch.enter(n - (4 + 2 * g), 4)
                                for s in range(2):
                                    unit_in(n * 2 + s, s, True, g)
                            ch.leave(2)
                        pool.wait_ge(on_sum, 1)
                        pool.tensor_tensor(orstd, oss, halfpow[:, 0:16], ALU.pow).then_inc(on_pow, 1)

                    @block.scalar
                    def _(act):
                        ch = Chain(act, s_act)
                        act.sem_inc(exp_done, 4)
                        norm_act(act, ch)
                        split_hi(act, 0, 0)

                        def project(first, count, func, bias):
                            def body(k, blk, ring, n, i):
                                split_hi(act, blk + 1, (ring + 1) % 4)
                                act.wait_ge(w_used, blk * 2 + 6)
                                dst = one((gates if bias else proj)[:, bass.ds(blk - (N_IN if bias else 0), 1), :])
                                b = vec[:, bass.ds(k + V_BGATE, 1)] if bias else 0.0
                                act.activation(dst, bank[ring % 2][:, 0:SEQ], func, bias=b).then_inc(up_read, 1)
                            blocks_loop(act, first, count, body)
                        project(T_LRUX, 8, ACT.Copy, False)
                        table_of(act, ch, ACT.Gelu_apprx_tanh)
                        project(T_LRUG, 8, ACT.Gelu_apprx_tanh, False)
                        project(T_DQ, N_IN - T_DQ, ACT.Copy, False)
                        table_of(act, ch, ACT.Sigmoid)
                        project(N_IN, N_GATE, ACT.Sigmoid, True)
                        act.wait_ge(up_read, 2 + N_IN + N_GATE)
                        act.sem_inc(proj_done, N_IN + N_GATE)

                        with act.Fori(0, DC // 2) as n:
                            for s in range(2):
                                act.wait_ge(lru_mm, n * 2 + (s + 1))
                                act.activation(one(gate_x[:, bass.ds(n * 2 + s, 1), :]), bank[2 + s][:, 0:SEQ], ACT.Sigmoid, bias=vec[:, bass.ds(n * 2 + (V_BX + s), 1)])
                                act.activation(one(proj[:, bass.ds(n * 2 + (T_LRUX + s), 1), :]), bank[2 + s][:, SEQ:2 * SEQ], ACT.Sigmoid, bias=vec[:, bass.ds(n * 2 + (V_BA + s), 1)]).then_inc(lru_sig, 1)
                        act.wait_ge(lam_sum, 1)
                        act.activation(lam_e, lsum, ACT.Exp)
                        act.activation(ls_e, ls_e, ACT.Exp).then_inc(lam_exp, 1)
                        act.wait_ge(lam_done, 1)
                        act.wait_ge(lru_xg, 1)
                        act.wait_ge(lru_sig, DC)
                        with act.Fori(0, DC) as m:
                            ga = one(proj[:, bass.ds(m, 1), :])
                            act.activation(one(gate_x[:, bass.ds(m, 1), :]), ga, ACT.Tanh, scale=small[:, bass.ds(m + 28, 1)])
                            act.activation(ga, ga, ACT.Exp, scale=small[:, bass.ds(m + 28, 1)]).then_inc(lru_exp, 1)
                        act.wait_ge(lru_u, 1)
                        act.activation(gate_x, gate_x, ACT.Sqrt, scale=-2.0).then_inc(lru_sqrt, 1)
                        act.wait_ge(lru_done, 1)
                        act.activation(o_hi[:, 0:8, :], proj[:, T_LRUG:T_LRUG + 8, :], ACT.Copy).then_inc(o_hi_done, 1)
                        for i in range(5):
                            act.wait_ge(vt_done, i + 1)
                            if i < 4:
                                act.activation(v_nat[:, i // 2, 512 * (i % 2):512 * (i % 2) + 512], bank[6 + i % 2][:, :], ACT.Copy).then_inc(vt_read, 1)
                            else:
                                act.activation(v_nat[:, :, D:D + P], bank[6][:, 0:SEQ].rearrange("p (a b) -> p a b", a=TT), ACT.Copy).then_inc(vt_read, 1)

                        def unit(m, s, swa):
                            for t in range(TT):
                                S = bank[2 + 2 * s + t][:, :].rearrange("p (a b) -> p a b", a=2)
                                lo, hi = (64 if swa and t else 0), P * (t + 1)
                                act.wait_ge(max_done, m * 2 + (t + 1))
                                act.wait_ge(pt_done, m * 2 + (t + 1))
                                if swa:
                                    act.activation(esink[:, 2 * t:2 * t + 2], esink[:, 2 * t:2 * t + 2], ACT.Exp)
                                for c in range(2):
                                    ins = act.activation(prob[:, t, c, lo:hi], S[:, c, lo:hi], ACT.Exp, scale=SCALE,
                                                         bias=nmax[:, 2 * t + c:2 * t + c + 1], accum_out=zsum[:, 2 * t + c:2 * t + c + 1])
                                ins.then_inc(exp_done, 1)
                            for t in range(TT):
                                act.wait_ge(pt_done, m * 2 + (t + 3))
                                T = bank[6 + t][:, :].rearrange("p (a b) -> p a b", a=4)
                                pick = slice(0, 2 * t + 2 if t else 1) if not swa else (slice(0, 4) if t else slice(0, 4, 2))
                                if not swa:
                                    pick = slice(0, t + 1)
                                act.activation(prob_t[:, t, pick, :], T[:, pick, :], ACT.Copy).then_inc(pt_read, 1)
                            for t in range(TT):
                                act.wait_ge(pv_done, m * 2 + (t + 1))
                                dst = one(proj[:, bass.ds(m + (T_SQ - HEADS_DIFF), 1), P * t:P * t + P]) if swa else one(o_nat[:, t, bass.ds(m, 1), :])
                                act.activation(dst, bank[6 + t][:, 0:P], ACT.Copy).then_inc(pv_read, 1)
                        for swa in (False, True):
                            if swa:
                                act.wait_ge(pad_done, 1)
                            with act.Fori(4 * swa, 4 * swa + 4) as n:
                                for s in range(2):
                                    unit(n * 2 + s, s, swa)
                        act.wait_ge(pv_read, 2 + 4 * HEADS_DIFF)
                        act.activation(o_hi[:, 16:24, :], proj[:, T_SQ:T_SQ + 8, :], ACT.Copy).then_inc(o_hi_done, 1)
                        act.wait_ge(ot_read, 4)
                        act.activation(o_hi[:, 8:16, :], proj[:, T_DQ:T_DQ + 8, :], ACT.Copy).then_inc(o_hi_done, 1)

                        blocks_loop(act, B_BR, N_BRANCH, lambda k, blk, ring, n, i: split_hi(act, blk + 1, (ring + 1) % 4))
                        src = lambda k: one(mix[:, bass.ds(k, 1), :])
                        act.wait_ge(mix_done, 1)
                        part_hi(act, src, 0, B_OUT % 2)

                        def ahead(k, blk, ring, n, i):
                            split_hi(act, blk + 1, (ring + 1) % 4)
                            part_hi(act, src, k + 1, (ring + 1) % 2)
                        blocks_loop(act, B_OUT, N_OUT - 1, ahead)

                    @block.vector
                    def _(dve):
                        ch = Chain(dve, s_dve)
                        norm_dve(dve, ch, V_MIXG, proj[:, 0:DC, :])
                        split_lo(dve, 0, 0)
                        blocks_loop(dve, 0, B_BR, lambda k, blk, ring, n, i: split_lo(dve, blk + 1, (ring + 1) % 4))
                        for i in range(2):
                            ch(dve.tensor_tensor(gated[:, 1, 64 * i:64 * i + 64], lamv[:, 2 * i, :], lamv[:, 2 * i + 1, :], ALU.mult))
                            ch(dve.tensor_reduce(lsum[:, i:i + 1], gated[:, 1, 64 * i:64 * i + 64], AX, ALU.add))
                        apar = vec[:, V_APAR:V_APAR + DC]
                        ch(dve.tensor_scalar(ls_p, apar, -1.0, None, ALU.mult))
                        dve.tensor_tensor(ls_e, apar, ls_p, ALU.min).then_inc(lam_sum, 1)
                        ch(dve.tensor_scalar(nsink, nsink, -1.0, None, ALU.mult))
                        dve.wait_ge(proj_done, N_IN + N_GATE)
                        with dve.Fori(0, DC) as m:
                            ch.enter(m, 3)
                            src = one(proj[:, bass.ds(m, 1), :])
                            dst = one(mix[:, bass.ds(m, 1), :])
                            ch(dve.tensor_scalar(dst, src, vec[:, bass.ds(m + (V_CONVW + 24), 1)], vec[:, bass.ds(m + V_CONVB, 1)], ALU.mult, ALU.add))
                            for j in (2, 1, 0):
                                back = 3 - j
                                ins = dve.scalar_tensor_tensor(out=one(mix[:, bass.ds(m, 1), back:SEQ]), in0=one(proj[:, bass.ds(m, 1), 0:SEQ - back]),
                                                               scalar=vec[:, bass.ds(m + (V_CONVW + 8 * j), 1)], in1=one(mix[:, bass.ds(m, 1), back:SEQ]),
                                                               op0=ALU.mult, op1=ALU.add)
                                if j:
                                    ch(ins)
                            ins.then_inc(conv_done, 1)
                        ch.leave(DC)
                        dve.wait_ge(lam_exp, 1)
                        ch(dve.tensor_scalar(ls_z, ls_e, 2.0, None, ALU.add))
                        ch(dve.reciprocal(ls_z, ls_z))
                        ch(dve.tensor_tensor(ls_z, ls_z, ls_e, ALU.mult))
                        ch(dve.tensor_tensor(ls_e, ls_z, ls_z, ALU.mult))
                        ch(dve.tensor_scalar(ls_p, ls_e, 1.0 / 15, None, ALU.mult))
                        for odd in (13, 11, 9, 7, 5, 3):
                            ch(dve.scalar_tensor_tensor(out=ls_p, in0=ls_p, scalar=1.0 / odd, in1=ls_e, op0=ALU.add, op1=ALU.mult))
                        ch(dve.scalar_tensor_tensor(out=ls_p, in0=ls_p, scalar=1.0, in1=ls_z, op0=ALU.add, op1=ALU.mult))
                        ch(dve.tensor_scalar(ls_z, apar, 0.0, LRU_C, ALU.min, ALU.mult))
                        ch(dve.scalar_tensor_tensor(out=log_a, in0=ls_p, scalar=-2.0 * LRU_C, in1=ls_z, op0=ALU.mult, op1=ALU.add))
                        ch(dve.tensor_tensor(nlam, lam_e[:, 1:2], lam_e[:, 0:1], ALU.subtract))
                        dve.tensor_tensor(nlam, nlam, lam_c[:, 0:1], ALU.subtract).then_inc(lam_done, 1)
                        dve.wait_ge(lru_sig, DC)
                        dve.tensor_tensor(mix[:, :, :], mix[:, :, :], gate_x, ALU.mult).then_inc(lru_xg, 1)
                        dve.wait_ge(lru_exp, DC)
                        den = hank[:].rearrange("p a b s -> p (a b) s")
                        for half in range(2):
                            u = gate_x[:, 4 * half:4 * half + 4, :]
                            ch(dve.tensor_scalar(den, u, -1.0, 1.0, ALU.mult, ALU.add))
                            ch(dve.reciprocal(den, den))
                            ins = dve.tensor_tensor(u, u, den, ALU.mult)
                            if half:
                                ins.then_inc(lru_u, 1)
                            else:
                                ch(ins)
                        dve.wait_ge(lru_sqrt, 1)
                        dve.wait_ge(lru_xg, 1)
                        ch(dve.tensor_tensor(mix[:, :, :], mix[:, :, :], gate_x, ALU.mult))
                        with dve.Fori(0, DC) as m:
                            ch.enter(m, 2)
                            h = one(gate_x[:, bass.ds(m, 1), :])
                            ch(dve.tensor_tensor_scan(h, one(proj[:, bass.ds(m, 1), :]), one(mix[:, bass.ds(m, 1), :]), 0.0, ALU.mult, ALU.add))
                            g = one(proj[:, bass.ds(m + T_LRUG, 1), :])
                            ch(dve.tensor_tensor(g, g, h, ALU.mult))
                        ch.leave(DC)
                        dve.sem_inc(lru_done, 1)
                        dve.wait_ge(o_hi_done, 1)
                        dve.tensor_tensor(o_lo[:, 0:8, :], proj[:, T_LRUG:T_LRUG + 8, :], o_hi[:, 0:8, :].bitcast(F32), ALU.subtract).then_inc(o_parts, 1)

                        def unit(m, s, swa):
                            for t in range(TT):
                                S = bank[2 + 2 * s + t][:, :].rearrange("p (a b) -> p a b", a=2)
                                lo, hi = (64 if swa and t else 0), P * (t + 1)
                                a = slice(2 * t, 2 * t + 2)
                                dve.wait_ge(scored, m * 2 + (t + 5))
                                ch(dve.tensor_reduce(top_s[:, a], S[:, :, lo:hi], AX, ALU.max))
                                if swa:
                                    ns = small[:, bass.ds(m * 2 + (64 - HEADS_SWA), 2)]
                                    ch(dve.scalar_tensor_tensor(out=nmax[:, a], in0=top_s[:, a], scalar=-SCALE, in1=ns, op0=ALU.mult, op1=ALU.min))
                                    dve.tensor_tensor(esink[:, a], nmax[:, a], ns, ALU.subtract).then_inc(max_done, 1)
                                else:
                                    dve.tensor_scalar(nmax[:, a], top_s[:, a], -SCALE, None, ALU.mult).then_inc(max_done, 1)
                            for t in range(TT):
                                lo, hi = (64 if swa and t else 0), P * (t + 1)
                                a = slice(2 * t, 2 * t + 2)
                                z0, z1 = rz[:, 2 * t:2 * t + 1], rz[:, 2 * t + 1:2 * t + 2]
                                dve.wait_ge(exp_done, m * 2 + (t + 5))
                                if swa:
                                    ch(dve.tensor_tensor(zsum[:, a], zsum[:, a], esink[:, a], ALU.add))
                                ch(dve.reciprocal(rz[:, a], zsum[:, a]))
                                if swa:
                                    dve.tensor_scalar(prob[:, t, 0, lo:hi], prob[:, t, 0, lo:hi], z0, None, ALU.mult)
                                    dve.tensor_scalar(prob[:, t, 1, lo:hi], prob[:, t, 1, lo:hi], z1, None, ALU.mult).then_inc(attn_done, 1)
                                else:
                                    dve.tensor_scalar(z1, z1, nlam, None, ALU.mult)
                                    ch(dve.tensor_scalar(prob[:, t, 0, lo:hi], prob[:, t, 0, lo:hi], z0, None, ALU.mult))
                                    dve.scalar_tensor_tensor(out=prob[:, t, 0, lo:hi], in0=prob[:, t, 1, lo:hi], scalar=z1, in1=prob[:, t, 0, lo:hi],
                                                             op0=ALU.mult, op1=ALU.add).then_inc(attn_done, 1)
                        with dve.Fori(0, 4) as n:
                            ch.enter(n, 2 * 2 * 3)
                            for s in range(2):
                                unit(n * 2 + s, s, False)
                        ch.leave(4)
                        dve.wait_ge(pt_done, 2 + 2 * HEADS_DIFF)
                        dve.memset(prob[:, 1, :, 0:64], 0.0).then_inc(pad_done, 1)
                        with dve.Fori(4, 8) as n:
                            ch.enter(n - 4, 2 * 2 * 4)
                            for s in range(2):
                                unit(n * 2 + s, s, True)
                        ch.leave(4)
                        dve.wait_ge(pv_read, 2 + 4 * HEADS_DIFF)
                        ch(dve.tensor_tensor(o_sq, o_nat, o_nat, ALU.mult))
                        ch(dve.tensor_reduce(oss, o_sq.rearrange("p a b s -> p (a b) s"), AX, ALU.add))
                        dve.tensor_scalar(oss, oss, 1.0 / P, EPS, ALU.mult, ALU.add).then_inc(on_sum, 1)
                        dve.wait_ge(on_pow, 1)
                        on = o_nat.rearrange("p a b s -> p (a b) s")
                        dve.tensor_tensor(on, on, spread(orstd.rearrange("p (a o) -> p a o", o=1), 2, P), ALU.mult).then_inc(on_done, 1)
                        for i in range(4):
                            t, h = i // 2, 4 * (i % 2)
                            dve.wait_ge(ot_done, i + 1)
                            dve.tensor_scalar(proj[:, T_DQ + h:T_DQ + h + 4, P * t:P * t + P], bank[2 + i][:, :].rearrange("p (a b) -> p a b", a=4),
                                              vec[:, V_SUBLN:V_SUBLN + 1], lam_c[:, 1:2], ALU.mult, ALU.mult).then_inc(ot_read, 1)
                        for k, b in ((2, 2), (3, 1)):
                            dve.wait_ge(o_hi_done, k)
                            dve.wait_ge(ot_read, 4)
                            dve.tensor_tensor(o_lo[:, 8 * b:8 * b + 8, :], proj[:, OUTS[b]:OUTS[b] + 8, :], o_hi[:, 8 * b:8 * b + 8, :].bitcast(F32), ALU.subtract).then_inc(o_parts, 1)
                        ch(dve.memset(mix[:, :, :], 0.0))
                        for b in range(3):
                            with dve.Fori(0, 2) as n:
                                ch.enter(n, 8)
                                for i in range(4):
                                    m = 4 * n + i
                                    blk = 4 * n + (B_BR + 8 * b + i)
                                    ring = (B_BR + 8 * b + i) % 4
                                    split_lo(dve, blk + 1, (ring + 1) % 4)
                                    dve.wait_ge(w_used, blk * 2 + 6)
                                    ins = dve.tensor_tensor(gated[:, i % 2, :], one(gates[:, bass.ds(m + 8 * b, 1), :]), bank[ring % 2][:, 0:SEQ], ALU.mult)
                                    ch(ins)
                                    dve.sem_inc(up_read, 1)
                                    acc = one(mix[:, bass.ds(m, 1), :])
                                    ch(dve.tensor_tensor(acc, acc, gated[:, i % 2, :], ALU.add))
                            ch.leave(2)
                        dve.sem_inc(mix_done, 1)
                        src = lambda k: one(mix[:, bass.ds(k, 1), :])
                        part_lo(dve, src, 0, B_OUT % 2)

                        def ahead(k, blk, ring, n, i):
                            split_lo(dve, blk + 1, (ring + 1) % 4)
                            part_lo(dve, src, k + 1, (ring + 1) % 2)
                        blocks_loop(dve, B_OUT, N_OUT - 1, ahead)
                        add_to_x(dve, bank[2:6], 2 * MIX_BLOCKS + 4)

                    @block.tensor
                    def _(pe):
                        pe.sem_inc(w_used, 4)
                        pe.sem_inc(up_read, 2)
                        pe.sem_inc(scored, 4)
                        pe.sem_inc(pt_done, 2)
                        pe.sem_inc(pv_read, 2)
                        norm_pe(pe)
                        pe.wait_ge(h_done, DC)
                        blocks_loop(pe, 0, B_BR, lambda k, blk, ring, n, i: up_block(
                            pe, blk, ring, blk, bank[ring % 2][:, 0:SEQ], lambda c: h_hi[:, c, :], lambda c: h_lo[:, c, :]))
                        for m in range(DC):
                            pe.wait_ge(conv_done, m + 1)
                            if m >= 2:
                                pe.wait_ge(lru_sig, m - 1)
                            for kind in range(2):
                                for b in range(2):
                                    r = slice(64 * b, 64 * b + 64)
                                    ins = pe.matmul(bank[2 + m % 2][r, SEQ * kind:SEQ * kind + SEQ], lru_ws[r, m, kind, :], mix[r, m, :], start=True, stop=True)
                            ins.then_inc(lru_mm, 1)
                        pe.wait_ge(lru_done, 1)
                        for i in range(5):
                            if i >= 2:
                                pe.wait_ge(vt_read, i - 1)
                            for j in range(4 if i < 4 else 2):
                                src = proj[:, T_DV + 4 * (i % 2) + j, P * (i // 2):P * (i // 2) + P] if i < 4 else proj[:, T_SV, P * j:P * j + P]
                                ins = pe.transpose(bank[6 + i % 2][:, P * j:P * j + P], src, ident)
                            ins.then_inc(vt_done, 1)
                        pe.wait_ge(vt_read, 5)
                        pe.wait_ge(lru_sig, DC)

                        def scores(m, s, swa):
                            pe.wait_ge(staged, m + 1)
                            pe.wait_ge(hank_in[s], m * 8 + (16 - 8 * s))
                            pe.wait_ge(exp_done, m * 2 + 2)
                            for t in range(TT):
                                S = bank[2 + 2 * s + t][:, :].rearrange("p (a b) -> p a b", a=2)
                                lo, hi = (64 if swa and t else 0), P * (t + 1)
                                f = P if t == 0 else 0
                                for c in range(2):
                                    pe.matmul(S[:, c, lo:hi], flip8, hank[:, s, c if swa else 0, lo + f:hi + f], start=True, stop=False)
                                    pe.matmul(S[:, c, lo:hi], qk[:, s, c, P * t:P * t + P], qk[:, s, 2, lo:hi], start=False, stop=False)
                                    if swa and t:
                                        pe.matmul(S[:, c, 64:128], row_hi, neg, start=False, stop=False)
                                    ins = pe.matmul(S[:, c, hi - 64:hi], row_lo, neg, start=False, stop=True)
                                ins.then_inc(scored, 1)

                        def values(m, s, swa, g):
                            for t in range(TT):
                                pe.wait_ge(attn_done, m * 2 + (t + 1))
                                pe.wait_ge(pv_read, m * 2 + (t + 1))
                                for c in range(2 if swa else 1):
                                    for kt in range(t + 1):
                                        at = P * (2 * c + kt)
                                        ins = pe.transpose(bank[6 + t][:, at:at + P], prob[:, t, c, P * kt:P * kt + P], ident)
                                ins.then_inc(pt_done, 1)
                            for t in range(TT):
                                pe.wait_ge(pt_read, m * 2 + (t + 1))
                                for c in range(2 if swa else 1):
                                    for kt in range(t + 1):
                                        first, last = kt == 0, kt == t
                                        if swa:
                                            ins = pe.matmul(bank[6 + t][64 * c:64 * c + 64, 0:P], v_nat[:, kt, D + 64 * g:D + 64 * g + 64], prob_t[:, t, 2 * c + kt, :], start=first, stop=last)
                                        else:
                                            ins = pe.matmul(bank[6 + t][:, 0:P], prob_t[:, t, kt, :], v_nat[:, kt, bass.ds(m * P, P)], start=first, stop=last)
                                ins.then_inc(pv_done, 1)
                        scores(0, 0, False)
                        with pe.Fori(0, 3) as n:
                            scores(n * 2 + 1, 1, False)
                            values(n * 2, 0, False, 0)
                            scores(n * 2 + 2, 0, False)
                            values(n * 2 + 1, 1, False, 0)
                        scores(7, 1, False)
                        values(6, 0, False, 0)
                        scores(8, 0, True)
                        values(7, 1, False, 0)
                        for g, turns in ((0, (4, 6)), (1, (6, 7))):
                            with pe.Fori(*turns) as n:
                                scores(n * 2 + 1, 1, True)
                                values(n * 2, 0, True, g)
                                scores(n * 2 + 2, 0, True)
                                values(n * 2 + 1, 1, True, g)
                        scores(15, 1, True)
                        values(14, 0, True, 1)
                        values(15, 1, True, 1)
                        pe.wait_ge(on_done, 1)
                        for i in range(4):
                            for j in range(4):
                                ins = pe.transpose(bank[2 + i][:, P * j:P * j + P], o_nat[:, i // 2, 4 * (i % 2) + j, :], ident)
                            ins.then_inc(ot_done, 1)
                        pe.wait_ge(o_parts, 3)
                        for b in range(3):
                            blocks_loop(pe, B_BR + 8 * b, 8, lambda k, blk, ring, n, i: up_block(
                                pe, blk, ring, blk, bank[ring % 2][:, 0:SEQ], lambda c: o_hi[:, 8 * b + c, :], lambda c: o_lo[:, 8 * b + c, :]))
                        pe.wait_ge(ot_read, 4)
                        down_block(pe, B_OUT, B_OUT % 4, 0, bank[2:6], True, False)
                        blocks_loop(pe, B_OUT + 1, N_OUT - 2, lambda k, blk, ring, n, i: down_block(pe, blk, ring, k + 1, bank[2:6], False, False))
                        down_block(pe, MIX_BLOCKS - 1, (MIX_BLOCKS - 1) % 4, N_OUT - 1, bank[2:6], False, True)
            clear()
            with ExitStack() as part:
                A = sb(part, "A", [P, KEYS, SEQ])
                picks = sb(part, "picks", [P, 3, TT, P])
                picks_t = sb(part, "picks_t", [P, 3, SEQ])
                hot = sb(part, "hot", [P, 2, 2, 4, P])
                cur = sb(part, "cur", [P, 2, P])
                best = sb(part, "best", [P, TOPK])
                best_at = sb(part, "best_at", [P, TOPK], U32)
                best_f = sb(part, "best_f", [P, TOPK])
                whole = sb(part, "whole", [P, TT, P], I32)
                xr = A[:, 0:8, :].rearrange("p (a b) s -> p a (b s)", a=TT)
                h_f = A[:, 8:16, :]
                FREE = 96
                keys_t = A[:, 88:96, :].rearrange("p a (b k) -> p (a b) k", b=2)
                score = A[:, 96:112, :].rearrange("p a (b k) -> p (a b) k", b=2)
                q_t = A[:, 112:128, :]
                flat = A[:, 112:128, :].rearrange("p a b -> p (a b)")
                UNITS = TT * PEER_HEADS
                spot = [0]

                def scratch(n, k):
                    a = spot[0]
                    spot[0] += n * k
                    return flat[:, a:a + n * k].rearrange("p (n k) -> p n k", n=n)
                cand, cand_i = scratch(UNITS, N_CAND), scratch(UNITS, N_CAND)
                hit = scratch(TOPK, N_CAND)
                s16, i16 = scratch(2 * UNITS, TOPK), scratch(2 * UNITS, TOPK)
                sel_s, sel_i = scratch(UNITS, TOPK), scratch(UNITS, TOPK)
                B_U, B_V = N_WQ, N_WQ + N_U
                VEC_LOADS = 16

                with nc.Block() as block:
                    @block.sync
                    def _(sp):
                        sp.sem_inc(w_parts, 8)
                        sp.dma_start(vec[:], vecs[bass.ds(layer, 1)].rearrange("o p c -> (o p) c")).then_inc(vec_in, 16)
                        sp.dma_start(keys_t, subkeys[bass.ds(layer, 1)].rearrange("o p a k -> (o p) a k")).then_inc(const_in, 16)
                        load_pairs(sp, layer, MIX_BLOCKS // 2, 0, PEER_BLOCKS // 2)

                    @block.gpsimd
                    def _(pool):
                        norm_pool(pool)

                    @block.scalar
                    def _(act):
                        ch = Chain(act, s_act)
                        norm_act(act, ch)
                        split_hi(act, 0, 0)

                        def read_up(dst, func):
                            def body(k, blk, ring, n, i):
                                split_hi(act, blk + 1, (ring + 1) % 4)
                                act.wait_ge(w_used, blk * 2 + 6)
                                act.activation(one(dst(k)), bank[ring % 2][:, 0:SEQ], func).then_inc(up_read, 1)
                            return body
                        blocks_loop(act, 0, N_WQ, read_up(lambda k: q_t[:, bass.ds(k, 1), :] if not isinstance(k, int) else q_t[:, k:k + 1, :], ACT.Copy))
                        for i in range(8):
                            act.wait_ge(sc_done, i + 1)
                            act.activation(score[:, 4 * i:4 * i + 4, :].rearrange("p a b -> p (a b)"), bank[2 + i % 6][:, :], ACT.Copy).then_inc(sc_read, 1)
                        table_of(act, ch, ACT.Gelu_apprx_tanh)
                        blocks_loop(act, B_U, FREE, read_up(lambda k: A[:, bass.ds(k, 1), :], ACT.Gelu_apprx_tanh))
                        act.wait_ge(soft_in, 1)
                        act.activation(sel_s, sel_s, ACT.Exp).then_inc(soft_out, 1)
                        act.wait_ge(routed, 1)
                        table_of(act, ch, ACT.Gelu_apprx_tanh)
                        blocks_loop(act, B_U + FREE, N_U - FREE, read_up(lambda k: A[:, bass.ds(k + FREE, 1), :], ACT.Gelu_apprx_tanh))
                        src = lambda k: one(A[:, bass.ds(k, 1), :])
                        act.wait_ge(g_read, N_GROUPS)
                        part_hi(act, src, 0, 0)

                        def ahead(k, blk, ring, n, i):
                            split_hi(act, blk + 1, (ring + 1) % 4)
                            part_hi(act, src, k + 1, (ring + 1) % 2)
                        blocks_loop(act, B_V, N_V - 1, ahead)

                    @block.vector
                    def _(dve):
                        ch = Chain(dve, s_dve, drains=True)
                        norm_dve(dve, ch, V_FFNG, h_f)
                        split_lo(dve, 0, 0)
                        ahead = lambda k, blk, ring, n, i: split_lo(dve, blk + 1, (ring + 1) % 4)
                        blocks_loop(dve, 0, N_WQ, ahead)
                        dve.wait_ge(sc_read, 8)

                        def top16(values, again):
                            ch(dve.max(best[:, 0:8], values))
                            ch(dve.max_index(best_at[:, 0:8], best[:, 0:8], values))
                            ch(dve.match_replace(again, best[:, 0:8], values, TAKEN))
                            ch(dve.max(best[:, 8:16], again))
                            ch(dve.max_index(best_at[:, 8:16], best[:, 8:16], again))

                        with dve.Fori(0, 8) as n:
                            ch.enter(n, 4 * 8)
                            for i in range(4):
                                split_lo(dve, n * 4 + (B_U + i + 1), (i + 1) % 4)
                                u = n * 4 + i
                                ch(dve.tensor_copy(cur[:, 0, :], one(score[:, bass.ds(u, 1), :])))
                                top16(cur[:, 0, :], cur[:, 1, :])
                                ch(dve.tensor_copy(one(s16[:, bass.ds(u, 1), :]), best[:]))
                                ch(dve.tensor_copy(one(i16[:, bass.ds(u, 1), :]), best_at[:]))
                        ch.leave(8)
                        s_pair = s16.rearrange("p (u c) k -> p u c k", c=2)
                        i_pair = i16.rearrange("p (u c) k -> p u c k", c=2)
                        for i in range(PAIR_RANKS + 1):
                            m = CAND_N[i] if i < PAIR_RANKS else TOPK - PAIR_RANKS
                            o = CAND_OFF[i]
                            if i < PAIR_RANKS:
                                s1, s2 = spread(s_pair[:, :, 0, i:i + 1], 2, m), s_pair[:, :, 1, 0:m]
                                i1, i2 = spread(i_pair[:, :, 0, i:i + 1], 2, m), i_pair[:, :, 1, 0:m]
                            else:
                                s1, s2 = s_pair[:, :, 0, i:TOPK], spread(s_pair[:, :, 1, 0:1], 2, m)
                                i1, i2 = i_pair[:, :, 0, i:TOPK], spread(i_pair[:, :, 1, 0:1], 2, m)
                            dve.tensor_tensor(cand[:, :, o:o + m], s1, s2, ALU.add)
                            ch(dve.scalar_tensor_tensor(out=cand_i[:, :, o:o + m], in0=i1, scalar=float(KEYS), in1=i2, op0=ALU.mult, op1=ALU.add))
                        with dve.Fori(0, UNITS) as n:
                            ch.enter(n, 11)
                            for i in range(4):
                                split_lo(dve, n * 4 + (B_U + 33 + i), (i + 1) % 4)
                            ch(dve.tensor_copy(cur[:, 0, 0:N_CAND], one(cand[:, bass.ds(n, 1), :])))
                            top16(cur[:, 0, 0:N_CAND], cur[:, 1, 0:N_CAND])
                            ch(dve.tensor_copy(one(sel_s[:, bass.ds(n, 1), :]), best[:]))
                            ch(dve.tensor_copy(best_f[:], best_at[:]))
                            ch(dve.tensor_tensor(hit, spread(best_f[:].rearrange("p (k o) -> p k o", o=1), 2, N_CAND),
                                                 spread(iota[:, 0:N_CAND].rearrange("p (o c) -> p o c", o=1), 1, TOPK), ALU.is_equal))
                            ch(dve.tensor_tensor(hit, hit, spread(cand_i[:, bass.ds(n, 1), :], 1, TOPK), ALU.mult))
                            ch(dve.tensor_reduce(one(sel_i[:, bass.ds(n, 1), :]), hit, AX, ALU.add))
                        ch.leave(UNITS)
                        ch(dve.tensor_copy(best[:], sel_s[:, :, 0:1].rearrange("p u o -> p (u o)")))
                        dve.tensor_tensor(sel_s, sel_s, spread(best[:].rearrange("p (u o) -> p u o", o=1), 2, TOPK), ALU.subtract).then_inc(soft_in, 1)
                        sel_i2 = sel_i.rearrange("p (a h) k -> p a (h k)", a=TT)
                        ch(dve.tensor_copy(whole[:], sel_i2))
                        dve.tensor_scalar(whole[:], whole[:], 7, None, ALU.logical_shift_right).then_inc(s_dve, 1)
                        ch.n += 1
                        dve.wait_ge(s_dve, ch.value())
                        ch(dve.tensor_copy(picks[:, 0, :, :], whole[:]))
                        ch(dve.scalar_tensor_tensor(out=picks[:, 1, :, :], in0=picks[:, 0, :, :], scalar=-float(KEYS), in1=sel_i2, op0=ALU.mult, op1=ALU.add))
                        dve.wait_ge(soft_out, 1)
                        ch(dve.tensor_reduce(best_f[:], sel_s, AX, ALU.add))
                        ch(dve.reciprocal(best_f[:], best_f[:]))
                        dve.tensor_tensor(picks[:, 2, :, :].rearrange("p a (h k) -> p (a h) k", h=PEER_HEADS), sel_s,
                                          spread(best_f[:].rearrange("p (u o) -> p u o", o=1), 2, TOPK), ALU.mult).then_inc(routed, 1)
                        with dve.Fori(0, 8) as n:
                            for i in range(4):
                                split_lo(dve, n * 4 + (B_U + 97 + i), (i + 1) % 4)
                        for i in range(3):
                            dve.wait_ge(rt_done, i + 1)
                            ch(dve.tensor_copy(picks_t[:, i, :], bank[4 + i][:, 0:SEQ]))
                        dve.wait_ge(up_read, 2 + B_V)

                        def one_hot(g, s):
                            for k in range(4):
                                t = g * 4 + k
                                dve.tensor_scalar(hot[:, s, 0, k, :], iota, picks_t[:, 0, bass.ds(t, 1)], None, ALU.is_equal)
                                ins = dve.tensor_scalar(hot[:, s, 1, k, :], iota, picks_t[:, 1, bass.ds(t, 1)], picks_t[:, 2, bass.ds(t, 1)], ALU.is_equal, ALU.mult)
                            ins.then_inc(hot_done, 1)

                        def weigh(g, s):
                            dve.wait_ge(g_done, g + 1)
                            a = A[:, :, bass.ds(g * 4, 4)]
                            dve.tensor_tensor(a, a, bank[2 + s][:, :].rearrange("p (k j) -> p j k", k=4), ALU.mult).then_inc(g_read, 1)
                        one_hot(0, 0)
                        with dve.Fori(0, N_GROUPS // 2 - 1) as n:
                            one_hot(n * 2 + 1, 1)
                            weigh(n * 2, 0)
                            one_hot(n * 2 + 2, 0)
                            weigh(n * 2 + 1, 1)
                        one_hot(N_GROUPS - 1, 1)
                        weigh(N_GROUPS - 2, 0)
                        weigh(N_GROUPS - 1, 1)
                        src = lambda k: one(A[:, bass.ds(k, 1), :])
                        part_lo(dve, src, 0, 0)

                        def ahead_v(k, blk, ring, n, i):
                            split_lo(dve, blk + 1, (ring + 1) % 4)
                            part_lo(dve, src, k + 1, (ring + 1) % 2)
                        blocks_loop(dve, B_V, N_V - 1, ahead_v)
                        add_to_x(dve, bank[4:8], 2 * PEER_BLOCKS + 4)

                    @block.tensor
                    def _(pe):
                        pe.sem_inc(w_used, 4)
                        pe.sem_inc(up_read, 2)
                        norm_pe(pe)
                        pe.wait_ge(h_done, DC)
                        h_rhs = (lambda c: h_hi[:, c, :], lambda c: h_lo[:, c, :])
                        body = lambda k, blk, ring, n, i: up_block(pe, blk, ring, blk, bank[ring % 2][:, 0:SEQ], *h_rhs)
                        blocks_loop(pe, 0, N_WQ, body)
                        pe.wait_ge(up_read, 2 + N_WQ)
                        pe.wait_ge(const_in, 16)
                        for i in range(8):
                            if i >= 6:
                                pe.wait_ge(sc_read, i - 5)
                            for j in range(4):
                                t, hc = i // 4, 4 * (i % 4) + j
                                ins = pe.matmul(bank[2 + i % 6][:, P * j:P * j + P], q_t[:, hc, P * t:P * t + P], keys_t[:, hc, :], start=True, stop=True)
                            ins.then_inc(sc_done, 1)
                        blocks_loop(pe, B_U, N_U, body)
                        pe.wait_ge(routed, 1)
                        for i in range(3):
                            for t in range(TT):
                                ins = pe.transpose(bank[4 + i][:, P * t:P * t + P], picks[:, i, t, :], ident)
                            ins.then_inc(rt_done, 1)

                        def weights(g, s):
                            pe.wait_ge(hot_done, g + 1)
                            for k in range(4):
                                ins = pe.matmul(bank[2 + s][:, P * k:P * k + P], hot[:, s, 0, k, :], hot[:, s, 1, k, :], start=True, stop=True)
                            ins.then_inc(g_done, 1)
                        with pe.Fori(0, N_GROUPS // 2) as n:
                            for s in range(2):
                                weights(n * 2 + s, s)
                        down_block(pe, B_V, 0, 0, bank[4:8], True, False)
                        blocks_loop(pe, B_V + 1, N_V - 2, lambda k, blk, ring, n, i: down_block(pe, blk, ring, k + 1, bank[4:8], False, False))
                        down_block(pe, PEER_BLOCKS - 1, (PEER_BLOCKS - 1) % 4, N_V - 1, bank[4:8], False, True)
            clear()

        with ExitStack() as part:
            xr = sb(part, "xr", [P, TT, D])
            g_all = sb(part, "g_all", [P, D])
            with nc.Block() as block:
                @block.sync
                def _(sp):
                    sp.dma_start(g_all[:], spread(final_g, 0, P)).then_inc(const_in, 16)
                    for t in range(TT):
                        sp.wait_ge(x_done, t + 1)
                        sp.dma_start(out[P * t:P * t + P, :], xr[:, t, :]).then_inc(stored, 16)
                    sp.wait_ge(stored, 16 * TT)

                @block.scalar
                def _(act):
                    norm_act(act, Chain(act, s_act))

                @block.gpsimd
                def _(pool):
                    norm_pool(pool)

                @block.vector
                def _(dve):
                    dve.wait_ge(const_in, 16)
                    dve.wait_ge(rstd_done, 1)
                    for t in range(TT):
                        dve.scalar_tensor_tensor(out=xr[:, t, :], in0=x[:, t, :], scalar=rstd[:, t:t + 1], in1=g_all[:],
                                                 op0=ALU.mult, op1=ALU.mult).then_inc(x_done, 1)


def buckets():
    rel = np.arange(N_REL) - (SEQ - 1)
    n = np.abs(rel)
    large = 8 + (np.log(np.maximum(n, 1).astype(np.float32) / 8) / np.float32(np.log(128.0)) * 8).astype(np.int32)
    bucket = np.where(rel > 0, 16, 0) + np.where(n < 8, n, np.minimum(large, 15))
    return (bucket[None, :] == np.arange(32)[:, None]).astype(np.float32)


def constants():
    c = np.zeros((P, N_CST), np.float32)
    c[:, C_ID:C_ID + P] = np.eye(P)
    c[:, C_FLIP:C_FLIP + P] = np.eye(P)[::-1] / SCALE
    c[:, C_IOTA:C_IOTA + P] = np.arange(P)
    c[0, C_LO:C_LO + 64] = 1
    c[0, C_HI + 64:C_HI + P] = 1
    c[0, C_NEG:C_NEG + CHUNK] = MASKED
    return c


def kernel(**inputs):
    import math
    import concourse.bacc as _bacc
    from concourse.bass_utils import run_bass_kernel_spmd as _run
    a = {k: np.asarray(v) for k, v in inputs.items()}

    def up(w):
        return np.ascontiguousarray(w.reshape(DC, P, -1, P).transpose(2, 1, 0, 3)).reshape(-1, P, D)

    blocks = []
    for l in range(DEPTH):
        blocks += [up(a["w_in"][l]), up(a["w_gate"][l])] + [up(a["w_branch"][l, b]) for b in range(3)]
        blocks += [a["w_out"][l].reshape(DC, P, D), up(a["peer_wq"][l])]
        u = a["peer_u"][l].reshape(P, KEYS, DC, P)
        blocks.append(u.transpose(1, 3, 2, 0).reshape(KEYS, P, D))
        blocks.append(a["peer_v"][l].reshape(P, KEYS, D).transpose(1, 0, 2))
    stream = np.concatenate(blocks).reshape(DEPTH * LAYER_PAIRS, 2, P, D)

    def cols(v):
        return v.reshape(DEPTH, -1, P).transpose(0, 2, 1)

    vecs = np.concatenate([cols(a[n]) for n in ("norm_mix_g", "conv_w", "conv_b", "lru_bx", "lru_ba", "lru_a_param", "b_gate",
                                                "norm_ffn_g", "diff_subln_g")], axis=2)
    lru = np.stack([a["lru_wx"], a["lru_wa"]], axis=3)
    lru = lru.reshape(DEPTH, DC, 2, 64, 2, 64).transpose(0, 2, 3, 1, 4, 5).reshape(DEPTH, P, DC, 2, 64)
    subk = a["peer_subkeys"].reshape(DEPTH, 2 * PEER_HEADS, KEYS, P).transpose(0, 3, 1, 2)
    init = [0.8 - 0.6 * math.exp(-0.3 * l) for l in range(DEPTH)]
    arrays = {
        "stream": stream, "vecs": vecs, "cst": constants(), "rel_bias": a["rel_bias"], "bucket_onehot": buckets(),
        "lam_consts": np.array([[i, 1.0 - i] for i in init], np.float32), "final_g": a["final_norm_g"].reshape(1, D),
        "diff_lambda": a["diff_lambda"].reshape(DEPTH, -1), "sinks": a["swa_sinks"], "lru_w": lru, "subkeys": subk,
        "x_in": a["x"].reshape(SEQ, D),
    }
    arrays = {k: np.ascontiguousarray(v) for k, v in arrays.items()}
    nc = _bacc.Bacc("TRN2", target_bir_lowering=False, num_devices=1, dynamic_dma_scratch_size=8192)
    args = [nc.dram_tensor(k, v.shape, mybir.dt.from_np(v.dtype), kind="ExternalInput").ap() for k, v in arrays.items()]
    out = nc.dram_tensor("out", (SEQ, D), F32, kind="ExternalOutput").ap()
    trunk(nc, *args, out)
    r = _run(nc, [arrays], core_ids=[0])
    return r.results[0]["out"].reshape(1, SEQ, D)
```

```python
import concourse.bass as bass
from concourse import mybir
from contextlib import ExitStack
import numpy as np

F32 = mybir.dt.float32
F32R = mybir.dt.float32r
U32 = mybir.dt.uint32
I32 = mybir.dt.int32
ALU = mybir.AluOpType
ACT = mybir.ActivationFunctionType
AX = mybir.AxisListType.X

P = 128
DEPTH = 2
SEQ = 256
D = 1024
DC = D // P
TT = SEQ // P
HEADS_DIFF = 8
HEADS_SWA = 16
CHUNK = 64
N_GROUPS = SEQ // 4
TOPK = 16
PEER_HEADS = 8
KEYS = 128
EPS = 1e-6
LRU_C = 8.0
SCALE = 0.125
MASKED = -1e30
TAKEN = -3e38

N_IN = 50
N_GATE = 24
N_BRANCH = 24
N_OUT = 8
N_WQ = 16
N_U = KEYS
N_V = KEYS
T_LRUX, T_LRUG, T_DQ, T_DK, T_DV, T_SQ, T_SK, T_SV = 0, 8, 16, 24, 32, 40, 48, 49
MIX_BLOCKS = N_IN + N_GATE + N_BRANCH + N_OUT
PEER_BLOCKS = N_WQ + N_U + N_V
LAYER_PAIRS = (MIX_BLOCKS + PEER_BLOCKS) // 2

V_MIXG, V_CONVW, V_CONVB, V_BX, V_BA, V_APAR, V_BGATE, V_FFNG, V_SUBLN, N_VEC = 0, 8, 40, 48, 56, 64, 72, 96, 104, 105
C_ID, C_FLIP, C_IOTA, C_LO, C_HI, C_NEG, N_CST = 0, 128, 256, 384, 512, 640, 704

N_REL = 384
N_BIAS = HEADS_DIFF + HEADS_SWA

CAND_N = [TOPK // (i + 1) for i in range(TOPK)]
CAND_OFF = [sum(CAND_N[:i]) for i in range(TOPK)]
N_CAND = sum(CAND_N)
PAIR_RANKS = sum(n > 1 for n in CAND_N)


def spread(ap, dim, n):
    shape = list(ap.shape)
    shape[dim] = n
    return ap.to_broadcast(shape)


class Chain:

    def __init__(self, eng, sem, drains=False):
        self.eng, self.sem, self.drains = eng, sem, drains
        self.base, self.turn, self.per, self.n = 0, None, 0, 0

    def value(self):
        done = self.base + self.n
        return done if self.turn is None else self.turn * self.per + done

    def __call__(self, ins):
        self.n += 1
        ins.then_inc(self.sem, 1)
        if self.turn is not None and self.drains:
            self.eng.drain()
        else:
            self.eng.wait_ge(self.sem, self.value())

    def enter(self, turn, per):
        self.base, self.turn, self.per, self.n = self.base + self.n, turn, per, 0

    def leave(self, turns):
        assert self.n == self.per, (self.n, self.per)
        self.base, self.turn, self.n = self.base + turns * self.per, None, 0


def blocks_loop(eng, first, count, body):
    fours = count // 4
    if fours:
        with eng.Fori(0, fours) as n:
            for i in range(4):
                body(n * 4 + i, n * 4 + (first + i), (first + i) % 4, n, i)
    for b in range(4 * fours, count):
        body(b, first + b, (first + b) % 4, None, b - 4 * fours)


def trunk(nc, stream, vecs, cst, rel_bias, bucket_onehot, lam_consts, final_g, diff_lambda, sinks,
          lru_w, subkeys, x_in, out):
    top = ExitStack()

    def sb(stack, name, shape, dt=F32):
        return stack.enter_context(nc.sbuf_tensor(name, shape, dt))

    with top:
        sem_list = []

        def sem(name):
            s = top.enter_context(nc.semaphore(name))
            sem_list.append(s)
            return s

        x = sb(top, "x", [P, TT, D])
        consts = sb(top, "consts", [P, N_CST])
        vec = sb(top, "vec", [P, N_VEC])
        raw = sb(top, "raw", [P, 2, 2, D])
        w_hi = sb(top, "w_hi", [P, 4, 512], F32R)
        w_lo = sb(top, "w_lo", [P, 4, 512], F32R)
        h_hi = sb(top, "h_hi", [P, DC, SEQ], F32R)
        h_lo = sb(top, "h_lo", [P, DC, SEQ], F32R)
        a_hi = sb(top, "a_hi", [P, 2, SEQ], F32R)
        a_lo = sb(top, "a_lo", [P, 2, SEQ], F32R)
        ss = sb(top, "ss", [P, TT])
        rstd = sb(top, "rstd", [P, TT])
        warm = sb(top, "warm", [P, 1])
        halfpow = sb(top, "halfpow", [P, 16])
        bank = [top.enter_context(nc.psum_tensor(f"bank{i}", [P, 512], F32)) for i in range(8)]
        ident = consts[:, C_ID:C_ID + P]
        flip8 = consts[:, C_FLIP:C_FLIP + P]
        iota = consts[:, C_IOTA:C_IOTA + P]
        row_lo = consts[0:1, C_LO:C_LO + P]
        row_hi = consts[0:1, C_HI:C_HI + P]
        neg = consts[0:1, C_NEG:C_NEG + CHUNK]
        tdram = nc.dram_tensor("rel_line", (N_BIAS, N_REL), F32, kind="Internal").ap()
        hankel = nc.dram_tensor("rel_hankel", (N_BIAS, P, SEQ), F32, kind="Internal").ap()

        raw_in = [sem(f"raw_in{i}") for i in range(2)]
        w_hi_done = sem("w_hi_done")
        w_parts = sem("w_parts")
        w_used = sem("w_used")
        up_read = sem("up_read")
        a_hi_done = sem("a_hi_done")
        a_parts = sem("a_parts")
        s_act, s_dve, s_pool = sem("s_act"), sem("s_dve"), sem("s_pool")
        sums_done = sem("sums_done")
        rstd_done = sem("rstd_done")
        xr_done = sem("xr_done")
        tp_done = sem("tp_done")
        tp_read = sem("tp_read")
        h_done = sem("h_done")
        const_in = sem("const_in")
        vec_in = sem("vec_in")
        stored = sem("stored")
        once = sem("once")
        proj_done = sem("proj_done")
        lam_sum, lam_exp, lam_done = sem("lam_sum"), sem("lam_exp"), sem("lam_done")
        conv_done, lru_mm, lru_sig = sem("conv_done"), sem("lru_mm"), sem("lru_sig")
        lru_xg, lru_exp, lru_u, lru_sqrt, lru_done = sem("lru_xg"), sem("lru_exp"), sem("lru_u"), sem("lru_sqrt"), sem("lru_done")
        lru_out = sem("lru_out")
        vt_done, vt_read = sem("vt_done"), sem("vt_read")
        sk_turned = sem("sk_turned")
        hank_in = [sem(f"hank_in{i}") for i in range(2)]
        staged = sem("staged")
        scored, max_done, exp_done, attn_done = sem("scored"), sem("max_done"), sem("exp_done"), sem("attn_done")
        pt_done, pt_read, pv_done, pv_read = sem("pt_done"), sem("pt_read"), sem("pv_done"), sem("pv_read")
        pad_done = sem("pad_done")
        on_sum, on_pow, on_done, ot_done, ot_read = sem("on_sum"), sem("on_pow"), sem("on_done"), sem("ot_done"), sem("ot_read")
        o_hi_done, o_parts = sem("o_hi_done"), sem("o_parts")
        mix_done = sem("mix_done")
        x_done = sem("x_done")
        q_done, sc_done, sc_read = sem("q_done"), sem("sc_done"), sem("sc_read")
        soft_in, soft_out, routed = sem("soft_in"), sem("soft_out"), sem("routed")
        rt_done, rt_read = sem("rt_done"), sem("rt_read")
        lists_in, lists_top, lists_out = sem("lists_in"), sem("lists_top"), sem("lists_out")
        cand_done, cand_in, cand_top = sem("cand_done"), sem("cand_in"), sem("cand_top")
        hot_done, g_done, g_read = sem("hot_done"), sem("g_done"), sem("g_read")
        per_layer = list(sem_list)

        def clear():
            with nc.Block() as block:
                @block.sync
                def _(sp):
                    for s in per_layer:
                        sp.sem_clear(s)

        with ExitStack() as part:
            onehot_sb = sb(part, "onehot_sb", [32, N_REL])
            rel_sb = sb(part, "rel_sb", [32, N_BIAS])
            line_sb = sb(part, "line_sb", [N_BIAS, N_REL])
            with nc.Block() as block:
                @block.sync
                def _(sp):
                    sp.dma_start(onehot_sb[:], bucket_onehot).then_inc(const_in, 16)
                    sp.dma_start(rel_sb[:], rel_bias).then_inc(const_in, 16)
                    sp.dma_start(consts[:], cst).then_inc(vec_in, 16)
                    sp.dma_start(x[:], x_in.rearrange("(a p) d -> p a d", p=P)).then_inc(vec_in, 16)
                    sp.wait_ge(once, 3)
                    sp.dma_start(tdram, line_sb[:]).then_inc(stored, 16)
                    sp.wait_ge(stored, 16)
                    sp.dma_start(hankel, bass.AP(tdram.tensor, 0, [[N_REL, N_BIAS], [1, P], [1, SEQ]])).then_inc(stored, 16)
                    sp.wait_ge(stored, 32)
                    sp.wait_ge(vec_in, 32)

                @block.tensor
                def _(pe):
                    pe.wait_ge(const_in, 32)
                    pe.matmul(bank[0][0:N_BIAS, 0:N_REL], rel_sb[:], onehot_sb[:], start=True, stop=True).then_inc(once, 1)

                @block.vector
                def _(dve):
                    dve.memset(halfpow[:], -0.5).then_inc(once, 1)
                    dve.wait_ge(once, 2)
                    dve.tensor_copy(line_sb[:], bank[0][0:N_BIAS, 0:N_REL]).then_inc(once, 1)
        clear()

        def load_pairs(sp, layer, part_pair, first, end):
            base = layer * LAYER_PAIRS + part_pair

            def load(p, slot):
                sp.wait_ge(w_parts, p * 4 + 4)
                sp.dma_start(raw[:, slot, :, :], stream[bass.ds(base + p, 1)].rearrange("o b p c -> p (o b) c")).then_inc(raw_in[slot], 16)
            twos = (end - first) // 2
            with sp.Fori(0, twos) as n:
                load(n * 2 + first, first % 2)
                load(n * 2 + (first + 1), (first + 1) % 2)
            if (end - first) % 2:
                load(end - 1, (end - 1) % 2)

        def split_hi(act, blk, ring):
            slot, sub = ring // 2, ring % 2
            if sub == 0:
                act.wait_ge(raw_in[slot], blk * 4 + (16 - 4 * ring))
            for k in range(2):
                act.wait_ge(w_used, blk * 2 + (k + 1))
                act.activation(w_hi[:, (ring % 2) * 2 + k, :], raw[:, slot, sub, 512 * k:512 * k + 512], ACT.Copy).then_inc(w_hi_done, 1)

        def split_half(dve, blk, ring, k):
            slot, sub = ring // 2, ring % 2
            q = (ring % 2) * 2 + k
            dve.wait_ge(w_hi_done, blk * 2 + (k + 1))
            dve.tensor_tensor(w_lo[:, q, :], raw[:, slot, sub, 512 * k:512 * k + 512], w_hi[:, q, :].bitcast(F32), ALU.subtract).then_inc(w_parts, 1)

        def split_lo(dve, blk, ring):
            for k in range(2):
                split_half(dve, blk, ring, k)

        def up_block(pe, blk, ring, n_up, ps, rhs_hi, rhs_lo):
            pe.wait_ge(up_read, n_up + 1)
            for k in range(2):
                q = (ring % 2) * 2 + k
                pe.wait_ge(w_parts, blk * 2 + (k + 9))
                for c in range(4):
                    hi, lo = w_hi[:, q, P * c:P * c + P], w_lo[:, q, P * c:P * c + P]
                    first, last = k == 0 and c == 0, k == 1 and c == 3
                    pe.matmul(ps, hi, rhs_hi(4 * k + c), start=first, stop=False)
                    pe.matmul(ps, hi, rhs_lo(4 * k + c), start=False, stop=False)
                    ins = pe.matmul(ps, lo, rhs_hi(4 * k + c), start=False, stop=last)
                ins.then_inc(w_used, 1)

        def down_block(pe, blk, ring, k_blk, acc, first, last):
            pe.wait_ge(a_parts, k_blk + 1)
            a = ring % 2
            for k in range(2):
                q = (ring % 2) * 2 + k
                pe.wait_ge(w_parts, blk * 2 + (k + 9))
                for t in range(TT):
                    hi, lo = a_hi[:, a, P * t:P * t + P], a_lo[:, a, P * t:P * t + P]
                    ps = acc[2 * t + k][:, :]
                    pe.matmul(ps, hi, w_hi[:, q, :], start=first, stop=False)
                    pe.matmul(ps, hi, w_lo[:, q, :], start=False, stop=False)
                    ins = pe.matmul(ps, lo, w_hi[:, q, :], start=False, stop=last)
                ins.then_inc(w_used, 1)

        def table_of(act, ch, func):
            ch(act.activation(warm[:], halfpow[:, 0:1], func))

        def norm_act(act, ch):
            for t in range(TT):
                ch(act.activation(xr[:, t, :], x[:, t, :], ACT.Square, accum_out=ss[:, t:t + 1]))
            act.activation(rstd[:], ss[:], ACT.Copy, scale=1.0 / D, bias=EPS).then_inc(sums_done, 1)

        def norm_pool(pool):
            pool.wait_ge(sums_done, 1)
            pool.tensor_tensor(rstd[:], rstd[:], halfpow[:, 0:TT], ALU.pow).then_inc(rstd_done, 1)

        def norm_dve(dve, ch, g_col, h):
            dve.wait_ge(rstd_done, 1)
            for t in range(TT):
                dve.tensor_scalar(xr[:, t, :], x[:, t, :], rstd[:, t:t + 1], None, ALU.mult).then_inc(xr_done, 1)
            dve.wait_ge(vec_in, VEC_LOADS)
            for c in range(DC):
                dve.wait_ge(tp_done, c + 1)
                dve.tensor_scalar(h[:, c, :], bank[4 + c % 2][:, 0:SEQ], vec[:, g_col + c:g_col + c + 1], None, ALU.mult).then_inc(tp_read, 1)
                dve.wait_ge(tp_read, c + 1)
                ch(dve.tensor_copy(h_hi[:, c, :], h[:, c, :]))
                dve.tensor_tensor(h_lo[:, c, :], h[:, c, :], h_hi[:, c, :].bitcast(F32), ALU.subtract).then_inc(h_done, 1)

        def norm_pe(pe):
            pe.wait_ge(xr_done, TT)
            for c in range(DC):
                if c >= 2:
                    pe.wait_ge(tp_read, c - 1)
                for t in range(TT):
                    ins = pe.transpose(bank[4 + c % 2][:, P * t:P * t + P], xr[:, t, P * c:P * c + P], ident)
                ins.then_inc(tp_done, 1)

        def part_hi(act, src, k, a):
            act.activation(a_hi[:, a, :], src(k), ACT.Copy).then_inc(a_hi_done, 1)

        def part_lo(dve, src, k, a):
            dve.wait_ge(a_hi_done, k + 1)
            dve.tensor_tensor(a_lo[:, a, :], src(k), a_hi[:, a, :].bitcast(F32), ALU.subtract).then_inc(a_parts, 1)

        def add_to_x(dve, acc, halves):
            dve.wait_ge(w_used, halves)
            for t in range(TT):
                for k in range(2):
                    part = x[:, t, 512 * k:512 * k + 512]
                    dve.tensor_tensor(part, part, acc[2 * t + k][:, :], ALU.add).then_inc(x_done, 1)
            dve.wait_ge(x_done, 2 * TT)

        def one(ap):
            return ap.rearrange("p o s -> p (o s)")

        with nc.Fori(0, DEPTH) as layer:
            with ExitStack() as part:
                proj = sb(part, "proj", [P, N_IN, SEQ])
                gates = sb(part, "gates", [P, N_GATE, SEQ])
                o_hi = sb(part, "o_hi", [P, N_BRANCH, SEQ], F32R)
                o_lo = sb(part, "o_lo", [P, N_BRANCH, SEQ], F32R)
                mix = sb(part, "mix", [P, DC, SEQ])
                v_nat = sb(part, "v_nat", [P, TT, D + P])
                hank = sb(part, "hank", [P, 2, 2, SEQ])
                qk = sb(part, "qk", [P, 2, 3, SEQ])
                small = sb(part, "small", [P, 96])
                lru_st = sb(part, "lru_st", [P, 2, 2, P])
                xr = mix[:].rearrange("p (a b) s -> p a (b s)", a=TT)
                lru_ws = qk[:].rearrange("p a b s -> p (a b s)")[:, 0:D].rearrange("p (m i c) -> p m i c", i=2, c=64)
                lamv = hank[:, 0, 0, :].rearrange("p (a b) -> p a b", a=4)
                gate_x = v_nat[:].rearrange("p a b -> p (a b)")[:, 0:DC * SEQ].rearrange("p (a b) -> p a b", a=DC)
                prob = mix[:, 0:4, :].rearrange("p (a b) s -> p a b s", a=2)
                prob_t = mix[:, 4:8, :].rearrange("p (a b) (c s) -> p a (b c) s", a=2, c=2)
                o_nat = proj[:, T_DV:T_DV + 8, :].rearrange("p (a b) (c s) -> p a (b c) s", a=TT, c=2)
                o_sq = proj[:, T_DK:T_DK + 8, :].rearrange("p (a b) (c s) -> p a (b c) s", a=TT, c=2)
                skd = proj[:, T_LRUX:T_LRUX + 2, :]
                gated = hank[:, 0, :, :]
                a_sq = hank[:, 1, :, :]
                log_a2 = small[:, 84:92]
                top_s, nmax, zsum, rz, esink = [small[:, 4 * i:4 * i + 4] for i in range(5)]
                nlam, lsum, lam_e = small[:, 20:21], small[:, 22:24], small[:, 24:26]
                log_a, ls_e, ls_z, ls_p = [small[:, 28 + 8 * i:36 + 8 * i] for i in range(4)]
                oss, orstd = small[:, 28:44], small[:, 44:60]
                nsink, lam_c = small[:, 64:80], small[:, 80:82]
                B_BR, B_OUT = N_IN + N_GATE, N_IN + N_GATE + N_BRANCH
                OUTS = (T_LRUG, T_DQ, T_SQ)
                VEC_LOADS = 5 * 16

                with nc.Block() as block:
                    @block.sync
                    def _(sp):
                        sp.sem_inc(w_parts, 8)
                        sp.dma_start(vec[:], vecs[bass.ds(layer, 1)].rearrange("o p c -> (o p) c")).then_inc(vec_in, 16)
                        sp.dma_start(hank[:, 0, 0, :], spread(diff_lambda[bass.ds(layer, 1)], 0, P)).then_inc(vec_in, 16)
                        sp.dma_start(nsink, spread(sinks[bass.ds(layer, 1)], 0, P)).then_inc(vec_in, 16)
                        sp.dma_start(lam_c, spread(lam_consts[bass.ds(layer, 1)], 0, P)).then_inc(vec_in, 16)
                        sp.dma_start(lru_ws, lru_w[bass.ds(layer, 1)].rearrange("o p a b c -> (o p) a b c")).then_inc(vec_in, 16)
                        before = B_BR // 2 + 2
                        load_pairs(sp, layer, 0, 0, before)
                        sp.wait_ge(lru_done, 1)
                        for g in range(2):
                            for side in range(2):
                                sp.dma_start(skd[64 * side:64 * side + 64, g, :], proj[64 * g:64 * g + 64, T_SK, :]).then_inc(sk_turned, 16)
                        with sp.Fori(0, 4) as n:
                            for s in range(2):
                                sp.wait_ge(scored, n * 4 + (2 * s + 2))
                                sp.dma_start(hank[:, s, 0, :], hankel[bass.ds(n * 2 + s, 1)].rearrange("h p f -> (h p) f")).then_inc(hank_in[s], 16)
                        with sp.Fori(4, 8) as n:
                            for s in range(2):
                                sp.wait_ge(scored, n * 4 + (2 * s + 2))
                                sp.dma_start(hank[:, s, :, :], hankel[bass.ds(n * 4 + (2 * s - HEADS_DIFF), 2)].rearrange("h p f -> p h f")).then_inc(hank_in[s], 16)
                        load_pairs(sp, layer, 0, before, MIX_BLOCKS // 2)

                    @block.gpsimd
                    def _(pool):
                        ch = Chain(pool, s_pool, drains=True)
                        norm_pool(pool)
                        pool.wait_ge(proj_done, N_IN + N_GATE)
                        pool.wait_ge(lru_done, 1)
                        for s in range(2):
                            for c in range(2):
                                ch(pool.memset(qk[64 - 64 * c:128 - 64 * c, s, c, :], 0.0))

                        def unit_in(m, s, swa, g):
                            pool.wait_ge(scored, m * 2 + 2)
                            if swa:
                                for c in range(2):
                                    r = slice(64 * c, 64 * c + 64)
                                    ch(pool.tensor_copy(qk[r, s, c, :], one(proj[r, bass.ds(m + (T_SQ - HEADS_DIFF), 1), :])))
                                pool.tensor_copy(qk[:, s, 2, :], skd[:, g, :]).then_inc(staged, 1)
                            else:
                                for c in range(2):
                                    r = slice(64 * c, 64 * c + 64)
                                    ch(pool.tensor_copy(qk[r, s, c, :], one(proj[r, bass.ds(m + T_DQ, 1), :])))
                                pool.tensor_copy(qk[:, s, 2, :], one(proj[:, bass.ds(m + T_DK, 1), :])).then_inc(staged, 1)
                        with pool.Fori(0, 4) as n:
                            ch.enter(n, 4)
                            for s in range(2):
                                unit_in(n * 2 + s, s, False, 0)
                        ch.leave(4)
                        pool.wait_ge(sk_turned, 64)
                        for g in range(2):
                            with pool.Fori(4 + 2 * g, 6 + 2 * g) as n:
                                ch.enter(n - (4 + 2 * g), 4)
                                for s in range(2):
                                    unit_in(n * 2 + s, s, True, g)
                            ch.leave(2)
                        pool.wait_ge(on_sum, 1)
                        pool.tensor_tensor(orstd, oss, halfpow[:, 0:16], ALU.pow).then_inc(on_pow, 1)

                    @block.scalar
                    def _(act):
                        ch = Chain(act, s_act)
                        act.sem_inc(exp_done, 4)
                        norm_act(act, ch)
                        split_hi(act, 0, 0)

                        def project(first, count, func, bias):
                            def body(k, blk, ring, n, i):
                                split_hi(act, blk + 1, (ring + 1) % 4)
                                act.wait_ge(w_used, blk * 2 + 6)
                                dst = one((gates if bias else proj)[:, bass.ds(blk - (N_IN if bias else 0), 1), :])
                                b = vec[:, bass.ds(k + V_BGATE, 1)] if bias else 0.0
                                act.activation(dst, bank[ring % 2][:, 0:SEQ], func, bias=b).then_inc(up_read, 1)
                            blocks_loop(act, first, count, body)
                        project(T_LRUX, 8, ACT.Copy, False)
                        act.wait_ge(lam_sum, 1)
                        act.activation(lam_e, lsum, ACT.Exp)
                        act.activation(ls_e, ls_e, ACT.Exp).then_inc(lam_exp, 1)
                        table_of(act, ch, ACT.Gelu_apprx_tanh)
                        project(T_LRUG, 8, ACT.Gelu_apprx_tanh, False)
                        table_of(act, ch, ACT.Sigmoid)

                        def read_proj(blk, ring):
                            act.wait_ge(w_used, blk * 2 + 6)
                            act.activation(one(proj[:, bass.ds(blk, 1), :]), bank[ring % 2][:, 0:SEQ], ACT.Copy).then_inc(up_read, 1)
                        with act.Fori(0, 4) as n:
                            for i in range(4):
                                blk = n * 4 + (T_DQ + i)
                                split_hi(act, blk + 1, (i + 1) % 4)
                                if i % 2:
                                    k = i // 2
                                    m = n * 2 + k
                                    act.wait_ge(lru_mm, m + 3)
                                    act.activation(one(gate_x[:, bass.ds(m, 1), :]), bank[2 + k][:, 0:SEQ], ACT.Sigmoid, bias=vec[:, bass.ds(n * 2 + (V_BX + k), 1)])
                                    act.activation(one(proj[:, bass.ds(n * 2 + (T_LRUX + k), 1), :]), bank[2 + k][:, SEQ:2 * SEQ], ACT.Sigmoid, bias=vec[:, bass.ds(n * 2 + (V_BA + k), 1)]).then_inc(lru_sig, 1)
                                read_proj(blk, i)
                        act.wait_ge(lam_done, 1)
                        table_of(act, ch, ACT.Exp)
                        with act.Fori(0, 4) as n:
                            for i in range(4):
                                blk = n * 4 + (T_DV + i)
                                split_hi(act, blk + 1, (i + 1) % 4)
                                if i % 2:
                                    k = i // 2
                                    m = n * 2 + k
                                    act.wait_ge(lru_xg, m + 1)
                                    ga = one(proj[:, bass.ds(m, 1), :])
                                    act.activation(one(gate_x[:, bass.ds(m, 1), :]), ga, ACT.Tanh, scale=small[:, bass.ds(n * 2 + (28 + k), 1)])
                                    act.activation(a_sq[:, k, :], ga, ACT.Exp, scale=small[:, bass.ds(n * 2 + (84 + k), 1)])
                                    act.activation(ga, ga, ACT.Exp, scale=small[:, bass.ds(n * 2 + (28 + k), 1)]).then_inc(lru_exp, 1)
                                read_proj(blk, i)
                        project(48, 2, ACT.Copy, False)
                        act.wait_ge(lru_u, DC)
                        act.activation(gate_x, gate_x, ACT.Sqrt, scale=-1.0).then_inc(lru_sqrt, 1)
                        table_of(act, ch, ACT.Sigmoid)
                        project(N_IN, N_GATE, ACT.Sigmoid, True)
                        act.wait_ge(up_read, 2 + N_IN + N_GATE)
                        act.sem_inc(proj_done, N_IN + N_GATE)
                        act.wait_ge(lru_done, 1)
                        act.activation(o_hi[:, 0:8, :], proj[:, T_LRUG:T_LRUG + 8, :], ACT.Copy).then_inc(o_hi_done, 1)
                        for i in range(5):
                            act.wait_ge(vt_done, i + 1)
                            if i < 4:
                                act.activation(v_nat[:, i // 2, 512 * (i % 2):512 * (i % 2) + 512], bank[6 + i % 2][:, :], ACT.Copy).then_inc(vt_read, 1)
                            else:
                                act.activation(v_nat[:, :, D:D + P], bank[6][:, 0:SEQ].rearrange("p (a b) -> p a b", a=TT), ACT.Copy).then_inc(vt_read, 1)

                        def unit(m, s, swa):
                            for t in range(TT):
                                S = bank[2 + 2 * s + t][:, :].rearrange("p (a b) -> p a b", a=2)
                                lo, hi = (64 if swa and t else 0), P * (t + 1)
                                act.wait_ge(max_done, m * 2 + (t + 1))
                                act.wait_ge(pt_done, m * 2 + (t + 1))
                                if swa:
                                    act.activation(esink[:, 2 * t:2 * t + 2], esink[:, 2 * t:2 * t + 2], ACT.Exp)
                                for c in range(2):
                                    ins = act.activation(prob[:, t, c, lo:hi], S[:, c, lo:hi], ACT.Exp, scale=SCALE,
                                                         bias=nmax[:, 2 * t + c:2 * t + c + 1], accum_out=zsum[:, 2 * t + c:2 * t + c + 1])
                                ins.then_inc(exp_done, 1)
                            for t in range(TT):
                                act.wait_ge(pt_done, m * 2 + (t + 3))
                                T = bank[6 + t][:, :].rearrange("p (a b) -> p a b", a=4)
                                pick = slice(0, 2 * t + 2 if t else 1) if not swa else (slice(0, 4) if t else slice(0, 4, 2))
                                if not swa:
                                    pick = slice(0, t + 1)
                                act.activation(prob_t[:, t, pick, :], T[:, pick, :], ACT.Copy).then_inc(pt_read, 1)
                            for t in range(TT):
                                act.wait_ge(pv_done, m * 2 + (t + 1))
                                dst = one(proj[:, bass.ds(m + (T_SQ - HEADS_DIFF), 1), P * t:P * t + P]) if swa else one(o_nat[:, t, bass.ds(m, 1), :])
                                act.activation(dst, bank[6 + t][:, 0:P], ACT.Copy).then_inc(pv_read, 1)
                        for swa in (False, True):
                            if swa:
                                act.wait_ge(pad_done, 1)
                            with act.Fori(4 * swa, 4 * swa + 4) as n:
                                for s in range(2):
                                    unit(n * 2 + s, s, swa)
                        act.wait_ge(pv_read, 2 + 4 * HEADS_DIFF)
                        act.activation(o_hi[:, 16:24, :], proj[:, T_SQ:T_SQ + 8, :], ACT.Copy).then_inc(o_hi_done, 1)
                        act.wait_ge(ot_read, 4)
                        act.activation(o_hi[:, 8:16, :], proj[:, T_DQ:T_DQ + 8, :], ACT.Copy).then_inc(o_hi_done, 1)

                        blocks_loop(act, B_BR, N_BRANCH, lambda k, blk, ring, n, i: split_hi(act, blk + 1, (ring + 1) % 4))
                        src = lambda k: one(mix[:, bass.ds(k, 1), :])
                        act.wait_ge(mix_done, 1)
                        part_hi(act, src, 0, B_OUT % 2)

                        def ahead(k, blk, ring, n, i):
                            split_hi(act, blk + 1, (ring + 1) % 4)
                            part_hi(act, src, k + 1, (ring + 1) % 2)
                        blocks_loop(act, B_OUT, N_OUT - 1, ahead)

                    @block.vector
                    def _(dve):
                        ch = Chain(dve, s_dve)
                        norm_dve(dve, ch, V_MIXG, proj[:, 0:DC, :])
                        split_lo(dve, 0, 0)
                        ch(dve.memset(lru_st[:], 0.0))
                        blocks_loop(dve, 0, 4, lambda k, blk, ring, n, i: split_lo(dve, blk + 1, (ring + 1) % 4))
                        for i in range(2):
                            split_lo(dve, 5 + i, 1 + i)
                            ch(dve.tensor_tensor(gated[:, 1, 64 * i:64 * i + 64], lamv[:, 2 * i, :], lamv[:, 2 * i + 1, :], ALU.mult))
                            ch(dve.tensor_reduce(lsum[:, i:i + 1], gated[:, 1, 64 * i:64 * i + 64], AX, ALU.add))
                        split_lo(dve, 7, 3)
                        apar = vec[:, V_APAR:V_APAR + DC]
                        ch(dve.tensor_scalar(ls_p, apar, -1.0, None, ALU.mult))
                        dve.tensor_tensor(ls_e, apar, ls_p, ALU.min).then_inc(lam_sum, 1)
                        ch(dve.tensor_scalar(nsink, nsink, -1.0, None, ALU.mult))
                        split_lo(dve, 8, 0)
                        half = lambda j: split_half(dve, 9 + j // 2, (1 + j // 2) % 4, j % 2)
                        half(0)
                        dve.wait_ge(lam_exp, 1)
                        ch(dve.tensor_scalar(ls_z, ls_e, 2.0, None, ALU.add))
                        ch(dve.reciprocal(ls_z, ls_z))
                        half(1)
                        ch(dve.tensor_tensor(ls_z, ls_z, ls_e, ALU.mult))
                        ch(dve.tensor_tensor(ls_e, ls_z, ls_z, ALU.mult))
                        half(2)
                        ch(dve.tensor_scalar(ls_p, ls_e, 1.0 / 15, None, ALU.mult))
                        for odd in (13, 11, 9, 7, 5, 3):
                            ch(dve.scalar_tensor_tensor(out=ls_p, in0=ls_p, scalar=1.0 / odd, in1=ls_e, op0=ALU.add, op1=ALU.mult))
                            if odd in (11, 7, 3):
                                half({11: 3, 7: 4, 3: 5}[odd])
                        ch(dve.scalar_tensor_tensor(out=ls_p, in0=ls_p, scalar=1.0, in1=ls_z, op0=ALU.add, op1=ALU.mult))
                        ch(dve.tensor_scalar(ls_z, apar, 0.0, LRU_C, ALU.min, ALU.mult))
                        half(6)
                        ch(dve.scalar_tensor_tensor(out=log_a, in0=ls_p, scalar=-2.0 * LRU_C, in1=ls_z, op0=ALU.mult, op1=ALU.add))
                        dve.tensor_scalar(log_a2, log_a, 2.0, None, ALU.mult)
                        ch(dve.tensor_tensor(nlam, lam_e[:, 1:2], lam_e[:, 0:1], ALU.subtract))
                        dve.tensor_tensor(nlam, nlam, lam_c[:, 0:1], ALU.subtract).then_inc(lam_done, 1)
                        for j in range(7, 12):
                            half(j)
                        dve.wait_ge(up_read, 2 + T_LRUG)
                        with dve.Fori(0, 4) as n:
                            ch.enter(n, 2 * 3)
                            for k in range(2):
                                m = n * 2 + k
                                half = lambda j: split_half(dve, n * 4 + (15 + 2 * k + j // 2), (3 + 2 * k + j // 2) % 4, j % 2)
                                dve.wait_ge(lru_mm, m + 1)
                                for b in range(2):
                                    r = slice(64 * b, 64 * b + 64)
                                    dve.tensor_copy(lru_st[r, k, :, r], lru_ws[r, bass.ds(m, 1), :, :].rearrange("p o i c -> p (o i) c"))
                                half(0)
                                ch(dve.tensor_scalar(one(mix[:, bass.ds(m, 1), :]), one(proj[:, bass.ds(m, 1), :]), vec[:, bass.ds(n * 2 + (V_CONVW + 24 + k), 1)],
                                                     vec[:, bass.ds(n * 2 + (V_CONVB + k), 1)], ALU.mult, ALU.add))
                                for j in (2, 1, 0):
                                    back = 3 - j
                                    half(back)
                                    ins = dve.scalar_tensor_tensor(out=one(mix[:, bass.ds(m, 1), back:SEQ]), in0=one(proj[:, bass.ds(m, 1), 0:SEQ - back]),
                                                                   scalar=vec[:, bass.ds(n * 2 + (V_CONVW + 8 * j + k), 1)], in1=one(mix[:, bass.ds(m, 1), back:SEQ]),
                                                                   op0=ALU.mult, op1=ALU.add)
                                    if j:
                                        ch(ins)
                                ins.then_inc(conv_done, 1)
                        ch.leave(4)
                        split_lo(dve, 31, 3)
                        split_lo(dve, 32, 0)
                        with dve.Fori(0, 4) as n:
                            for k in range(2):
                                m = n * 2 + k
                                g, c = one(gate_x[:, bass.ds(m, 1), :]), one(mix[:, bass.ds(m, 1), :])
                                split_lo(dve, n * 4 + (33 + 2 * k), (1 + 2 * k) % 4)
                                dve.wait_ge(lru_sig, m + 3)
                                dve.tensor_tensor(c, c, g, ALU.mult).then_inc(lru_xg, 1)
                                split_lo(dve, n * 4 + (34 + 2 * k), (2 + 2 * k) % 4)
                                dve.wait_ge(lru_exp, m + 1)
                                dve.scalar_tensor_tensor(out=g, in0=a_sq[:, k, :], scalar=1.0, in1=g, op0=ALU.add, op1=ALU.mult).then_inc(lru_u, 1)
                        for b in range(49, 53):
                            split_lo(dve, b, b % 4)
                        dve.wait_ge(lru_sqrt, 1)
                        with dve.Fori(0, 4) as n:
                            ch.enter(n, 2 * 2)
                            for k in range(2):
                                m = n * 2 + k
                                half = lambda j: split_half(dve, n * 4 + (53 + 2 * k + j // 2), (1 + 2 * k + j // 2) % 4, j % 2)
                                h, c, g = one(gate_x[:, bass.ds(m, 1), :]), one(mix[:, bass.ds(m, 1), :]), one(proj[:, bass.ds(m + T_LRUG, 1), :])
                                half(0)
                                ch(dve.tensor_tensor(c, c, h, ALU.mult))
                                half(1)
                                half(2)
                                ch(dve.tensor_tensor_scan(h, one(proj[:, bass.ds(m, 1), :]), c, 0.0, ALU.mult, ALU.add))
                                half(3)
                                dve.tensor_tensor(g, g, h, ALU.mult).then_inc(lru_out, 1)
                        ch.leave(4)
                        dve.wait_ge(lru_out, DC)
                        dve.sem_inc(lru_done, 1)
                        for b in range(69, 75):
                            split_lo(dve, b, b % 4)
                        dve.wait_ge(o_hi_done, 1)
                        dve.tensor_tensor(o_lo[:, 0:8, :], proj[:, T_LRUG:T_LRUG + 8, :], o_hi[:, 0:8, :].bitcast(F32), ALU.subtract).then_inc(o_parts, 1)

                        def unit(m, s, swa):
                            for t in range(TT):
                                S = bank[2 + 2 * s + t][:, :].rearrange("p (a b) -> p a b", a=2)
                                lo, hi = (64 if swa and t else 0), P * (t + 1)
                                a = slice(2 * t, 2 * t + 2)
                                dve.wait_ge(scored, m * 2 + (t + 5))
                                ch(dve.tensor_reduce(top_s[:, a], S[:, :, lo:hi], AX, ALU.max))
                                if swa:
                                    ns = small[:, bass.ds(m * 2 + (64 - HEADS_SWA), 2)]
                                    ch(dve.scalar_tensor_tensor(out=nmax[:, a], in0=top_s[:, a], scalar=-SCALE, in1=ns, op0=ALU.mult, op1=ALU.min))
                                    dve.tensor_tensor(esink[:, a], nmax[:, a], ns, ALU.subtract).then_inc(max_done, 1)
                                else:
                                    dve.tensor_scalar(nmax[:, a], top_s[:, a], -SCALE, None, ALU.mult).then_inc(max_done, 1)
                            for t in range(TT):
                                lo, hi = (64 if swa and t else 0), P * (t + 1)
                                a = slice(2 * t, 2 * t + 2)
                                z0, z1 = rz[:, 2 * t:2 * t + 1], rz[:, 2 * t + 1:2 * t + 2]
                                dve.wait_ge(exp_done, m * 2 + (t + 5))
                                if swa:
                                    ch(dve.tensor_tensor(zsum[:, a], zsum[:, a], esink[:, a], ALU.add))
                                ch(dve.reciprocal(rz[:, a], zsum[:, a]))
                                if swa:
                                    dve.tensor_scalar(prob[:, t, 0, lo:hi], prob[:, t, 0, lo:hi], z0, None, ALU.mult)
                                    dve.tensor_scalar(prob[:, t, 1, lo:hi], prob[:, t, 1, lo:hi], z1, None, ALU.mult).then_inc(attn_done, 1)
                                else:
                                    dve.tensor_scalar(z1, z1, nlam, None, ALU.mult)
                                    ch(dve.tensor_scalar(prob[:, t, 0, lo:hi], prob[:, t, 0, lo:hi], z0, None, ALU.mult))
                                    dve.scalar_tensor_tensor(out=prob[:, t, 0, lo:hi], in0=prob[:, t, 1, lo:hi], scalar=z1, in1=prob[:, t, 0, lo:hi],
                                                             op0=ALU.mult, op1=ALU.add).then_inc(attn_done, 1)
                        with dve.Fori(0, 4) as n:
                            ch.enter(n, 2 * 2 * 3)
                            for s in range(2):
                                unit(n * 2 + s, s, False)
                        ch.leave(4)
                        dve.wait_ge(pt_done, 2 + 2 * HEADS_DIFF)
                        dve.memset(prob[:, 1, :, 0:64], 0.0).then_inc(pad_done, 1)
                        with dve.Fori(4, 8) as n:
                            ch.enter(n - 4, 2 * 2 * 4)
                            for s in range(2):
                                unit(n * 2 + s, s, True)
                        ch.leave(4)
                        dve.wait_ge(pv_read, 2 + 4 * HEADS_DIFF)
                        ch(dve.tensor_tensor(o_sq, o_nat, o_nat, ALU.mult))
                        ch(dve.tensor_reduce(oss, o_sq.rearrange("p a b s -> p (a b) s"), AX, ALU.add))
                        dve.tensor_scalar(oss, oss, 1.0 / P, EPS, ALU.mult, ALU.add).then_inc(on_sum, 1)
                        dve.wait_ge(on_pow, 1)
                        on = o_nat.rearrange("p a b s -> p (a b) s")
                        dve.tensor_tensor(on, on, spread(orstd.rearrange("p (a o) -> p a o", o=1), 2, P), ALU.mult).then_inc(on_done, 1)
                        for i in range(4):
                            t, h = i // 2, 4 * (i % 2)
                            dve.wait_ge(ot_done, i + 1)
                            dve.tensor_scalar(proj[:, T_DQ + h:T_DQ + h + 4, P * t:P * t + P], bank[2 + i][:, :].rearrange("p (a b) -> p a b", a=4),
                                              vec[:, V_SUBLN:V_SUBLN + 1], lam_c[:, 1:2], ALU.mult, ALU.mult).then_inc(ot_read, 1)
                        for k, b in ((2, 2), (3, 1)):
                            dve.wait_ge(o_hi_done, k)
                            dve.wait_ge(ot_read, 4)
                            dve.tensor_tensor(o_lo[:, 8 * b:8 * b + 8, :], proj[:, OUTS[b]:OUTS[b] + 8, :], o_hi[:, 8 * b:8 * b + 8, :].bitcast(F32), ALU.subtract).then_inc(o_parts, 1)
                        ch(dve.memset(mix[:, :, :], 0.0))
                        for b in range(3):
                            with dve.Fori(0, 2) as n:
                                ch.enter(n, 8)
                                for i in range(4):
                                    m = 4 * n + i
                                    blk = 4 * n + (B_BR + 8 * b + i)
                                    ring = (B_BR + 8 * b + i) % 4
                                    split_lo(dve, blk + 1, (ring + 1) % 4)
                                    dve.wait_ge(w_used, blk * 2 + 6)
                                    ins = dve.tensor_tensor(gated[:, i % 2, :], one(gates[:, bass.ds(m + 8 * b, 1), :]), bank[ring % 2][:, 0:SEQ], ALU.mult)
                                    ch(ins)
                                    dve.sem_inc(up_read, 1)
                                    acc = one(mix[:, bass.ds(m, 1), :])
                                    ch(dve.tensor_tensor(acc, acc, gated[:, i % 2, :], ALU.add))
                            ch.leave(2)
                        dve.sem_inc(mix_done, 1)
                        src = lambda k: one(mix[:, bass.ds(k, 1), :])
                        part_lo(dve, src, 0, B_OUT % 2)

                        def ahead(k, blk, ring, n, i):
                            split_lo(dve, blk + 1, (ring + 1) % 4)
                            part_lo(dve, src, k + 1, (ring + 1) % 2)
                        blocks_loop(dve, B_OUT, N_OUT - 1, ahead)
                        add_to_x(dve, bank[2:6], 2 * MIX_BLOCKS + 4)

                    @block.tensor
                    def _(pe):
                        pe.sem_inc(w_used, 4)
                        pe.sem_inc(up_read, 2)
                        pe.sem_inc(lru_mm, 2)
                        pe.sem_inc(lru_sig, 2)
                        pe.sem_inc(scored, 4)
                        pe.sem_inc(pt_done, 2)
                        pe.sem_inc(pv_read, 2)
                        norm_pe(pe)
                        pe.wait_ge(h_done, DC)
                        body = lambda k, blk, ring, n, i: up_block(pe, blk, ring, blk, bank[ring % 2][:, 0:SEQ], lambda c: h_hi[:, c, :], lambda c: h_lo[:, c, :])
                        blocks_loop(pe, 0, T_DQ, body)
                        with pe.Fori(0, 4) as n:
                            for i in range(4):
                                body(None, n * 4 + (T_DQ + i), i, n, i)
                                if i % 2 == 0:
                                    s = i // 2
                                    m = n * 2 + s
                                    pe.wait_ge(conv_done, m + 1)
                                    pe.wait_ge(lru_sig, m + 1)
                                    for kind in range(2):
                                        ins = pe.matmul(bank[2 + s][:, SEQ * kind:SEQ * kind + SEQ], lru_st[:, s, kind, :], one(mix[:, bass.ds(m, 1), :]), start=True, stop=True)
                                    ins.then_inc(lru_mm, 1)
                        blocks_loop(pe, T_DV, B_BR - T_DV, body)
                        pe.wait_ge(lru_done, 1)
                        for i in range(5):
                            if i >= 2:
                                pe.wait_ge(vt_read, i - 1)
                            for j in range(4 if i < 4 else 2):
                                src = proj[:, T_DV + 4 * (i % 2) + j, P * (i // 2):P * (i // 2) + P] if i < 4 else proj[:, T_SV, P * j:P * j + P]
                                ins = pe.transpose(bank[6 + i % 2][:, P * j:P * j + P], src, ident)
                            ins.then_inc(vt_done, 1)
                        pe.wait_ge(vt_read, 5)
                        pe.wait_ge(lru_sig, DC + 2)

                        def scores(m, s, swa):
                            pe.wait_ge(staged, m + 1)
                            pe.wait_ge(hank_in[s], m * 8 + (16 - 8 * s))
                            pe.wait_ge(exp_done, m * 2 + 2)
                            for t in range(TT):
                                S = bank[2 + 2 * s + t][:, :].rearrange("p (a b) -> p a b", a=2)
                                lo, hi = (64 if swa and t else 0), P * (t + 1)
                                f = P if t == 0 else 0
                                for c in range(2):
                                    pe.matmul(S[:, c, lo:hi], flip8, hank[:, s, c if swa else 0, lo + f:hi + f], start=True, stop=False)
                                    pe.matmul(S[:, c, lo:hi], qk[:, s, c, P * t:P * t + P], qk[:, s, 2, lo:hi], start=False, stop=False)
                                    if swa and t:
                                        pe.matmul(S[:, c, 64:128], row_hi, neg, start=False, stop=False)
                                    ins = pe.matmul(S[:, c, hi - 64:hi], row_lo, neg, start=False, stop=True)
                                ins.then_inc(scored, 1)

                        def values(m, s, swa, g):
                            for t in range(TT):
                                pe.wait_ge(attn_done, m * 2 + (t + 1))
                                pe.wait_ge(pv_read, m * 2 + (t + 1))
                                for c in range(2 if swa else 1):
                                    for kt in range(t + 1):
                                        at = P * (2 * c + kt)
                                        ins = pe.transpose(bank[6 + t][:, at:at + P], prob[:, t, c, P * kt:P * kt + P], ident)
                                ins.then_inc(pt_done, 1)
                            for t in range(TT):
                                pe.wait_ge(pt_read, m * 2 + (t + 1))
                                for c in range(2 if swa else 1):
                                    for kt in range(t + 1):
                                        first, last = kt == 0, kt == t
                                        if swa:
                                            ins = pe.matmul(bank[6 + t][64 * c:64 * c + 64, 0:P], v_nat[:, kt, D + 64 * g:D + 64 * g + 64], prob_t[:, t, 2 * c + kt, :], start=first, stop=last)
                                        else:
                                            ins = pe.matmul(bank[6 + t][:, 0:P], prob_t[:, t, kt, :], v_nat[:, kt, bass.ds(m * P, P)], start=first, stop=last)
                                ins.then_inc(pv_done, 1)
                        scores(0, 0, False)
                        with pe.Fori(0, 3) as n:
                            scores(n * 2 + 1, 1, False)
                            values(n * 2, 0, False, 0)
                            scores(n * 2 + 2, 0, False)
                            values(n * 2 + 1, 1, False, 0)
                        scores(7, 1, False)
                        values(6, 0, False, 0)
                        scores(8, 0, True)
                        values(7, 1, False, 0)
                        for g, turns in ((0, (4, 6)), (1, (6, 7))):
                            with pe.Fori(*turns) as n:
                                scores(n * 2 + 1, 1, True)
                                values(n * 2, 0, True, g)
                                scores(n * 2 + 2, 0, True)
                                values(n * 2 + 1, 1, True, g)
                        scores(15, 1, True)
                        values(14, 0, True, 1)
                        values(15, 1, True, 1)
                        pe.wait_ge(on_done, 1)
                        for i in range(4):
                            for j in range(4):
                                ins = pe.transpose(bank[2 + i][:, P * j:P * j + P], o_nat[:, i // 2, 4 * (i % 2) + j, :], ident)
                            ins.then_inc(ot_done, 1)
                        pe.wait_ge(o_parts, 3)
                        for b in range(3):
                            blocks_loop(pe, B_BR + 8 * b, 8, lambda k, blk, ring, n, i: up_block(
                                pe, blk, ring, blk, bank[ring % 2][:, 0:SEQ], lambda c: o_hi[:, 8 * b + c, :], lambda c: o_lo[:, 8 * b + c, :]))
                        pe.wait_ge(ot_read, 4)
                        down_block(pe, B_OUT, B_OUT % 4, 0, bank[2:6], True, False)
                        blocks_loop(pe, B_OUT + 1, N_OUT - 2, lambda k, blk, ring, n, i: down_block(pe, blk, ring, k + 1, bank[2:6], False, False))
                        down_block(pe, MIX_BLOCKS - 1, (MIX_BLOCKS - 1) % 4, N_OUT - 1, bank[2:6], False, True)
            clear()
            with ExitStack() as part:
                A = sb(part, "A", [P, KEYS, SEQ])
                picks = sb(part, "picks", [P, 3, TT, P])
                picks_t = sb(part, "picks_t", [P, 3, SEQ])
                hot = sb(part, "hot", [P, 2, 2, 4, P])
                best = sb(part, "best", [P, 2, 2, TOPK])
                best_at = sb(part, "best_at", [P, 2, 2, TOPK], U32)
                best_f = sb(part, "best_f", [P, TOPK])
                whole = sb(part, "whole", [P, TT, P], I32)
                xr = A[:, 0:8, :].rearrange("p (a b) s -> p a (b s)", a=TT)
                h_f = A[:, 8:16, :]
                lists = hot[:, 0, :, 0:2, :]
                again = hot[:, 1, 0, 0:2, :]
                FREE = 112
                keys_t = A[:, 88:96, :].rearrange("p a (b k) -> p (a b) k", b=2)
                score = A[:, 96:112, :].rearrange("p a (b k) -> p (a b) k", b=2)
                q_t = A[:, 112:128, :]
                flat = A[:, 112:128, :].rearrange("p a b -> p (a b)")
                UNITS = TT * PEER_HEADS
                spot = [0]

                def scratch(n, k):
                    a = spot[0]
                    spot[0] += n * k
                    return flat[:, a:a + n * k].rearrange("p (n k) -> p n k", n=n)
                cand, cand_i = scratch(UNITS, N_CAND), scratch(UNITS, N_CAND)
                hit = scratch(TOPK, N_CAND)
                s16, i16 = scratch(2 * UNITS, TOPK), scratch(2 * UNITS, TOPK)
                sel_s, sel_i = scratch(UNITS, TOPK), scratch(UNITS, TOPK)
                B_U, B_V = N_WQ, N_WQ + N_U
                VEC_LOADS = 16

                with nc.Block() as block:
                    @block.sync
                    def _(sp):
                        sp.sem_inc(w_parts, 8)
                        sp.dma_start(vec[:], vecs[bass.ds(layer, 1)].rearrange("o p c -> (o p) c")).then_inc(vec_in, 16)
                        sp.dma_start(keys_t, subkeys[bass.ds(layer, 1)].rearrange("o p a k -> (o p) a k")).then_inc(const_in, 16)
                        load_pairs(sp, layer, MIX_BLOCKS // 2, 0, PEER_BLOCKS // 2)

                    @block.gpsimd
                    def _(pool):
                        norm_pool(pool)

                    @block.scalar
                    def _(act):
                        ch = Chain(act, s_act)
                        norm_act(act, ch)
                        split_hi(act, 0, 0)

                        def read_up(dst, func):
                            def body(k, blk, ring, n, i):
                                split_hi(act, blk + 1, (ring + 1) % 4)
                                act.wait_ge(w_used, blk * 2 + 6)
                                act.activation(one(dst(k)), bank[ring % 2][:, 0:SEQ], func).then_inc(up_read, 1)
                            return body
                        blocks_loop(act, 0, N_WQ, read_up(lambda k: q_t[:, bass.ds(k, 1), :] if not isinstance(k, int) else q_t[:, k:k + 1, :], ACT.Copy))
                        for i in range(8):
                            act.wait_ge(sc_done, i + 1)
                            act.activation(score[:, 4 * i:4 * i + 4, :].rearrange("p a b -> p (a b)"), bank[2 + i % 6][:, :], ACT.Copy).then_inc(sc_read, 1)
                        def lists_from_top(p, s):
                            act.wait_ge(lists_top, p + 1)
                            act.activation(s16[:, bass.ds(p * 2, 2), :], best[:, s, :, :], ACT.Copy)
                            return act.activation(i16[:, bass.ds(p * 2, 2), :], best_at[:, s, :, :], ACT.Copy)

                        def stage_lists(p, s):
                            act.activation(lists[:, s, :, :], score[:, bass.ds(p * 2, 2), :], ACT.Copy).then_inc(lists_in, 1)
                        act.wait_ge(sc_read, 8)
                        stage_lists(0, 0)
                        stage_lists(1, 1)
                        table_of(act, ch, ACT.Gelu_apprx_tanh)

                        def read_gelu(k, ring):
                            act.wait_ge(w_used, (k + B_U) * 2 + 6)
                            act.activation(one(A[:, bass.ds(k, 1), :]), bank[ring % 2][:, 0:SEQ], ACT.Gelu_apprx_tanh).then_inc(up_read, 1)

                        def plain(first, count):
                            blocks_loop(act, B_U + first, count, lambda k, blk, ring, n, i: (split_hi(act, blk + 1, (ring + 1) % 4), read_gelu(k + first, ring)))
                        plain(0, 2)
                        with act.Fori(0, 7) as n:
                            for i in range(4):
                                k, ring = n * 4 + (2 + i), (B_U + 2 + i) % 4
                                split_hi(act, k + (B_U + 1), (ring + 1) % 4)
                                if i % 2 == 0:
                                    s = i // 2
                                    lists_from_top(n * 2 + s, s)
                                    stage_lists(n * 2 + (2 + s), s)
                                read_gelu(k, ring)
                        for k in range(30, 36):
                            ring = (B_U + k) % 4
                            split_hi(act, B_U + k + 1, (ring + 1) % 4)
                            if k in (30, 32):
                                lists_from_top((k - 2) // 2, (k - 2) // 2 % 2).then_inc(lists_out, 1)
                            if k == 35:
                                act.wait_ge(cand_done, 1)
                                act.activation(lists[:, 0, 0, 0:N_CAND], cand[:, 0, :], ACT.Copy).then_inc(cand_in, 1)
                            read_gelu(k, ring)
                        with act.Fori(0, UNITS - 1) as n:
                            for i in range(4):
                                k, ring = n * 4 + (36 + i), (B_U + 36 + i) % 4
                                split_hi(act, k + (B_U + 1), (ring + 1) % 4)
                                if i == 3:
                                    act.wait_ge(cand_top, n + 1)
                                    act.activation(one(sel_s[:, bass.ds(n, 1), :]), best[:, 0, 0, :], ACT.Copy)
                                    act.activation(lists[:, 0, 0, 0:N_CAND], one(cand[:, bass.ds(n + 1, 1), :]), ACT.Copy).then_inc(cand_in, 1)
                                read_gelu(k, ring)
                        plain(96, 4)
                        split_hi(act, B_U + 101, (B_U + 101) % 4)
                        act.wait_ge(cand_top, UNITS)
                        act.activation(sel_s[:, UNITS - 1, :], best[:, 0, 0, :], ACT.Copy).then_inc(cand_in, 1)
                        read_gelu(100, (B_U + 100) % 4)
                        act.wait_ge(soft_in, 1)
                        act.activation(sel_s, sel_s, ACT.Exp).then_inc(soft_out, 1)
                        table_of(act, ch, ACT.Gelu_apprx_tanh)
                        plain(101, FREE - 101)
                        act.wait_ge(routed, 1)
                        plain(FREE, N_U - FREE)
                        src = lambda k: one(A[:, bass.ds(k, 1), :])
                        act.wait_ge(g_read, N_GROUPS)
                        part_hi(act, src, 0, 0)

                        def ahead(k, blk, ring, n, i):
                            split_hi(act, blk + 1, (ring + 1) % 4)
                            part_hi(act, src, k + 1, (ring + 1) % 2)
                        blocks_loop(act, B_V, N_V - 1, ahead)

                    @block.vector
                    def _(dve):
                        ch = Chain(dve, s_dve, drains=True)
                        norm_dve(dve, ch, V_FFNG, h_f)
                        split_lo(dve, 0, 0)
                        ahead = lambda k, blk, ring, n, i: split_lo(dve, blk + 1, (ring + 1) % 4)
                        blocks_loop(dve, 0, N_WQ, ahead)
                        with dve.Fori(0, 8) as n:
                            dve.sem_clear(s_dve)
                            for s in range(2):
                                done = 6 * s
                                val = [lists[:, s, c, :] for c in range(2)]
                                rest = [again[:, c, :] for c in range(2)]
                                big = [best[:, s, c, :] for c in range(2)]
                                at = [best_at[:, s, c, :] for c in range(2)]
                                half = lambda j: split_half(dve, n * 4 + (B_U + 1 + 2 * s + j // 2), (1 + 2 * s + j // 2) % 4, j % 2)
                                dve.wait_ge(lists_in, n * 2 + (s + 1))
                                half(0)
                                for c in range(2):
                                    dve.max(big[c][:, 0:8], val[c]).then_inc(s_dve, 1)
                                half(1)
                                for c in range(2):
                                    dve.wait_ge(s_dve, done + 1 + c)
                                    dve.max_index(at[c][:, 0:8], big[c][:, 0:8], val[c])
                                    dve.match_replace(rest[c], big[c][:, 0:8], val[c], TAKEN).then_inc(s_dve, 1)
                                half(2)
                                for c in range(2):
                                    dve.wait_ge(s_dve, done + 3 + c)
                                    dve.max(big[c][:, 8:16], rest[c]).then_inc(s_dve, 1)
                                half(3)
                                for c in range(2):
                                    dve.wait_ge(s_dve, done + 5 + c)
                                    ins = dve.max_index(at[c][:, 8:16], big[c][:, 8:16], rest[c])
                                ins.then_inc(lists_top, 1)
                        s_pair = s16.rearrange("p (u c) k -> p u c k", c=2)
                        i_pair = i16.rearrange("p (u c) k -> p u c k", c=2)
                        split_half(dve, B_U + 33, 1, 0)
                        dve.wait_ge(lists_out, 2)
                        for i in range(PAIR_RANKS + 1):
                            m = CAND_N[i] if i < PAIR_RANKS else TOPK - PAIR_RANKS
                            o = CAND_OFF[i]
                            if i < PAIR_RANKS:
                                s1, s2 = spread(s_pair[:, :, 0, i:i + 1], 2, m), s_pair[:, :, 1, 0:m]
                                i1, i2 = spread(i_pair[:, :, 0, i:i + 1], 2, m), i_pair[:, :, 1, 0:m]
                            else:
                                s1, s2 = s_pair[:, :, 0, i:TOPK], spread(s_pair[:, :, 1, 0:1], 2, m)
                                i1, i2 = i_pair[:, :, 0, i:TOPK], spread(i_pair[:, :, 1, 0:1], 2, m)
                            dve.tensor_tensor(cand[:, :, o:o + m], s1, s2, ALU.add)
                            ins = dve.scalar_tensor_tensor(out=cand_i[:, :, o:o + m], in0=i1, scalar=float(KEYS), in1=i2, op0=ALU.mult, op1=ALU.add)
                            if i == PAIR_RANKS:
                                ins.then_inc(cand_done, 1)
                            elif i < 7:
                                split_half(dve, B_U + 33 + (i + 1) // 2, (1 + (i + 1) // 2) % 4, (i + 1) % 2)
                        val, rest, big, at = lists[:, 0, 0, 0:N_CAND], again[:, 0, 0:N_CAND], best[:, 0, 0, :], best_at[:, 0, 0, :]
                        with dve.Fori(0, UNITS) as n:
                            dve.sem_clear(s_dve)
                            half = lambda j: split_half(dve, n * 4 + (B_U + 37 + j // 2), (1 + j // 2) % 4, j % 2)
                            dve.wait_ge(cand_in, n + 1)
                            half(0)
                            dve.max(big[:, 0:8], val).then_inc(s_dve, 1)
                            half(1)
                            dve.wait_ge(s_dve, 1)
                            dve.max_index(at[:, 0:8], big[:, 0:8], val)
                            dve.match_replace(rest, big[:, 0:8], val, TAKEN).then_inc(s_dve, 1)
                            half(2)
                            dve.wait_ge(s_dve, 2)
                            dve.max(big[:, 8:16], rest).then_inc(s_dve, 1)
                            half(3)
                            dve.wait_ge(s_dve, 3)
                            dve.max_index(at[:, 8:16], big[:, 8:16], rest).then_inc(cand_top, 1)
                            half(4)
                            dve.wait_ge(cand_top, n + 1)
                            dve.tensor_copy(best_f[:], at).then_inc(s_dve, 1)
                            half(5)
                            dve.wait_ge(s_dve, 4)
                            dve.tensor_tensor(hit, spread(best_f[:].rearrange("p (k o) -> p k o", o=1), 2, N_CAND),
                                              spread(iota[:, 0:N_CAND].rearrange("p (o c) -> p o c", o=1), 1, TOPK), ALU.is_equal).then_inc(s_dve, 1)
                            half(6)
                            dve.wait_ge(s_dve, 5)
                            dve.tensor_tensor(hit, hit, spread(cand_i[:, bass.ds(n, 1), :], 1, TOPK), ALU.mult).then_inc(s_dve, 1)
                            half(7)
                            dve.wait_ge(s_dve, 6)
                            dve.tensor_reduce(one(sel_i[:, bass.ds(n, 1), :]), hit, AX, ALU.add)
                        dve.drain()
                        dve.sem_clear(s_dve)
                        ch = Chain(dve, s_dve)
                        half = lambda j: split_half(dve, B_U + 101 + j // 2, (1 + j // 2) % 4, j % 2)
                        half(0)
                        dve.wait_ge(cand_in, UNITS + 1)
                        soft_max = best[:].rearrange("p a b c -> p (a b c)")[:, 0:UNITS]
                        ch(dve.tensor_copy(soft_max, sel_s[:, :, 0:1].rearrange("p u o -> p (u o)")))
                        dve.tensor_tensor(sel_s, sel_s, spread(soft_max.rearrange("p (u o) -> p u o", o=1), 2, TOPK), ALU.subtract).then_inc(soft_in, 1)
                        half(1)
                        sel_i2 = sel_i.rearrange("p (a h) k -> p a (h k)", a=TT)
                        ch(dve.tensor_copy(whole[:], sel_i2))
                        ch(dve.tensor_scalar(whole[:], whole[:], 7, None, ALU.logical_shift_right))
                        ch(dve.tensor_copy(picks[:, 0, :, :], whole[:]))
                        half(2)
                        dve.scalar_tensor_tensor(out=picks[:, 1, :, :], in0=picks[:, 0, :, :], scalar=-float(KEYS), in1=sel_i2, op0=ALU.mult, op1=ALU.add)
                        half(3)
                        dve.wait_ge(soft_out, 1)
                        ch(dve.tensor_reduce(best_f[:], sel_s, AX, ALU.add))
                        ch(dve.reciprocal(best_f[:], best_f[:]))
                        dve.tensor_tensor(picks[:, 2, :, :].rearrange("p a (h k) -> p (a h) k", h=PEER_HEADS), sel_s,
                                          spread(best_f[:].rearrange("p (u o) -> p u o", o=1), 2, TOPK), ALU.mult).then_inc(routed, 1)
                        for j in range(4, 24):
                            half(j)
                        for i in range(3):
                            dve.wait_ge(rt_done, i + 1)
                            ch(dve.tensor_copy(picks_t[:, i, :], bank[4 + i][:, 0:SEQ]))
                        with dve.Fori(0, 4) as n:
                            for i in range(4):
                                split_lo(dve, n * 4 + (B_U + 113 + i), (i + 1) % 4)
                        dve.wait_ge(up_read, 2 + B_V)

                        def one_hot(g, s):
                            for k in range(4):
                                t = g * 4 + k
                                dve.tensor_scalar(hot[:, s, 0, k, :], iota, picks_t[:, 0, bass.ds(t, 1)], None, ALU.is_equal)
                                ins = dve.tensor_scalar(hot[:, s, 1, k, :], iota, picks_t[:, 1, bass.ds(t, 1)], picks_t[:, 2, bass.ds(t, 1)], ALU.is_equal, ALU.mult)
                            ins.then_inc(hot_done, 1)

                        def weigh(g, s):
                            dve.wait_ge(g_done, g + 1)
                            a = A[:, :, bass.ds(g * 4, 4)]
                            dve.tensor_tensor(a, a, bank[2 + s][:, :].rearrange("p (k j) -> p j k", k=4), ALU.mult).then_inc(g_read, 1)
                        one_hot(0, 0)
                        with dve.Fori(0, N_GROUPS // 2 - 1) as n:
                            one_hot(n * 2 + 1, 1)
                            weigh(n * 2, 0)
                            one_hot(n * 2 + 2, 0)
                            weigh(n * 2 + 1, 1)
                        one_hot(N_GROUPS - 1, 1)
                        weigh(N_GROUPS - 2, 0)
                        weigh(N_GROUPS - 1, 1)
                        src = lambda k: one(A[:, bass.ds(k, 1), :])
                        part_lo(dve, src, 0, 0)

                        def ahead_v(k, blk, ring, n, i):
                            split_lo(dve, blk + 1, (ring + 1) % 4)
                            part_lo(dve, src, k + 1, (ring + 1) % 2)
                        blocks_loop(dve, B_V, N_V - 1, ahead_v)
                        add_to_x(dve, bank[4:8], 2 * PEER_BLOCKS + 4)

                    @block.tensor
                    def _(pe):
                        pe.sem_inc(w_used, 4)
                        pe.sem_inc(up_read, 2)
                        norm_pe(pe)
                        pe.wait_ge(h_done, DC)
                        h_rhs = (lambda c: h_hi[:, c, :], lambda c: h_lo[:, c, :])
                        body = lambda k, blk, ring, n, i: up_block(pe, blk, ring, blk, bank[ring % 2][:, 0:SEQ], *h_rhs)
                        blocks_loop(pe, 0, N_WQ, body)
                        pe.wait_ge(up_read, 2 + N_WQ)
                        pe.wait_ge(const_in, 16)
                        for i in range(8):
                            if i >= 6:
                                pe.wait_ge(sc_read, i - 5)
                            for j in range(4):
                                t, hc = i // 4, 4 * (i % 4) + j
                                ins = pe.matmul(bank[2 + i % 6][:, P * j:P * j + P], q_t[:, hc, P * t:P * t + P], keys_t[:, hc, :], start=True, stop=True)
                            ins.then_inc(sc_done, 1)
                        blocks_loop(pe, B_U, FREE, body)
                        pe.wait_ge(routed, 1)
                        for i in range(3):
                            for t in range(TT):
                                ins = pe.transpose(bank[4 + i][:, P * t:P * t + P], picks[:, i, t, :], ident)
                            ins.then_inc(rt_done, 1)
                        blocks_loop(pe, B_U + FREE, N_U - FREE, body)

                        def weights(g, s):
                            pe.wait_ge(hot_done, g + 1)
                            for k in range(4):
                                ins = pe.matmul(bank[2 + s][:, P * k:P * k + P], hot[:, s, 0, k, :], hot[:, s, 1, k, :], start=True, stop=True)
                            ins.then_inc(g_done, 1)
                        with pe.Fori(0, N_GROUPS // 2) as n:
                            for s in range(2):
                                weights(n * 2 + s, s)
                        down_block(pe, B_V, 0, 0, bank[4:8], True, False)
                        blocks_loop(pe, B_V + 1, N_V - 2, lambda k, blk, ring, n, i: down_block(pe, blk, ring, k + 1, bank[4:8], False, False))
                        down_block(pe, PEER_BLOCKS - 1, (PEER_BLOCKS - 1) % 4, N_V - 1, bank[4:8], False, True)
            clear()

        with ExitStack() as part:
            xr = sb(part, "xr", [P, TT, D])
            g_all = sb(part, "g_all", [P, D])
            with nc.Block() as block:
                @block.sync
                def _(sp):
                    sp.dma_start(g_all[:], spread(final_g, 0, P)).then_inc(const_in, 16)
                    for t in range(TT):
                        sp.wait_ge(x_done, t + 1)
                        sp.dma_start(out[P * t:P * t + P, :], xr[:, t, :]).then_inc(stored, 16)
                    sp.wait_ge(stored, 16 * TT)

                @block.scalar
                def _(act):
                    norm_act(act, Chain(act, s_act))

                @block.gpsimd
                def _(pool):
                    norm_pool(pool)

                @block.vector
                def _(dve):
                    dve.wait_ge(const_in, 16)
                    dve.wait_ge(rstd_done, 1)
                    for t in range(TT):
                        dve.scalar_tensor_tensor(out=xr[:, t, :], in0=x[:, t, :], scalar=rstd[:, t:t + 1], in1=g_all[:],
                                                 op0=ALU.mult, op1=ALU.mult).then_inc(x_done, 1)


def buckets():
    rel = np.arange(N_REL) - (SEQ - 1)
    n = np.abs(rel)
    large = 8 + (np.log(np.maximum(n, 1).astype(np.float32) / 8) / np.float32(np.log(128.0)) * 8).astype(np.int32)
    bucket = np.where(rel > 0, 16, 0) + np.where(n < 8, n, np.minimum(large, 15))
    return (bucket[None, :] == np.arange(32)[:, None]).astype(np.float32)


def constants():
    c = np.zeros((P, N_CST), np.float32)
    c[:, C_ID:C_ID + P] = np.eye(P)
    c[:, C_FLIP:C_FLIP + P] = np.eye(P)[::-1] / SCALE
    c[:, C_IOTA:C_IOTA + P] = np.arange(P)
    c[0, C_LO:C_LO + 64] = 1
    c[0, C_HI + 64:C_HI + P] = 1
    c[0, C_NEG:C_NEG + CHUNK] = MASKED
    return c


def kernel(**inputs):
    import math
    import concourse.bacc as _bacc
    from concourse.bass_utils import run_bass_kernel_spmd as _run
    a = {k: np.asarray(v) for k, v in inputs.items()}

    def up(w):
        return np.ascontiguousarray(w.reshape(DC, P, -1, P).transpose(2, 1, 0, 3)).reshape(-1, P, D)

    blocks = []
    for l in range(DEPTH):
        blocks += [up(a["w_in"][l]), up(a["w_gate"][l])] + [up(a["w_branch"][l, b]) for b in range(3)]
        blocks += [a["w_out"][l].reshape(DC, P, D), up(a["peer_wq"][l])]
        u = a["peer_u"][l].reshape(P, KEYS, DC, P)
        blocks.append(u.transpose(1, 3, 2, 0).reshape(KEYS, P, D))
        blocks.append(a["peer_v"][l].reshape(P, KEYS, D).transpose(1, 0, 2))
    stream = np.concatenate(blocks).reshape(DEPTH * LAYER_PAIRS, 2, P, D)

    def cols(v):
        return v.reshape(DEPTH, -1, P).transpose(0, 2, 1)

    vecs = np.concatenate([cols(a[n]) for n in ("norm_mix_g", "conv_w", "conv_b", "lru_bx", "lru_ba", "lru_a_param", "b_gate",
                                                "norm_ffn_g", "diff_subln_g")], axis=2)
    lru = np.stack([a["lru_wx"], a["lru_wa"]], axis=3)
    lru = lru.reshape(DEPTH, DC, 2, 64, 2, 64).transpose(0, 2, 3, 1, 4, 5).reshape(DEPTH, P, DC, 2, 64)
    subk = a["peer_subkeys"].reshape(DEPTH, 2 * PEER_HEADS, KEYS, P).transpose(0, 3, 1, 2)
    init = [0.8 - 0.6 * math.exp(-0.3 * l) for l in range(DEPTH)]
    arrays = {
        "stream": stream, "vecs": vecs, "cst": constants(), "rel_bias": a["rel_bias"], "bucket_onehot": buckets(),
        "lam_consts": np.array([[i, 1.0 - i] for i in init], np.float32), "final_g": a["final_norm_g"].reshape(1, D),
        "diff_lambda": a["diff_lambda"].reshape(DEPTH, -1), "sinks": a["swa_sinks"], "lru_w": lru, "subkeys": subk,
        "x_in": a["x"].reshape(SEQ, D),
    }
    arrays = {k: np.ascontiguousarray(v) for k, v in arrays.items()}
    nc = _bacc.Bacc("TRN2", target_bir_lowering=False, num_devices=1, dynamic_dma_scratch_size=8192)
    args = [nc.dram_tensor(k, v.shape, mybir.dt.from_np(v.dtype), kind="ExternalInput").ap() for k, v in arrays.items()]
    out = nc.dram_tensor("out", (SEQ, D), F32, kind="ExternalOutput").ap()
    trunk(nc, *args, out)
    r = _run(nc, [arrays], core_ids=[0])
    return r.results[0]["out"].reshape(1, SEQ, D)
```

```python
import concourse.bass as bass
from concourse import mybir
from contextlib import ExitStack
import numpy as np

F32 = mybir.dt.float32
F32R = mybir.dt.float32r
U32 = mybir.dt.uint32
I32 = mybir.dt.int32
ALU = mybir.AluOpType
ACT = mybir.ActivationFunctionType
AX = mybir.AxisListType.X

P = 128
DEPTH = 2
SEQ = 256
D = 1024
DC = D // P
TT = SEQ // P
HEADS_DIFF = 8
HEADS_SWA = 16
CHUNK = 64
BRANCHES = (0, 2, 1)
N_GROUPS = SEQ // 4
TOPK = 16
PEER_HEADS = 8
KEYS = 128
EPS = 1e-6
LRU_C = 8.0
SCALE = 0.125
MASKED = -1e30
TAKEN = -3e38

N_IN = 50
N_GATE = 24
N_BRANCH = 24
N_OUT = 8
N_WQ = 16
N_U = KEYS
N_V = KEYS
T_LRUX, T_LRUG, T_DQ, T_DK, T_DV, T_SQ, T_SK, T_SV = 0, 8, 16, 24, 32, 40, 48, 49
MIX_BLOCKS = N_IN + N_GATE + N_BRANCH + N_OUT
PEER_BLOCKS = N_WQ + N_U + N_V
LAYER_PAIRS = (MIX_BLOCKS + PEER_BLOCKS) // 2

V_MIXG, V_CONVW, V_CONVB, V_BX, V_BA, V_APAR, V_BGATE, V_FFNG, V_SUBLN, N_VEC = 0, 8, 40, 48, 56, 64, 72, 96, 104, 105
C_ID, C_FLIP, C_IOTA, C_LO, C_HI, C_NEG, N_CST = 0, 128, 256, 384, 512, 640, 704

N_REL = 384
N_BIAS = HEADS_DIFF + HEADS_SWA

CAND_N = [TOPK // (i + 1) for i in range(TOPK)]
CAND_OFF = [sum(CAND_N[:i]) for i in range(TOPK)]
N_CAND = sum(CAND_N)
PAIR_RANKS = sum(n > 1 for n in CAND_N)


def spread(ap, dim, n):
    shape = list(ap.shape)
    shape[dim] = n
    return ap.to_broadcast(shape)


class Chain:

    def __init__(self, eng, sem, drains=False):
        self.eng, self.sem, self.drains = eng, sem, drains
        self.base, self.turn, self.per, self.n = 0, None, 0, 0

    def value(self):
        done = self.base + self.n
        return done if self.turn is None else self.turn * self.per + done

    def __call__(self, ins):
        self.n += 1
        ins.then_inc(self.sem, 1)
        if self.turn is not None and self.drains:
            self.eng.drain()
        else:
            self.eng.wait_ge(self.sem, self.value())

    def enter(self, turn, per):
        self.base, self.turn, self.per, self.n = self.base + self.n, turn, per, 0

    def leave(self, turns):
        assert self.n == self.per, (self.n, self.per)
        self.base, self.turn, self.n = self.base + turns * self.per, None, 0


def blocks_loop(eng, first, count, body):
    fours = count // 4
    if fours:
        with eng.Fori(0, fours) as n:
            for i in range(4):
                body(n * 4 + i, n * 4 + (first + i), (first + i) % 4, n, i)
    for b in range(4 * fours, count):
        body(b, first + b, (first + b) % 4, None, b - 4 * fours)


def trunk(nc, stream, vecs, cst, rel_bias, bucket_onehot, lam_consts, final_g, diff_lambda, sinks,
          lru_w, subkeys, x_in, out):
    top = ExitStack()

    def sb(stack, name, shape, dt=F32):
        return stack.enter_context(nc.sbuf_tensor(name, shape, dt))

    with top:
        sem_list = []

        def sem(name):
            s = top.enter_context(nc.semaphore(name))
            sem_list.append(s)
            return s

        x = sb(top, "x", [P, TT, D])
        consts = sb(top, "consts", [P, N_CST])
        vec = sb(top, "vec", [P, N_VEC])
        raw = sb(top, "raw", [P, 2, 2, D])
        w_hi = sb(top, "w_hi", [P, 4, 512], F32R)
        w_lo = sb(top, "w_lo", [P, 4, 512], F32R)
        h_hi = sb(top, "h_hi", [P, DC, SEQ], F32R)
        h_lo = sb(top, "h_lo", [P, DC, SEQ], F32R)
        a_hi = sb(top, "a_hi", [P, 2, SEQ], F32R)
        a_lo = sb(top, "a_lo", [P, 2, SEQ], F32R)
        ss = sb(top, "ss", [P, TT])
        rstd = sb(top, "rstd", [P, TT])
        warm = sb(top, "warm", [P, 1])
        halfpow = sb(top, "halfpow", [P, 16])
        bank = [top.enter_context(nc.psum_tensor(f"bank{i}", [P, 512], F32)) for i in range(8)]
        ident = consts[:, C_ID:C_ID + P]
        flip8 = consts[:, C_FLIP:C_FLIP + P]
        iota = consts[:, C_IOTA:C_IOTA + P]
        row_lo = consts[0:1, C_LO:C_LO + P]
        row_hi = consts[0:1, C_HI:C_HI + P]
        neg = consts[0:1, C_NEG:C_NEG + CHUNK]
        tdram = nc.dram_tensor("rel_line", (N_BIAS, N_REL), F32, kind="Internal").ap()
        hankel = nc.dram_tensor("rel_hankel", (N_BIAS, P, SEQ), F32, kind="Internal").ap()

        raw_in = [sem(f"raw_in{i}") for i in range(2)]
        w_hi_done = sem("w_hi_done")
        w_parts = sem("w_parts")
        w_used = sem("w_used")
        up_read = sem("up_read")
        a_hi_done = sem("a_hi_done")
        a_parts = sem("a_parts")
        s_act, s_dve, s_pool = sem("s_act"), sem("s_dve"), sem("s_pool")
        sums_done = sem("sums_done")
        rstd_done = sem("rstd_done")
        xr_done = sem("xr_done")
        tp_done = sem("tp_done")
        h_hi_done = sem("h_hi_done")
        h_done = sem("h_done")
        const_in = sem("const_in")
        vec_in = sem("vec_in")
        stored = sem("stored")
        once = sem("once")
        proj_done = sem("proj_done")
        lam_sum, lam_exp, lam_done = sem("lam_sum"), sem("lam_exp"), sem("lam_done")
        conv_done, lru_mm, lru_sig = sem("conv_done"), sem("lru_mm"), sem("lru_sig")
        lru_xg, lru_exp, lru_u, lru_sqrt, lru_done = sem("lru_xg"), sem("lru_exp"), sem("lru_u"), sem("lru_sqrt"), sem("lru_done")
        lru_out = sem("lru_out")
        vt_done, vt_read = sem("vt_done"), sem("vt_read")
        sk_turned = sem("sk_turned")
        hank_in = [sem(f"hank_in{i}") for i in range(2)]
        staged = sem("staged")
        scored, max_done, exp_done, attn_done = sem("scored"), sem("max_done"), sem("exp_done"), sem("attn_done")
        pt_done, pt_read, pv_done, pv_read = sem("pt_done"), sem("pt_read"), sem("pv_done"), sem("pv_read")
        pad_done = sem("pad_done")
        on_sum, on_pow, on_done, ot_done, ot_read = sem("on_sum"), sem("on_pow"), sem("on_done"), sem("ot_done"), sem("ot_read")
        o_hi_done, o_parts = sem("o_hi_done"), sem("o_parts")
        mix_done = sem("mix_done")
        x_done = sem("x_done")
        q_done, sc_done, sc_read = sem("q_done"), sem("sc_done"), sem("sc_read")
        soft_in, soft_out, routed = sem("soft_in"), sem("soft_out"), sem("routed")
        rt_done, rt_read = sem("rt_done"), sem("rt_read")
        lists_in, lists_top, lists_out = sem("lists_in"), sem("lists_top"), sem("lists_out")
        cand_done, cand_in, cand_top = sem("cand_done"), sem("cand_in"), sem("cand_top")
        picks_in, dist_done, hot_act = sem("picks_in"), sem("dist_done"), sem("hot_act")
        hot_done, g_done, g_read = sem("hot_done"), sem("g_done"), sem("g_read")
        per_layer = list(sem_list)
        hankel_stored = sem("hankel_stored")

        def clear():
            with nc.Block() as block:
                @block.sync
                def _(sp):
                    for s in per_layer:
                        sp.sem_clear(s)

        with ExitStack() as part:
            onehot_sb = sb(part, "onehot_sb", [32, N_REL])
            rel_sb = sb(part, "rel_sb", [32, N_BIAS])
            line_sb = sb(part, "line_sb", [N_BIAS, N_REL])
            with nc.Block() as block:
                @block.sync
                def _(sp):
                    sp.dma_start(onehot_sb[:], bucket_onehot).then_inc(const_in, 16)
                    sp.dma_start(rel_sb[:], rel_bias).then_inc(const_in, 16)
                    sp.dma_start(consts[:], cst).then_inc(vec_in, 16)
                    sp.dma_start(x[:], x_in.rearrange("(a p) d -> p a d", p=P)).then_inc(vec_in, 16)
                    sp.wait_ge(once, 3)
                    sp.dma_start(tdram, line_sb[:]).then_inc(stored, 16)
                    sp.wait_ge(stored, 16)
                    sp.dma_start(hankel, bass.AP(tdram.tensor, 0, [[N_REL, N_BIAS], [1, P], [1, SEQ]])).then_inc(hankel_stored, 16)
                    sp.wait_ge(vec_in, 32)

                @block.tensor
                def _(pe):
                    pe.wait_ge(const_in, 32)
                    pe.matmul(bank[0][0:N_BIAS, 0:N_REL], rel_sb[:], onehot_sb[:], start=True, stop=True).then_inc(once, 1)

                @block.vector
                def _(dve):
                    dve.memset(halfpow[:], -0.5).then_inc(once, 1)
                    dve.wait_ge(once, 2)
                    dve.tensor_copy(line_sb[:], bank[0][0:N_BIAS, 0:N_REL]).then_inc(once, 1)
        clear()

        def load_pairs(sp, layer, part_pair, first, end):
            base = layer * LAYER_PAIRS + part_pair

            def load(p, slot):
                sp.wait_ge(w_parts, p * 4 + 4)
                sp.dma_start(raw[:, slot, :, :], stream[bass.ds(base + p, 1)].rearrange("o b p c -> p (o b) c")).then_inc(raw_in[slot], 16)
            twos = (end - first) // 2
            with sp.Fori(0, twos) as n:
                load(n * 2 + first, first % 2)
                load(n * 2 + (first + 1), (first + 1) % 2)
            if (end - first) % 2:
                load(end - 1, (end - 1) % 2)

        def split_hi(act, blk, ring):
            slot, sub = ring // 2, ring % 2
            if sub == 0:
                act.wait_ge(raw_in[slot], blk * 4 + (16 - 4 * ring))
            for k in range(2):
                act.wait_ge(w_used, blk * 2 + (k + 1))
                act.activation(w_hi[:, (ring % 2) * 2 + k, :], raw[:, slot, sub, 512 * k:512 * k + 512], ACT.Copy).then_inc(w_hi_done, 1)

        def split_half(dve, blk, ring, k):
            slot, sub = ring // 2, ring % 2
            q = (ring % 2) * 2 + k
            dve.wait_ge(w_hi_done, blk * 2 + (k + 1))
            dve.tensor_tensor(w_lo[:, q, :], raw[:, slot, sub, 512 * k:512 * k + 512], w_hi[:, q, :].bitcast(F32), ALU.subtract).then_inc(w_parts, 1)

        def split_lo(dve, blk, ring):
            for k in range(2):
                split_half(dve, blk, ring, k)

        def up_block(pe, blk, ring, n_up, ps, rhs_hi, rhs_lo):
            pe.wait_ge(up_read, n_up + 1)
            for k in range(2):
                q = (ring % 2) * 2 + k
                pe.wait_ge(w_parts, blk * 2 + (k + 9))
                for c in range(4):
                    hi, lo = w_hi[:, q, P * c:P * c + P], w_lo[:, q, P * c:P * c + P]
                    first, last = k == 0 and c == 0, k == 1 and c == 3
                    pe.matmul(ps, hi, rhs_hi(4 * k + c), start=first, stop=False)
                    pe.matmul(ps, hi, rhs_lo(4 * k + c), start=False, stop=False)
                    ins = pe.matmul(ps, lo, rhs_hi(4 * k + c), start=False, stop=last)
                ins.then_inc(w_used, 1)

        def down_block(pe, blk, ring, k_blk, acc, first, last):
            pe.wait_ge(a_parts, k_blk + 1)
            a = ring % 2
            for k in range(2):
                q = (ring % 2) * 2 + k
                pe.wait_ge(w_parts, blk * 2 + (k + 9))
                for t in range(TT):
                    hi, lo = a_hi[:, a, P * t:P * t + P], a_lo[:, a, P * t:P * t + P]
                    ps = acc[2 * t + k][:, :]
                    pe.matmul(ps, hi, w_hi[:, q, :], start=first, stop=False)
                    pe.matmul(ps, hi, w_lo[:, q, :], start=False, stop=False)
                    ins = pe.matmul(ps, lo, w_hi[:, q, :], start=False, stop=last)
                ins.then_inc(w_used, 1)

        def table_of(act, ch, func):
            ch(act.activation(warm[:], halfpow[:, 0:1], func))

        def norm_act(act, ch):
            for t in range(TT):
                ins = act.activation(xr[:, t, :], x[:, t, :], ACT.Square, accum_out=ss[:, t:t + 1])
            ch(ins)
            act.activation(rstd[:], ss[:], ACT.Copy, scale=1.0 / D, bias=EPS).then_inc(sums_done, 1)

        def norm_pool(pool):
            pool.wait_ge(sums_done, 1)
            pool.tensor_tensor(rstd[:], rstd[:], halfpow[:, 0:TT], ALU.pow).then_inc(rstd_done, 1)

        def norm_hi(act, g_col):
            act.wait_ge(rstd_done, 1)
            act.activation(xr[:, 1, :], x[:, 1, :], ACT.Copy, scale=rstd[:, 1:2]).then_inc(xr_done, 1)
            act.wait_ge(vec_in, VEC_LOADS)
            for c in range(DC):
                act.wait_ge(tp_done, c + 1)
                act.activation(h_hi[:, c, :], bank[2 + c % 6][:, 0:SEQ], ACT.Copy, scale=vec[:, g_col + c:g_col + c + 1]).then_inc(h_hi_done, 1)

        def norm_lo(dve, g_col):
            dve.wait_ge(rstd_done, 1)
            dve.tensor_scalar(xr[:, 0, :], x[:, 0, :], rstd[:, 0:1], None, ALU.mult).then_inc(xr_done, 1)
            dve.wait_ge(vec_in, VEC_LOADS)
            for c in range(DC):
                dve.wait_ge(h_hi_done, c + 1)
                dve.scalar_tensor_tensor(out=h_lo[:, c, :], in0=bank[2 + c % 6][:, 0:SEQ], scalar=vec[:, g_col + c:g_col + c + 1],
                                         in1=h_hi[:, c, :].bitcast(F32), op0=ALU.mult, op1=ALU.subtract).then_inc(h_done, 1)
            split_lo(dve, 0, 0)

        def norm_pe(pe):
            pe.wait_ge(xr_done, TT)
            for c in range(DC):
                if c >= 6:
                    pe.wait_ge(h_done, c - 5)
                for t in range(TT):
                    ins = pe.transpose(bank[2 + c % 6][:, P * t:P * t + P], xr[:, t, P * c:P * c + P], ident)
                ins.then_inc(tp_done, 1)

        def part_hi(act, src, k, a):
            act.activation(a_hi[:, a, :], src(k), ACT.Copy).then_inc(a_hi_done, 1)

        def part_lo(dve, src, k, a):
            dve.wait_ge(a_hi_done, k + 1)
            dve.tensor_tensor(a_lo[:, a, :], src(k), a_hi[:, a, :].bitcast(F32), ALU.subtract).then_inc(a_parts, 1)

        def add_to_x(dve, acc, halves):
            dve.wait_ge(w_used, halves)
            for t in range(TT):
                for k in range(2):
                    part = x[:, t, 512 * k:512 * k + 512]
                    dve.tensor_tensor(part, part, acc[2 * t + k][:, :], ALU.add).then_inc(x_done, 1)
            dve.wait_ge(x_done, 2 * TT)

        def one(ap):
            return ap.rearrange("p o s -> p (o s)")

        with nc.Fori(0, DEPTH) as layer:
            with ExitStack() as part:
                proj = sb(part, "proj", [P, N_IN, SEQ])
                gates = sb(part, "gates", [P, N_GATE, SEQ])
                o_hi = sb(part, "o_hi", [P, N_BRANCH, SEQ], F32R)
                o_lo = sb(part, "o_lo", [P, N_BRANCH, SEQ], F32R)
                mix = sb(part, "mix", [P, DC, SEQ])
                v_nat = sb(part, "v_nat", [P, TT, D + P])
                hank = sb(part, "hank", [P, 2, 2, SEQ])
                qk = sb(part, "qk", [P, 2, 3, SEQ])
                small = sb(part, "small", [P, 96])
                lru_st = sb(part, "lru_st", [P, 2, 2, P])
                xr = mix[:].rearrange("p (a b) s -> p a (b s)", a=TT)
                lru_ws = qk[:].rearrange("p a b s -> p (a b s)")[:, 0:D].rearrange("p (m i c) -> p m i c", i=2, c=64)
                lamv = hank[:, 0, 0, :].rearrange("p (a b) -> p a b", a=4)
                gate_x = v_nat[:].rearrange("p a b -> p (a b)")[:, 0:DC * SEQ].rearrange("p (a b) -> p a b", a=DC)
                probs = [v.rearrange("p (a b) s -> p a b s", a=2) for v in (mix[:, 0:4, :], proj[:, T_LRUX + 2:T_LRUX + 6, :])]
                prob_t = mix[:, 4:8, :].rearrange("p (a b) (c s) -> p a (b c) s", a=2, c=2)
                o_nat = proj[:, T_DV:T_DV + 8, :].rearrange("p (a b) (c s) -> p a (b c) s", a=TT, c=2)
                o_sq = proj[:, T_DK:T_DK + 8, :].rearrange("p (a b) (c s) -> p a (b c) s", a=TT, c=2)
                skd = proj[:, T_LRUX:T_LRUX + 2, :]
                gated = hank[:, 0, :, :]
                a_sq = hank[:, 1, :, :]
                log_a2 = small[:, 84:92]
                subln = small[:, 82:83]
                top_s, nmax, zsum, rz, esink = [small[:, 4 * i:4 * i + 4] for i in range(5)]
                nlam, lsum, lam_e = small[:, 20:21], small[:, 22:24], small[:, 24:26]
                log_a, ls_e, ls_z, ls_p = [small[:, 28 + 8 * i:36 + 8 * i] for i in range(4)]
                oss, orstd = small[:, 28:44], small[:, 44:60]
                nsink, lam_c = small[:, 64:80], small[:, 80:82]
                B_BR, B_OUT = N_IN + N_GATE, N_IN + N_GATE + N_BRANCH
                OUTS = (T_LRUG, T_DQ, T_SQ)
                VEC_LOADS = 5 * 16

                with nc.Block() as block:
                    @block.sync
                    def _(sp):
                        sp.sem_inc(w_parts, 8)
                        sp.dma_start(vec[:], vecs[bass.ds(layer, 1)].rearrange("o p c -> (o p) c")).then_inc(vec_in, 16)
                        sp.dma_start(hank[:, 0, 0, :], spread(diff_lambda[bass.ds(layer, 1)], 0, P)).then_inc(vec_in, 16)
                        sp.dma_start(nsink, spread(sinks[bass.ds(layer, 1)], 0, P)).then_inc(vec_in, 16)
                        sp.dma_start(lam_c, spread(lam_consts[bass.ds(layer, 1)], 0, P)).then_inc(vec_in, 16)
                        sp.dma_start(lru_ws, lru_w[bass.ds(layer, 1)].rearrange("o p a b c -> (o p) a b c")).then_inc(vec_in, 16)
                        before = B_BR // 2 + 2
                        load_pairs(sp, layer, 0, 0, before)
                        sp.wait_ge(lru_done, 1)
                        for g in range(2):
                            for side in range(2):
                                sp.dma_start(skd[64 * side:64 * side + 64, g, :], proj[64 * g:64 * g + 64, T_SK, :]).then_inc(sk_turned, 16)
                        sp.wait_ge(hankel_stored, 16)
                        with sp.Fori(0, 4) as n:
                            for s in range(2):
                                sp.wait_ge(scored, n * 4 + (2 * s + 2))
                                sp.dma_start(hank[:, s, 0, :], hankel[bass.ds(n * 2 + s, 1)].rearrange("h p f -> (h p) f")).then_inc(hank_in[s], 16)
                        with sp.Fori(4, 8) as n:
                            for s in range(2):
                                sp.wait_ge(scored, n * 4 + (2 * s + 2))
                                sp.dma_start(hank[:, s, :, :], hankel[bass.ds(n * 4 + (2 * s - HEADS_DIFF), 2)].rearrange("h p f -> p h f")).then_inc(hank_in[s], 16)
                        load_pairs(sp, layer, 0, before, MIX_BLOCKS // 2)

                    @block.gpsimd
                    def _(pool):
                        ch = Chain(pool, s_pool, drains=True)
                        norm_pool(pool)
                        pool.wait_ge(proj_done, N_IN + N_GATE)
                        pool.wait_ge(lru_done, 1)
                        for s in range(2):
                            for c in range(2):
                                ch(pool.memset(qk[64 - 64 * c:128 - 64 * c, s, c, :], 0.0))

                        def unit_in(m, s, swa, g):
                            pool.wait_ge(scored, m * 2 + 2)
                            if swa:
                                for c in range(2):
                                    r = slice(64 * c, 64 * c + 64)
                                    ch(pool.tensor_copy(qk[r, s, c, :], one(proj[r, bass.ds(m + (T_SQ - HEADS_DIFF), 1), :])))
                                pool.tensor_copy(qk[:, s, 2, :], skd[:, g, :]).then_inc(staged, 1)
                            else:
                                for c in range(2):
                                    r = slice(64 * c, 64 * c + 64)
                                    ch(pool.tensor_copy(qk[r, s, c, :], one(proj[r, bass.ds(m + T_DQ, 1), :])))
                                pool.tensor_copy(qk[:, s, 2, :], one(proj[:, bass.ds(m + T_DK, 1), :])).then_inc(staged, 1)
                        with pool.Fori(0, 4) as n:
                            ch.enter(n, 4)
                            for s in range(2):
                                unit_in(n * 2 + s, s, False, 0)
                        ch.leave(4)
                        pool.wait_ge(sk_turned, 64)
                        for g in range(2):
                            with pool.Fori(4 + 2 * g, 6 + 2 * g) as n:
                                ch.enter(n - (4 + 2 * g), 4)
                                for s in range(2):
                                    unit_in(n * 2 + s, s, True, g)
                            ch.leave(2)
                        pool.wait_ge(on_sum, 1)
                        pool.tensor_tensor(orstd, oss, halfpow[:, 0:16], ALU.pow).then_inc(on_pow, 1)

                    @block.scalar
                    def _(act):
                        ch = Chain(act, s_act)
                        act.sem_inc(exp_done, 4)
                        norm_act(act, ch)
                        norm_hi(act, V_MIXG)
                        split_hi(act, 0, 0)

                        def project(first, count, func, bias):
                            def body(k, blk, ring, n, i):
                                split_hi(act, blk + 1, (ring + 1) % 4)
                                act.wait_ge(w_used, blk * 2 + 6)
                                dst = one((gates if bias else proj)[:, bass.ds(blk - (N_IN if bias else 0), 1), :])
                                b = vec[:, bass.ds(k + V_BGATE, 1)] if bias else 0.0
                                act.activation(dst, bank[ring % 2][:, 0:SEQ], func, bias=b).then_inc(up_read, 1)
                            blocks_loop(act, first, count, body)
                        project(T_LRUX, 8, ACT.Copy, False)
                        act.wait_ge(lam_sum, 1)
                        act.activation(lam_e, lsum, ACT.Exp)
                        act.activation(ls_e, ls_e, ACT.Exp).then_inc(lam_exp, 1)
                        table_of(act, ch, ACT.Gelu_apprx_tanh)
                        project(T_LRUG, 8, ACT.Gelu_apprx_tanh, False)
                        table_of(act, ch, ACT.Sigmoid)

                        def read_proj(blk, ring):
                            act.wait_ge(w_used, blk * 2 + 6)
                            act.activation(one(proj[:, bass.ds(blk, 1), :]), bank[ring % 2][:, 0:SEQ], ACT.Copy).then_inc(up_read, 1)
                        with act.Fori(0, 4) as n:
                            for i in range(4):
                                blk = n * 4 + (T_DQ + i)
                                split_hi(act, blk + 1, (i + 1) % 4)
                                if i % 2:
                                    k = i // 2
                                    m = n * 2 + k
                                    act.wait_ge(lru_mm, m + 3)
                                    act.activation(one(gate_x[:, bass.ds(m, 1), :]), bank[2 + k][:, 0:SEQ], ACT.Sigmoid, bias=vec[:, bass.ds(n * 2 + (V_BX + k), 1)])
                                    act.activation(one(proj[:, bass.ds(n * 2 + (T_LRUX + k), 1), :]), bank[2 + k][:, SEQ:2 * SEQ], ACT.Sigmoid, bias=vec[:, bass.ds(n * 2 + (V_BA + k), 1)]).then_inc(lru_sig, 1)
                                read_proj(blk, i)
                        act.wait_ge(lam_done, 1)
                        table_of(act, ch, ACT.Exp)
                        with act.Fori(0, 4) as n:
                            for i in range(4):
                                blk = n * 4 + (T_DV + i)
                                split_hi(act, blk + 1, (i + 1) % 4)
                                if i % 2:
                                    k = i // 2
                                    m = n * 2 + k
                                    act.wait_ge(lru_xg, m + 1)
                                    ga = one(proj[:, bass.ds(m, 1), :])
                                    act.activation(one(gate_x[:, bass.ds(m, 1), :]), ga, ACT.Tanh, scale=small[:, bass.ds(n * 2 + (28 + k), 1)])
                                    act.activation(a_sq[:, k, :], ga, ACT.Exp, scale=small[:, bass.ds(n * 2 + (84 + k), 1)])
                                    act.activation(ga, ga, ACT.Exp, scale=small[:, bass.ds(n * 2 + (28 + k), 1)]).then_inc(lru_exp, 1)
                                read_proj(blk, i)
                        project(48, 2, ACT.Copy, False)
                        act.wait_ge(lru_u, DC)
                        act.activation(gate_x, gate_x, ACT.Sqrt, scale=-1.0).then_inc(lru_sqrt, 1)
                        table_of(act, ch, ACT.Sigmoid)
                        project(N_IN, N_GATE, ACT.Sigmoid, True)
                        act.wait_ge(up_read, 2 + N_IN + N_GATE)
                        act.sem_inc(proj_done, N_IN + N_GATE)
                        act.wait_ge(lru_done, 1)
                        act.activation(o_hi[:, 0:8, :], proj[:, T_LRUG:T_LRUG + 8, :], ACT.Copy).then_inc(o_hi_done, 1)
                        for i in range(5):
                            act.wait_ge(vt_done, i + 1)
                            if i < 4:
                                act.activation(v_nat[:, i // 2, 512 * (i % 2):512 * (i % 2) + 512], bank[6 + i % 2][:, :], ACT.Copy).then_inc(vt_read, 1)
                            else:
                                act.activation(v_nat[:, :, D:D + P], bank[6][:, 0:SEQ].rearrange("p (a b) -> p a b", a=TT), ACT.Copy).then_inc(vt_read, 1)

                        def exps(m, s, swa):
                            prob = probs[s]
                            for t in range(TT):
                                S = bank[2 + 2 * s + t][:, :].rearrange("p (a b) -> p a b", a=2)
                                lo, hi = (64 if swa and t else 0), P * (t + 1)
                                act.wait_ge(max_done, m * 2 + (t + 1))
                                act.wait_ge(pt_done, m * 2 + (t + 1))
                                if swa:
                                    act.activation(esink[:, 2 * t:2 * t + 2], esink[:, 2 * t:2 * t + 2], ACT.Exp)
                                for c in range(2):
                                    ins = act.activation(prob[:, t, c, lo:hi], S[:, c, lo:hi], ACT.Exp, scale=SCALE,
                                                         bias=nmax[:, 2 * t + c:2 * t + c + 1], accum_out=zsum[:, 2 * t + c:2 * t + c + 1])
                                ins.then_inc(exp_done, 1)

                        def outputs(m, swa):
                            for t in range(TT):
                                act.wait_ge(pt_done, m * 2 + (t + 5))
                                T = bank[6 + t][:, :].rearrange("p (a b) -> p a b", a=4)
                                pick = (slice(0, 4) if t else slice(0, 4, 2)) if swa else slice(0, t + 1)
                                act.activation(prob_t[:, t, pick, :], T[:, pick, :], ACT.Copy).then_inc(pt_read, 1)
                            for t in range(TT):
                                act.wait_ge(pv_done, m * 2 + (t + 1))
                                dst = one(proj[:, bass.ds(m + (T_SQ - HEADS_DIFF), 1), P * t:P * t + P]) if swa else one(o_nat[:, t, bass.ds(m, 1), :])
                                act.activation(dst, bank[6 + t][:, 0:P], ACT.Copy).then_inc(pv_read, 1)
                        table_of(act, ch, ACT.Exp)
                        exps(0, 0, False)
                        with act.Fori(0, 3) as n:
                            for s in range(2):
                                exps(n * 2 + (s + 1), 1 - s, False)
                                outputs(n * 2 + s, False)
                        exps(7, 1, False)
                        outputs(6, False)
                        act.wait_ge(pad_done, 1)
                        exps(8, 0, True)
                        outputs(7, False)
                        with act.Fori(4, 7) as n:
                            for s in range(2):
                                exps(n * 2 + (s + 1), 1 - s, True)
                                outputs(n * 2 + s, True)
                        exps(15, 1, True)
                        outputs(14, True)
                        outputs(15, True)

                        for k in range(16):
                            split_hi(act, B_BR + k + 1, (B_BR + k + 1) % 4)
                            if k in (0, 1):
                                c = 4 * k
                                act.wait_ge(pv_read, 2 + 4 * HEADS_DIFF)
                                act.activation(o_hi[:, 16 + c:20 + c, :], proj[:, T_SQ + c:T_SQ + c + 4, :], ACT.Copy).then_inc(o_hi_done, 1)
                            if k in (8, 9):
                                for i in (k - 8, k - 6):
                                    t, h = i // 2, 4 * (i % 2)
                                    act.wait_ge(ot_done, i + 1)
                                    act.activation(proj[:, T_DQ + h:T_DQ + h + 4, P * t:P * t + P], bank[2 + i][:, :].rearrange("p (a b) -> p a b", a=4),
                                                   ACT.Copy, scale=subln).then_inc(ot_read, 1)
                            if k in (11, 12):
                                c = 4 * (k - 11)
                                act.wait_ge(ot_read, 4)
                                act.activation(o_hi[:, 8 + c:12 + c, :], proj[:, T_DQ + c:T_DQ + c + 4, :], ACT.Copy).then_inc(o_hi_done, 1)
                        blocks_loop(act, B_BR + 16, N_BRANCH - 16, lambda k, blk, ring, n, i: split_hi(act, blk + 1, (ring + 1) % 4))
                        src = lambda k: one(mix[:, bass.ds(k, 1), :])
                        act.wait_ge(mix_done, 1)
                        part_hi(act, src, 0, B_OUT % 2)

                        def ahead(k, blk, ring, n, i):
                            split_hi(act, blk + 1, (ring + 1) % 4)
                            part_hi(act, src, k + 1, (ring + 1) % 2)
                        blocks_loop(act, B_OUT, N_OUT - 1, ahead)

                    @block.vector
                    def _(dve):
                        ch = Chain(dve, s_dve)
                        norm_lo(dve, V_MIXG)
                        ch(dve.memset(lru_st[:], 0.0))
                        blocks_loop(dve, 0, 4, lambda k, blk, ring, n, i: split_lo(dve, blk + 1, (ring + 1) % 4))
                        for i in range(2):
                            split_lo(dve, 5 + i, 1 + i)
                            ch(dve.tensor_tensor(gated[:, 1, 64 * i:64 * i + 64], lamv[:, 2 * i, :], lamv[:, 2 * i + 1, :], ALU.mult))
                            ch(dve.tensor_reduce(lsum[:, i:i + 1], gated[:, 1, 64 * i:64 * i + 64], AX, ALU.add))
                        split_lo(dve, 7, 3)
                        apar = vec[:, V_APAR:V_APAR + DC]
                        ch(dve.tensor_scalar(ls_p, apar, -1.0, None, ALU.mult))
                        dve.tensor_tensor(ls_e, apar, ls_p, ALU.min).then_inc(lam_sum, 1)
                        ch(dve.tensor_scalar(nsink, nsink, -1.0, None, ALU.mult))
                        split_lo(dve, 8, 0)
                        half = lambda j: split_half(dve, 9 + j // 2, (1 + j // 2) % 4, j % 2)
                        half(0)
                        dve.wait_ge(lam_exp, 1)
                        ch(dve.tensor_scalar(ls_z, ls_e, 2.0, None, ALU.add))
                        ch(dve.reciprocal(ls_z, ls_z))
                        half(1)
                        ch(dve.tensor_tensor(ls_z, ls_z, ls_e, ALU.mult))
                        ch(dve.tensor_tensor(ls_e, ls_z, ls_z, ALU.mult))
                        half(2)
                        ch(dve.tensor_scalar(ls_p, ls_e, 1.0 / 15, None, ALU.mult))
                        for odd in (13, 11, 9, 7, 5, 3):
                            ch(dve.scalar_tensor_tensor(out=ls_p, in0=ls_p, scalar=1.0 / odd, in1=ls_e, op0=ALU.add, op1=ALU.mult))
                            if odd in (11, 7, 3):
                                half({11: 3, 7: 4, 3: 5}[odd])
                        ch(dve.scalar_tensor_tensor(out=ls_p, in0=ls_p, scalar=1.0, in1=ls_z, op0=ALU.add, op1=ALU.mult))
                        ch(dve.tensor_scalar(ls_z, apar, 0.0, LRU_C, ALU.min, ALU.mult))
                        half(6)
                        ch(dve.scalar_tensor_tensor(out=log_a, in0=ls_p, scalar=-2.0 * LRU_C, in1=ls_z, op0=ALU.mult, op1=ALU.add))
                        dve.tensor_scalar(log_a2, log_a, 2.0, None, ALU.mult)
                        ch(dve.tensor_tensor(nlam, lam_e[:, 1:2], lam_e[:, 0:1], ALU.subtract))
                        dve.tensor_tensor(nlam, nlam, lam_c[:, 0:1], ALU.subtract).then_inc(lam_done, 1)
                        for j in range(7, 12):
                            half(j)
                        dve.wait_ge(up_read, 2 + T_LRUG)
                        with dve.Fori(0, 4) as n:
                            ch.enter(n, 2 * 3)
                            for k in range(2):
                                m = n * 2 + k
                                half = lambda j: split_half(dve, n * 4 + (15 + 2 * k + j // 2), (3 + 2 * k + j // 2) % 4, j % 2)
                                dve.wait_ge(lru_mm, m + 1)
                                for b in range(2):
                                    r = slice(64 * b, 64 * b + 64)
                                    dve.tensor_copy(lru_st[r, k, :, r], lru_ws[r, bass.ds(m, 1), :, :].rearrange("p o i c -> p (o i) c"))
                                half(0)
                                ch(dve.tensor_scalar(one(mix[:, bass.ds(m, 1), :]), one(proj[:, bass.ds(m, 1), :]), vec[:, bass.ds(n * 2 + (V_CONVW + 24 + k), 1)],
                                                     vec[:, bass.ds(n * 2 + (V_CONVB + k), 1)], ALU.mult, ALU.add))
                                for j in (2, 1, 0):
                                    back = 3 - j
                                    half(back)
                                    ins = dve.scalar_tensor_tensor(out=one(mix[:, bass.ds(m, 1), back:SEQ]), in0=one(proj[:, bass.ds(m, 1), 0:SEQ - back]),
                                                                   scalar=vec[:, bass.ds(n * 2 + (V_CONVW + 8 * j + k), 1)], in1=one(mix[:, bass.ds(m, 1), back:SEQ]),
                                                                   op0=ALU.mult, op1=ALU.add)
                                    if j:
                                        ch(ins)
                                ins.then_inc(conv_done, 1)
                        ch.leave(4)
                        split_lo(dve, 31, 3)
                        split_lo(dve, 32, 0)
                        with dve.Fori(0, 4) as n:
                            for k in range(2):
                                m = n * 2 + k
                                g, c = one(gate_x[:, bass.ds(m, 1), :]), one(mix[:, bass.ds(m, 1), :])
                                split_lo(dve, n * 4 + (33 + 2 * k), (1 + 2 * k) % 4)
                                dve.wait_ge(lru_sig, m + 3)
                                dve.tensor_tensor(c, c, g, ALU.mult).then_inc(lru_xg, 1)
                                split_lo(dve, n * 4 + (34 + 2 * k), (2 + 2 * k) % 4)
                                dve.wait_ge(lru_exp, m + 1)
                                dve.scalar_tensor_tensor(out=g, in0=a_sq[:, k, :], scalar=1.0, in1=g, op0=ALU.add, op1=ALU.mult).then_inc(lru_u, 1)
                        for b in range(49, 53):
                            split_lo(dve, b, b % 4)
                        dve.wait_ge(lru_sqrt, 1)
                        with dve.Fori(0, 4) as n:
                            ch.enter(n, 2 * 2)
                            for k in range(2):
                                m = n * 2 + k
                                half = lambda j: split_half(dve, n * 4 + (53 + 2 * k + j // 2), (1 + 2 * k + j // 2) % 4, j % 2)
                                h, c, g = one(gate_x[:, bass.ds(m, 1), :]), one(mix[:, bass.ds(m, 1), :]), one(proj[:, bass.ds(m + T_LRUG, 1), :])
                                half(0)
                                ch(dve.tensor_tensor(c, c, h, ALU.mult))
                                half(1)
                                half(2)
                                ch(dve.tensor_tensor_scan(h, one(proj[:, bass.ds(m, 1), :]), c, 0.0, ALU.mult, ALU.add))
                                half(3)
                                dve.tensor_tensor(g, g, h, ALU.mult).then_inc(lru_out, 1)
                        ch.leave(4)
                        dve.wait_ge(lru_out, DC)
                        dve.sem_inc(lru_done, 1)
                        for b in range(69, 75):
                            split_lo(dve, b, b % 4)
                        dve.wait_ge(o_hi_done, 1)
                        dve.tensor_tensor(o_lo[:, 0:8, :], proj[:, T_LRUG:T_LRUG + 8, :], o_hi[:, 0:8, :].bitcast(F32), ALU.subtract).then_inc(o_parts, 1)

                        def unit(m, s, swa):
                            prob = probs[s]
                            for t in range(TT):
                                S = bank[2 + 2 * s + t][:, :].rearrange("p (a b) -> p a b", a=2)
                                lo, hi = (64 if swa and t else 0), P * (t + 1)
                                a = slice(2 * t, 2 * t + 2)
                                dve.wait_ge(scored, m * 2 + (t + 5))
                                ch(dve.tensor_reduce(top_s[:, a], S[:, :, lo:hi], AX, ALU.max))
                                if swa:
                                    ns = small[:, bass.ds(m * 2 + (64 - HEADS_SWA), 2)]
                                    ch(dve.scalar_tensor_tensor(out=nmax[:, a], in0=top_s[:, a], scalar=-SCALE, in1=ns, op0=ALU.mult, op1=ALU.min))
                                    dve.tensor_tensor(esink[:, a], nmax[:, a], ns, ALU.subtract).then_inc(max_done, 1)
                                else:
                                    dve.tensor_scalar(nmax[:, a], top_s[:, a], -SCALE, None, ALU.mult).then_inc(max_done, 1)
                            for t in range(TT):
                                lo, hi = (64 if swa and t else 0), P * (t + 1)
                                a = slice(2 * t, 2 * t + 2)
                                z0, z1 = rz[:, 2 * t:2 * t + 1], rz[:, 2 * t + 1:2 * t + 2]
                                dve.wait_ge(exp_done, m * 2 + (t + 5))
                                if swa:
                                    ch(dve.tensor_tensor(zsum[:, a], zsum[:, a], esink[:, a], ALU.add))
                                ch(dve.reciprocal(rz[:, a], zsum[:, a]))
                                if swa:
                                    dve.tensor_scalar(prob[:, t, 0, lo:hi], prob[:, t, 0, lo:hi], z0, None, ALU.mult)
                                    dve.tensor_scalar(prob[:, t, 1, lo:hi], prob[:, t, 1, lo:hi], z1, None, ALU.mult).then_inc(attn_done, 1)
                                else:
                                    dve.tensor_scalar(z1, z1, nlam, None, ALU.mult)
                                    ch(dve.tensor_scalar(prob[:, t, 0, lo:hi], prob[:, t, 0, lo:hi], z0, None, ALU.mult))
                                    dve.scalar_tensor_tensor(out=prob[:, t, 0, lo:hi], in0=prob[:, t, 1, lo:hi], scalar=z1, in1=prob[:, t, 0, lo:hi],
                                                             op0=ALU.mult, op1=ALU.add).then_inc(attn_done, 1)
                        with dve.Fori(0, 4) as n:
                            ch.enter(n, 2 * 2 * 3)
                            for s in range(2):
                                unit(n * 2 + s, s, False)
                        ch.leave(4)
                        dve.wait_ge(pt_done, 4 + 2 * HEADS_DIFF)
                        dve.memset(probs[1][:, 1, :, 0:64], 0.0)
                        dve.memset(probs[0][:, 1, :, 0:64], 0.0).then_inc(pad_done, 1)
                        ch(dve.tensor_scalar(subln, lam_c[:, 1:2], vec[:, V_SUBLN:V_SUBLN + 1], None, ALU.mult))
                        on, on_sq = [v.rearrange("p a b s -> p (a b) s") for v in (o_nat, o_sq)]
                        with dve.Fori(4, 8) as n:
                            ch.enter(n - 4, 2 * 2 * 4 + 2)
                            for s in range(2):
                                unit(n * 2 + s, s, True)
                                quarter = bass.ds((n - 4) * 4, 4)
                                if s == 0:
                                    dve.wait_ge(pv_read, 2 + TT * HEADS_DIFF)
                                    ch(dve.tensor_tensor(on_sq[:, quarter, :], on[:, quarter, :], on[:, quarter, :], ALU.mult))
                                else:
                                    ch(dve.tensor_reduce(oss[:, quarter], on_sq[:, quarter, :], AX, ALU.add))
                        ch.leave(4)
                        dve.tensor_scalar(oss, oss, 1.0 / P, EPS, ALU.mult, ALU.add).then_inc(on_sum, 1)
                        dve.wait_ge(pv_read, 2 + 4 * HEADS_DIFF)

                        def o_rest(piece, count):
                            b, c = piece
                            dve.tensor_tensor(o_lo[:, 8 * b + c:8 * b + c + count, :], proj[:, OUTS[b] + c:OUTS[b] + c + count, :],
                                              o_hi[:, 8 * b + c:8 * b + c + count, :].bitcast(F32), ALU.subtract).then_inc(o_parts, 1)
                        for k in range(16):
                            blk, m, b = B_BR + k, k % 8, BRANCHES[k // 8]
                            ring = blk % 4
                            split_lo(dve, blk + 1, (ring + 1) % 4)
                            dve.wait_ge(w_used, blk * 2 + 6)
                            if k < 8:
                                ch(dve.tensor_tensor(mix[:, m, :], gates[:, 8 * b + m, :], bank[ring % 2][:, 0:SEQ], ALU.mult))
                                dve.sem_inc(up_read, 1)
                            else:
                                ch(dve.tensor_tensor(gated[:, m % 2, :], gates[:, 8 * b + m, :], bank[ring % 2][:, 0:SEQ], ALU.mult))
                                dve.sem_inc(up_read, 1)
                                ch(dve.tensor_tensor(mix[:, m, :], mix[:, m, :], gated[:, m % 2, :], ALU.add))
                            if k in (0, 1):
                                dve.wait_ge(on_pow, 1)
                                half = slice(8 * k, 8 * k + 8)
                                dve.tensor_tensor(on[:, half, :], on[:, half, :], spread(orstd[:, half].rearrange("p (a o) -> p a o", o=1), 2, P), ALU.mult).then_inc(on_done, 1)
                            if k in (3, 4, 5, 6):
                                dve.wait_ge(o_hi_done, 3)
                                o_rest((2, 2 * (k - 3)), 2)
                            if k in (12, 13, 14, 15):
                                dve.wait_ge(o_hi_done, 4 + (k - 12) // 2)
                                o_rest((1, 2 * (k - 12)), 2)
                        with dve.Fori(0, 2) as n:
                            ch.enter(n, 8)
                            for i in range(4):
                                m = 4 * n + i
                                blk = 4 * n + (B_BR + 16 + i)
                                ring = (B_BR + 16 + i) % 4
                                split_lo(dve, blk + 1, (ring + 1) % 4)
                                dve.wait_ge(w_used, blk * 2 + 6)
                                ch(dve.tensor_tensor(gated[:, i % 2, :], one(gates[:, bass.ds(m + 8 * BRANCHES[2], 1), :]), bank[ring % 2][:, 0:SEQ], ALU.mult))
                                dve.sem_inc(up_read, 1)
                                acc = one(mix[:, bass.ds(m, 1), :])
                                ch(dve.tensor_tensor(acc, acc, gated[:, i % 2, :], ALU.add))
                        ch.leave(2)
                        dve.sem_inc(mix_done, 1)
                        src = lambda k: one(mix[:, bass.ds(k, 1), :])
                        part_lo(dve, src, 0, B_OUT % 2)

                        def ahead(k, blk, ring, n, i):
                            split_lo(dve, blk + 1, (ring + 1) % 4)
                            part_lo(dve, src, k + 1, (ring + 1) % 2)
                        blocks_loop(dve, B_OUT, N_OUT - 1, ahead)
                        add_to_x(dve, bank[2:6], 2 * MIX_BLOCKS + 4)

                    @block.tensor
                    def _(pe):
                        pe.sem_inc(w_used, 4)
                        pe.sem_inc(up_read, 2)
                        pe.sem_inc(lru_mm, 2)
                        pe.sem_inc(lru_sig, 2)
                        pe.sem_inc(scored, 4)
                        pe.sem_inc(pt_done, 4)
                        pe.sem_inc(pv_read, 2)
                        norm_pe(pe)
                        pe.wait_ge(h_done, DC)
                        body = lambda k, blk, ring, n, i: up_block(pe, blk, ring, blk, bank[ring % 2][:, 0:SEQ], lambda c: h_hi[:, c, :], lambda c: h_lo[:, c, :])
                        blocks_loop(pe, 0, T_DQ, body)
                        with pe.Fori(0, 4) as n:
                            for i in range(4):
                                body(None, n * 4 + (T_DQ + i), i, n, i)
                                if i % 2 == 0:
                                    s = i // 2
                                    m = n * 2 + s
                                    pe.wait_ge(conv_done, m + 1)
                                    pe.wait_ge(lru_sig, m + 1)
                                    for kind in range(2):
                                        ins = pe.matmul(bank[2 + s][:, SEQ * kind:SEQ * kind + SEQ], lru_st[:, s, kind, :], one(mix[:, bass.ds(m, 1), :]), start=True, stop=True)
                                    ins.then_inc(lru_mm, 1)
                        blocks_loop(pe, T_DV, B_BR - T_DV, body)
                        pe.wait_ge(lru_done, 1)
                        for i in range(5):
                            if i >= 2:
                                pe.wait_ge(vt_read, i - 1)
                            for j in range(4 if i < 4 else 2):
                                src = proj[:, T_DV + 4 * (i % 2) + j, P * (i // 2):P * (i // 2) + P] if i < 4 else proj[:, T_SV, P * j:P * j + P]
                                ins = pe.transpose(bank[6 + i % 2][:, P * j:P * j + P], src, ident)
                            ins.then_inc(vt_done, 1)
                        pe.wait_ge(vt_read, 5)
                        pe.wait_ge(lru_sig, DC + 2)

                        def scores(m, s, swa):
                            pe.wait_ge(staged, m + 1)
                            pe.wait_ge(hank_in[s], m * 8 + (16 - 8 * s))
                            pe.wait_ge(exp_done, m * 2 + 2)
                            for t in range(TT):
                                S = bank[2 + 2 * s + t][:, :].rearrange("p (a b) -> p a b", a=2)
                                lo, hi = (64 if swa and t else 0), P * (t + 1)
                                f = P if t == 0 else 0
                                for c in range(2):
                                    pe.matmul(S[:, c, lo:hi], flip8, hank[:, s, c if swa else 0, lo + f:hi + f], start=True, stop=False)
                                    pe.matmul(S[:, c, lo:hi], qk[:, s, c, P * t:P * t + P], qk[:, s, 2, lo:hi], start=False, stop=False)
                                    if swa and t:
                                        pe.matmul(S[:, c, 64:128], row_hi, neg, start=False, stop=False)
                                    ins = pe.matmul(S[:, c, hi - 64:hi], row_lo, neg, start=False, stop=True)
                                ins.then_inc(scored, 1)

                        def transpose_p(m, s, swa):
                            prob = probs[s]
                            for t in range(TT):
                                pe.wait_ge(attn_done, m * 2 + (t + 1))
                                pe.wait_ge(pv_read, m * 2 + (t + 1))
                                for c in range(2 if swa else 1):
                                    for kt in range(t + 1):
                                        at = P * (2 * c + kt)
                                        ins = pe.transpose(bank[6 + t][:, at:at + P], prob[:, t, c, P * kt:P * kt + P], ident)
                                ins.then_inc(pt_done, 1)

                        def values(m, swa, g):
                            for t in range(TT):
                                pe.wait_ge(pt_read, m * 2 + (t + 1))
                                for c in range(2 if swa else 1):
                                    for kt in range(t + 1):
                                        first, last = kt == 0, kt == t
                                        if swa:
                                            ins = pe.matmul(bank[6 + t][64 * c:64 * c + 64, 0:P], v_nat[:, kt, D + 64 * g:D + 64 * g + 64], prob_t[:, t, 2 * c + kt, :], start=first, stop=last)
                                        else:
                                            ins = pe.matmul(bank[6 + t][:, 0:P], prob_t[:, t, kt, :], v_nat[:, kt, bass.ds(m * P, P)], start=first, stop=last)
                                ins.then_inc(pv_done, 1)
                        for s in range(2):
                            scores(s, s, False)
                        with pe.Fori(0, 3) as n:
                            for s in range(2):
                                transpose_p(n * 2 + s, s, False)
                                scores(n * 2 + (s + 2), s, False)
                                values(n * 2 + s, False, 0)
                        for s in range(2):
                            transpose_p(6 + s, s, False)
                            scores(8 + s, s, True)
                            values(6 + s, False, 0)
                        for g, turns in ((0, (4, 6)), (1, (6, 7))):
                            with pe.Fori(*turns) as n:
                                for s in range(2):
                                    transpose_p(n * 2 + s, s, True)
                                    scores(n * 2 + (s + 2), s, True)
                                    values(n * 2 + s, True, g)
                        for s in range(2):
                            transpose_p(14 + s, s, True)
                            values(14 + s, True, 1)
                        for b, parts in zip(BRANCHES, (1, 5, 9)):
                            pe.wait_ge(o_parts, parts)
                            blocks_loop(pe, B_BR + 8 * BRANCHES.index(b), 8, lambda k, blk, ring, n, i: up_block(
                                pe, blk, ring, blk, bank[ring % 2][:, 0:SEQ], lambda c: o_hi[:, 8 * b + c, :], lambda c: o_lo[:, 8 * b + c, :]))
                            if b == BRANCHES[0]:
                                pe.wait_ge(on_done, 2)
                                for i in range(4):
                                    for j in range(4):
                                        ins = pe.transpose(bank[2 + i][:, P * j:P * j + P], o_nat[:, i // 2, 4 * (i % 2) + j, :], ident)
                                    ins.then_inc(ot_done, 1)
                        pe.wait_ge(ot_read, 4)
                        down_block(pe, B_OUT, B_OUT % 4, 0, bank[2:6], True, False)
                        blocks_loop(pe, B_OUT + 1, N_OUT - 2, lambda k, blk, ring, n, i: down_block(pe, blk, ring, k + 1, bank[2:6], False, False))
                        down_block(pe, MIX_BLOCKS - 1, (MIX_BLOCKS - 1) % 4, N_OUT - 1, bank[2:6], False, True)
            clear()
            with ExitStack() as part:
                A = sb(part, "A", [P, KEYS, SEQ])
                picks = sb(part, "picks", [P, 3, TT, P])
                picks_t = sb(part, "picks_t", [P, 4, SEQ])
                hot = sb(part, "hot", [P, 2, 2, 4, P])
                best = sb(part, "best", [P, 2, 2, TOPK])
                best_at = sb(part, "best_at", [P, 2, 2, TOPK], U32)
                best_f = sb(part, "best_f", [P, TOPK])
                whole = sb(part, "whole", [P, TT, P], I32)
                xr = A[:, 0:8, :].rearrange("p (a b) s -> p a (b s)", a=TT)
                lists = hot[:, 0, :, 0:2, :]
                again = hot[:, 1, 0, 0:2, :]
                dist = picks[:].rearrange("p i a k -> p (i a) k").rearrange("p (s i) k -> p s i k", s=2)
                BY_ACT = (2, 2)
                FREE = 112
                keys_t = A[:, 88:96, :].rearrange("p a (b k) -> p (a b) k", b=2)
                score = A[:, 96:112, :].rearrange("p a (b k) -> p (a b) k", b=2)
                q_t = A[:, 112:128, :]
                flat = A[:, 112:128, :].rearrange("p a b -> p (a b)")
                UNITS = TT * PEER_HEADS
                spot = [0]

                def scratch(n, k):
                    a = spot[0]
                    spot[0] += n * k
                    return flat[:, a:a + n * k].rearrange("p (n k) -> p n k", n=n)
                cand, cand_i = scratch(UNITS, N_CAND), scratch(UNITS, N_CAND)
                hit = scratch(TOPK, N_CAND)
                s16, i16 = scratch(2 * UNITS, TOPK), scratch(2 * UNITS, TOPK)
                sel_s, sel_i = scratch(UNITS, TOPK), scratch(UNITS, TOPK)
                B_U, B_V = N_WQ, N_WQ + N_U
                VEC_LOADS = 16

                with nc.Block() as block:
                    @block.sync
                    def _(sp):
                        sp.sem_inc(w_parts, 8)
                        sp.dma_start(vec[:], vecs[bass.ds(layer, 1)].rearrange("o p c -> (o p) c")).then_inc(vec_in, 16)
                        sp.dma_start(keys_t, subkeys[bass.ds(layer, 1)].rearrange("o p a k -> (o p) a k")).then_inc(const_in, 16)
                        load_pairs(sp, layer, MIX_BLOCKS // 2, 0, PEER_BLOCKS // 2)

                    @block.gpsimd
                    def _(pool):
                        norm_pool(pool)

                    @block.scalar
                    def _(act):
                        ch = Chain(act, s_act)
                        norm_act(act, ch)
                        norm_hi(act, V_FFNG)
                        split_hi(act, 0, 0)

                        def read_up(dst, func):
                            def body(k, blk, ring, n, i):
                                split_hi(act, blk + 1, (ring + 1) % 4)
                                act.wait_ge(w_used, blk * 2 + 6)
                                act.activation(one(dst(k)), bank[ring % 2][:, 0:SEQ], func).then_inc(up_read, 1)
                            return body
                        blocks_loop(act, 0, N_WQ, read_up(lambda k: q_t[:, bass.ds(k, 1), :] if not isinstance(k, int) else q_t[:, k:k + 1, :], ACT.Copy))
                        for i in range(8):
                            act.wait_ge(sc_done, i + 1)
                            act.activation(score[:, 4 * i:4 * i + 4, :].rearrange("p a b -> p (a b)"), bank[2 + i % 6][:, :], ACT.Copy).then_inc(sc_read, 1)
                        def lists_from_top(p, s):
                            act.wait_ge(lists_top, p + 1)
                            act.activation(s16[:, bass.ds(p * 2, 2), :], best[:, s, :, :], ACT.Copy)
                            return act.activation(i16[:, bass.ds(p * 2, 2), :], best_at[:, s, :, :], ACT.Copy)

                        def stage_lists(p, s):
                            act.activation(lists[:, s, :, :], score[:, bass.ds(p * 2, 2), :], ACT.Copy).then_inc(lists_in, 1)
                        act.wait_ge(sc_read, 8)
                        stage_lists(0, 0)
                        stage_lists(1, 1)
                        table_of(act, ch, ACT.Gelu_apprx_tanh)

                        def read_gelu(k, ring):
                            act.wait_ge(w_used, (k + B_U) * 2 + 6)
                            act.activation(one(A[:, bass.ds(k, 1), :]), bank[ring % 2][:, 0:SEQ], ACT.Gelu_apprx_tanh).then_inc(up_read, 1)

                        def plain(first, count):
                            blocks_loop(act, B_U + first, count, lambda k, blk, ring, n, i: (split_hi(act, blk + 1, (ring + 1) % 4), read_gelu(k + first, ring)))
                        plain(0, 2)
                        with act.Fori(0, 7) as n:
                            for i in range(4):
                                k, ring = n * 4 + (2 + i), (B_U + 2 + i) % 4
                                split_hi(act, k + (B_U + 1), (ring + 1) % 4)
                                if i % 2 == 0:
                                    s = i // 2
                                    lists_from_top(n * 2 + s, s)
                                    stage_lists(n * 2 + (2 + s), s)
                                read_gelu(k, ring)
                        for k in range(30, 36):
                            ring = (B_U + k) % 4
                            split_hi(act, B_U + k + 1, (ring + 1) % 4)
                            if k in (30, 32):
                                lists_from_top((k - 2) // 2, (k - 2) // 2 % 2).then_inc(lists_out, 1)
                            if k == 35:
                                act.wait_ge(cand_done, 1)
                                act.activation(lists[:, 0, 0, 0:N_CAND], cand[:, 0, :], ACT.Copy).then_inc(cand_in, 1)
                            read_gelu(k, ring)
                        with act.Fori(0, UNITS - 1) as n:
                            for i in range(4):
                                k, ring = n * 4 + (36 + i), (B_U + 36 + i) % 4
                                split_hi(act, k + (B_U + 1), (ring + 1) % 4)
                                if i == 3:
                                    act.wait_ge(cand_top, n + 1)
                                    act.activation(one(sel_s[:, bass.ds(n, 1), :]), best[:, 0, 0, :], ACT.Copy)
                                    act.activation(lists[:, 0, 0, 0:N_CAND], one(cand[:, bass.ds(n + 1, 1), :]), ACT.Copy).then_inc(cand_in, 1)
                                read_gelu(k, ring)
                        plain(96, 4)
                        split_hi(act, B_U + 101, (B_U + 101) % 4)
                        act.wait_ge(cand_top, UNITS)
                        act.activation(sel_s[:, UNITS - 1, :], best[:, 0, 0, :], ACT.Copy).then_inc(cand_in, 1)
                        read_gelu(100, (B_U + 100) % 4)
                        act.wait_ge(soft_in, 1)
                        act.activation(sel_s, sel_s, ACT.Exp).then_inc(soft_out, 1)
                        table_of(act, ch, ACT.Gelu_apprx_tanh)
                        plain(101, FREE - 101)
                        act.wait_ge(routed, 1)
                        plain(FREE, N_U - FREE)
                        act.wait_ge(picks_in, 1)

                        def distances(g, s):
                            act.wait_ge(hot_act, g + 1)
                            for k in range(BY_ACT[s], 4):
                                ins = act.activation(dist[:, s, k - 1, :], iota, ACT.Abs, scale=-1.0, bias=picks_t[:, 1, bass.ds(g * 4 + k, 1)])
                            ins.then_inc(dist_done, 1)

                        def one_hot(g, s):
                            act.wait_ge(dist_done, g + 1)
                            act.wait_ge(g_done, g + 1)
                            for k in range(BY_ACT[s], 4):
                                t = g * 4 + k
                                ins = act.activation(hot[:, s, 1, k, :], dist[:, s, k - 1, :], ACT.Relu, scale=picks_t[:, 3, bass.ds(t, 1)], bias=picks_t[:, 2, bass.ds(t, 1)])
                            ins.then_inc(hot_act, 1)
                        distances(0, 0)
                        with act.Fori(0, N_GROUPS // 2 - 1) as n:
                            distances(n * 2 + 1, 1)
                            one_hot(n * 2, 0)
                            distances(n * 2 + 2, 0)
                            one_hot(n * 2 + 1, 1)
                        distances(N_GROUPS - 1, 1)
                        one_hot(N_GROUPS - 2, 0)
                        one_hot(N_GROUPS - 1, 1)
                        src = lambda k: one(A[:, bass.ds(k, 1), :])
                        act.wait_ge(g_read, N_GROUPS)
                        part_hi(act, src, 0, 0)

                        def ahead(k, blk, ring, n, i):
                            split_hi(act, blk + 1, (ring + 1) % 4)
                            part_hi(act, src, k + 1, (ring + 1) % 2)
                        blocks_loop(act, B_V, N_V - 1, ahead)

                    @block.vector
                    def _(dve):
                        ch = Chain(dve, s_dve, drains=True)
                        norm_lo(dve, V_FFNG)
                        ahead = lambda k, blk, ring, n, i: split_lo(dve, blk + 1, (ring + 1) % 4)
                        blocks_loop(dve, 0, N_WQ, ahead)
                        with dve.Fori(0, 8) as n:
                            dve.sem_clear(s_dve)
                            for s in range(2):
                                done = 6 * s
                                val = [lists[:, s, c, :] for c in range(2)]
                                rest = [again[:, c, :] for c in range(2)]
                                big = [best[:, s, c, :] for c in range(2)]
                                at = [best_at[:, s, c, :] for c in range(2)]
                                half = lambda j: split_half(dve, n * 4 + (B_U + 1 + 2 * s + j // 2), (1 + 2 * s + j // 2) % 4, j % 2)
                                dve.wait_ge(lists_in, n * 2 + (s + 1))
                                half(0)
                                for c in range(2):
                                    dve.max(big[c][:, 0:8], val[c]).then_inc(s_dve, 1)
                                half(1)
                                for c in range(2):
                                    dve.wait_ge(s_dve, done + 1 + c)
                                    dve.max_index(at[c][:, 0:8], big[c][:, 0:8], val[c])
                                    dve.match_replace(rest[c], big[c][:, 0:8], val[c], TAKEN).then_inc(s_dve, 1)
                                half(2)
                                for c in range(2):
                                    dve.wait_ge(s_dve, done + 3 + c)
                                    dve.max(big[c][:, 8:16], rest[c]).then_inc(s_dve, 1)
                                half(3)
                                for c in range(2):
                                    dve.wait_ge(s_dve, done + 5 + c)
                                    ins = dve.max_index(at[c][:, 8:16], big[c][:, 8:16], rest[c])
                                ins.then_inc(lists_top, 1)
                        s_pair = s16.rearrange("p (u c) k -> p u c k", c=2)
                        i_pair = i16.rearrange("p (u c) k -> p u c k", c=2)
                        split_half(dve, B_U + 33, 1, 0)
                        dve.wait_ge(lists_out, 2)
                        for i in range(PAIR_RANKS + 1):
                            m = CAND_N[i] if i < PAIR_RANKS else TOPK - PAIR_RANKS
                            o = CAND_OFF[i]
                            if i < PAIR_RANKS:
                                s1, s2 = spread(s_pair[:, :, 0, i:i + 1], 2, m), s_pair[:, :, 1, 0:m]
                                i1, i2 = spread(i_pair[:, :, 0, i:i + 1], 2, m), i_pair[:, :, 1, 0:m]
                            else:
                                s1, s2 = s_pair[:, :, 0, i:TOPK], spread(s_pair[:, :, 1, 0:1], 2, m)
                                i1, i2 = i_pair[:, :, 0, i:TOPK], spread(i_pair[:, :, 1, 0:1], 2, m)
                            dve.tensor_tensor(cand[:, :, o:o + m], s1, s2, ALU.add)
                            ins = dve.scalar_tensor_tensor(out=cand_i[:, :, o:o + m], in0=i1, scalar=float(KEYS), in1=i2, op0=ALU.mult, op1=ALU.add)
                            if i == PAIR_RANKS:
                                ins.then_inc(cand_done, 1)
                            elif i < 7:
                                split_half(dve, B_U + 33 + (i + 1) // 2, (1 + (i + 1) // 2) % 4, (i + 1) % 2)
                        val, rest, big, at = lists[:, 0, 0, 0:N_CAND], again[:, 0, 0:N_CAND], best[:, 0, 0, :], best_at[:, 0, 0, :]
                        with dve.Fori(0, UNITS) as n:
                            dve.sem_clear(s_dve)
                            half = lambda j: split_half(dve, n * 4 + (B_U + 37 + j // 2), (1 + j // 2) % 4, j % 2)
                            dve.wait_ge(cand_in, n + 1)
                            half(0)
                            dve.max(big[:, 0:8], val).then_inc(s_dve, 1)
                            half(1)
                            dve.wait_ge(s_dve, 1)
                            dve.max_index(at[:, 0:8], big[:, 0:8], val)
                            dve.match_replace(rest, big[:, 0:8], val, TAKEN).then_inc(s_dve, 1)
                            half(2)
                            dve.wait_ge(s_dve, 2)
                            dve.max(big[:, 8:16], rest).then_inc(s_dve, 1)
                            half(3)
                            dve.wait_ge(s_dve, 3)
                            dve.max_index(at[:, 8:16], big[:, 8:16], rest).then_inc(cand_top, 1)
                            half(4)
                            dve.wait_ge(cand_top, n + 1)
                            dve.tensor_copy(best_f[:], at).then_inc(s_dve, 1)
                            half(5)
                            dve.wait_ge(s_dve, 4)
                            dve.tensor_tensor(hit, spread(best_f[:].rearrange("p (k o) -> p k o", o=1), 2, N_CAND),
                                              spread(iota[:, 0:N_CAND].rearrange("p (o c) -> p o c", o=1), 1, TOPK), ALU.is_equal).then_inc(s_dve, 1)
                            half(6)
                            dve.wait_ge(s_dve, 5)
                            dve.tensor_tensor(hit, hit, spread(cand_i[:, bass.ds(n, 1), :], 1, TOPK), ALU.mult).then_inc(s_dve, 1)
                            half(7)
                            dve.wait_ge(s_dve, 6)
                            dve.tensor_reduce(one(sel_i[:, bass.ds(n, 1), :]), hit, AX, ALU.add)
                        dve.drain()
                        dve.sem_clear(s_dve)
                        ch = Chain(dve, s_dve)
                        half = lambda j: split_half(dve, B_U + 101 + j // 2, (1 + j // 2) % 4, j % 2)
                        half(0)
                        dve.wait_ge(cand_in, UNITS + 1)
                        soft_max = best[:].rearrange("p a b c -> p (a b c)")[:, 0:UNITS]
                        ch(dve.tensor_copy(soft_max, sel_s[:, :, 0:1].rearrange("p u o -> p (u o)")))
                        dve.tensor_tensor(sel_s, sel_s, spread(soft_max.rearrange("p (u o) -> p u o", o=1), 2, TOPK), ALU.subtract).then_inc(soft_in, 1)
                        half(1)
                        sel_i2 = sel_i.rearrange("p (a h) k -> p a (h k)", a=TT)
                        ch(dve.tensor_copy(whole[:], sel_i2))
                        ch(dve.tensor_scalar(whole[:], whole[:], 7, None, ALU.logical_shift_right))
                        ch(dve.tensor_copy(picks[:, 0, :, :], whole[:]))
                        half(2)
                        dve.scalar_tensor_tensor(out=picks[:, 1, :, :], in0=picks[:, 0, :, :], scalar=-float(KEYS), in1=sel_i2, op0=ALU.mult, op1=ALU.add)
                        half(3)
                        dve.wait_ge(soft_out, 1)
                        ch(dve.tensor_reduce(best_f[:], sel_s, AX, ALU.add))
                        ch(dve.reciprocal(best_f[:], best_f[:]))
                        dve.tensor_tensor(picks[:, 2, :, :].rearrange("p a (h k) -> p (a h) k", h=PEER_HEADS), sel_s,
                                          spread(best_f[:].rearrange("p (u o) -> p u o", o=1), 2, TOPK), ALU.mult).then_inc(routed, 1)
                        for j in range(4, 24):
                            half(j)
                        for i in range(3):
                            dve.wait_ge(rt_done, i + 1)
                            ins = dve.tensor_copy(picks_t[:, i, :], bank[4 + i][:, 0:SEQ])
                        ch(ins)
                        dve.tensor_scalar(picks_t[:, 3, :], picks_t[:, 2, :], -1.0, None, ALU.mult).then_inc(picks_in, 1)
                        with dve.Fori(0, 4) as n:
                            for i in range(4):
                                split_lo(dve, n * 4 + (B_U + 113 + i), (i + 1) % 4)
                        dve.wait_ge(up_read, 2 + B_V)

                        def one_hot(g, s):
                            dve.tensor_tensor(hot[:, s, 0, :, :], spread(iota.rearrange("p (o k) -> p o k", o=1), 1, 4),
                                              spread(picks_t[:, 0, bass.ds(g * 4, 4)].rearrange("p (k o) -> p k o", o=1), 2, KEYS), ALU.is_equal)
                            for k in range(BY_ACT[s]):
                                t = g * 4 + k
                                ins = dve.tensor_scalar(hot[:, s, 1, k, :], iota, picks_t[:, 1, bass.ds(t, 1)], picks_t[:, 2, bass.ds(t, 1)], ALU.is_equal, ALU.mult)
                            ins.then_inc(hot_done, 1)

                        def weigh(g, s):
                            dve.wait_ge(g_done, g + 3)
                            a = A[:, :, bass.ds(g * 4, 4)]
                            dve.tensor_tensor(a, a, bank[2 + s][:, :].rearrange("p (k j) -> p j k", k=4), ALU.mult).then_inc(g_read, 1)
                        one_hot(0, 0)
                        with dve.Fori(0, N_GROUPS // 2 - 1) as n:
                            one_hot(n * 2 + 1, 1)
                            weigh(n * 2, 0)
                            one_hot(n * 2 + 2, 0)
                            weigh(n * 2 + 1, 1)
                        one_hot(N_GROUPS - 1, 1)
                        weigh(N_GROUPS - 2, 0)
                        weigh(N_GROUPS - 1, 1)
                        src = lambda k: one(A[:, bass.ds(k, 1), :])
                        part_lo(dve, src, 0, 0)

                        def ahead_v(k, blk, ring, n, i):
                            split_lo(dve, blk + 1, (ring + 1) % 4)
                            part_lo(dve, src, k + 1, (ring + 1) % 2)
                        blocks_loop(dve, B_V, N_V - 1, ahead_v)
                        add_to_x(dve, bank[4:8], 2 * PEER_BLOCKS + 4)

                    @block.tensor
                    def _(pe):
                        pe.sem_inc(w_used, 4)
                        pe.sem_inc(up_read, 2)
                        pe.sem_inc(g_done, 2)
                        pe.sem_inc(hot_act, 2)
                        norm_pe(pe)
                        pe.wait_ge(h_done, DC)
                        h_rhs = (lambda c: h_hi[:, c, :], lambda c: h_lo[:, c, :])
                        body = lambda k, blk, ring, n, i: up_block(pe, blk, ring, blk, bank[ring % 2][:, 0:SEQ], *h_rhs)
                        blocks_loop(pe, 0, N_WQ, body)
                        pe.wait_ge(up_read, 2 + N_WQ)
                        pe.wait_ge(const_in, 16)
                        for i in range(8):
                            if i >= 6:
                                pe.wait_ge(sc_read, i - 5)
                            for j in range(4):
                                t, hc = i // 4, 4 * (i % 4) + j
                                ins = pe.matmul(bank[2 + i % 6][:, P * j:P * j + P], q_t[:, hc, P * t:P * t + P], keys_t[:, hc, :], start=True, stop=True)
                            ins.then_inc(sc_done, 1)
                        blocks_loop(pe, B_U, FREE, body)
                        pe.wait_ge(routed, 1)
                        for i in range(3):
                            for t in range(TT):
                                ins = pe.transpose(bank[4 + i][:, P * t:P * t + P], picks[:, i, t, :], ident)
                            ins.then_inc(rt_done, 1)
                        blocks_loop(pe, B_U + FREE, N_U - FREE, body)

                        def weights(g, s):
                            pe.wait_ge(hot_done, g + 1)
                            pe.wait_ge(hot_act, g + 3)
                            for k in range(4):
                                ins = pe.matmul(bank[2 + s][:, P * k:P * k + P], hot[:, s, 0, k, :], hot[:, s, 1, k, :], start=True, stop=True)
                            ins.then_inc(g_done, 1)
                        with pe.Fori(0, N_GROUPS // 2) as n:
                            for s in range(2):
                                weights(n * 2 + s, s)
                        down_block(pe, B_V, 0, 0, bank[4:8], True, False)
                        blocks_loop(pe, B_V + 1, N_V - 2, lambda k, blk, ring, n, i: down_block(pe, blk, ring, k + 1, bank[4:8], False, False))
                        down_block(pe, PEER_BLOCKS - 1, (PEER_BLOCKS - 1) % 4, N_V - 1, bank[4:8], False, True)
            clear()

        with ExitStack() as part:
            xr = sb(part, "xr", [P, TT, D])
            g_all = sb(part, "g_all", [P, D])
            with nc.Block() as block:
                @block.sync
                def _(sp):
                    sp.dma_start(g_all[:], spread(final_g, 0, P)).then_inc(const_in, 16)
                    for t in range(TT):
                        sp.wait_ge(x_done, t + 1)
                        sp.dma_start(out[P * t:P * t + P, :], xr[:, t, :]).then_inc(stored, 16)
                    sp.wait_ge(stored, 16 * TT)

                @block.scalar
                def _(act):
                    norm_act(act, Chain(act, s_act))

                @block.gpsimd
                def _(pool):
                    norm_pool(pool)

                @block.vector
                def _(dve):
                    dve.wait_ge(const_in, 16)
                    dve.wait_ge(rstd_done, 1)
                    for t in range(TT):
                        dve.scalar_tensor_tensor(out=xr[:, t, :], in0=x[:, t, :], scalar=rstd[:, t:t + 1], in1=g_all[:],
                                                 op0=ALU.mult, op1=ALU.mult).then_inc(x_done, 1)


def buckets():
    rel = np.arange(N_REL) - (SEQ - 1)
    n = np.abs(rel)
    large = 8 + (np.log(np.maximum(n, 1).astype(np.float32) / 8) / np.float32(np.log(128.0)) * 8).astype(np.int32)
    bucket = np.where(rel > 0, 16, 0) + np.where(n < 8, n, np.minimum(large, 15))
    return (bucket[None, :] == np.arange(32)[:, None]).astype(np.float32)


def constants():
    c = np.zeros((P, N_CST), np.float32)
    c[:, C_ID:C_ID + P] = np.eye(P)
    c[:, C_FLIP:C_FLIP + P] = np.eye(P)[::-1] / SCALE
    c[:, C_IOTA:C_IOTA + P] = np.arange(P)
    c[0, C_LO:C_LO + 64] = 1
    c[0, C_HI + 64:C_HI + P] = 1
    c[0, C_NEG:C_NEG + CHUNK] = MASKED
    return c


def kernel(**inputs):
    import math
    import concourse.bacc as _bacc
    from concourse.bass_utils import run_bass_kernel_spmd as _run
    a = {k: np.asarray(v) for k, v in inputs.items()}

    def up(w):
        return np.ascontiguousarray(w.reshape(DC, P, -1, P).transpose(2, 1, 0, 3)).reshape(-1, P, D)

    blocks = []
    for l in range(DEPTH):
        blocks += [up(a["w_in"][l]), up(a["w_gate"][l])] + [up(a["w_branch"][l, b]) for b in BRANCHES]
        blocks += [a["w_out"][l].reshape(DC, P, D), up(a["peer_wq"][l])]
        u = a["peer_u"][l].reshape(P, KEYS, DC, P)
        blocks.append(u.transpose(1, 3, 2, 0).reshape(KEYS, P, D))
        blocks.append(a["peer_v"][l].reshape(P, KEYS, D).transpose(1, 0, 2))
    stream = np.concatenate(blocks).reshape(DEPTH * LAYER_PAIRS, 2, P, D)

    def cols(v):
        return v.reshape(DEPTH, -1, P).transpose(0, 2, 1)

    vecs = np.concatenate([cols(a[n]) for n in ("norm_mix_g", "conv_w", "conv_b", "lru_bx", "lru_ba", "lru_a_param", "b_gate",
                                                "norm_ffn_g", "diff_subln_g")], axis=2)
    lru = np.stack([a["lru_wx"], a["lru_wa"]], axis=3)
    lru = lru.reshape(DEPTH, DC, 2, 64, 2, 64).transpose(0, 2, 3, 1, 4, 5).reshape(DEPTH, P, DC, 2, 64)
    subk = a["peer_subkeys"].reshape(DEPTH, 2 * PEER_HEADS, KEYS, P).transpose(0, 3, 1, 2)
    init = [0.8 - 0.6 * math.exp(-0.3 * l) for l in range(DEPTH)]
    arrays = {
        "stream": stream, "vecs": vecs, "cst": constants(), "rel_bias": a["rel_bias"], "bucket_onehot": buckets(),
        "lam_consts": np.array([[i, 1.0 - i] for i in init], np.float32), "final_g": a["final_norm_g"].reshape(1, D),
        "diff_lambda": a["diff_lambda"].reshape(DEPTH, -1), "sinks": a["swa_sinks"], "lru_w": lru, "subkeys": subk,
        "x_in": a["x"].reshape(SEQ, D),
    }
    arrays = {k: np.ascontiguousarray(v) for k, v in arrays.items()}
    nc = _bacc.Bacc("TRN2", target_bir_lowering=False, num_devices=1, dynamic_dma_scratch_size=8192)
    args = [nc.dram_tensor(k, v.shape, mybir.dt.from_np(v.dtype), kind="ExternalInput").ap() for k, v in arrays.items()]
    out = nc.dram_tensor("out", (SEQ, D), F32, kind="ExternalOutput").ap()
    trunk(nc, *args, out)
    r = _run(nc, [arrays], core_ids=[0])
    return r.results[0]["out"].reshape(1, SEQ, D)
```
